# Optimizing a Trainium2 kernel written in Bass

```python
import math
import jax, jax.numpy as jnp
from jax import lax
import numpy as np
import jax
import jax.numpy as jnp

D_MODEL = 1024
BATCH = 1
SEQ = 256
DEPTH = 2

N_MIXERS = 2
N_HEADS = 16
HEAD_DIM = D_MODEL // N_HEADS
BLOCK_Q = 128
POOL_WINDOWS = (2, 4, 8, 16)
N_POOL_GROUPS = len(POOL_WINDOWS)
POOL_GROUP = D_MODEL // N_POOL_GROUPS
D_FF = 2816
PLE_DIM = 256
EPS = 1e-6


def rms_norm(x, g):
    xf = x.astype(jnp.float32)
    y = xf * lax.rsqrt(jnp.mean(xf * xf, axis=-1, keepdims=True) + EPS)
    return (y * g.astype(jnp.float32)).astype(x.dtype)

def swiglu(h, w_gu, w_down):
    gate, up = jnp.split(h @ w_gu, 2, axis=-1)
    return (jax.nn.silu(gate) * up) @ w_down

def stick_breaking_attention(h, w_qkv, q_gain, k_gain, w_o):
    B, S, _ = h.shape
    q, k, v = jnp.split(h @ w_qkv, 3, axis=-1)
    q = rms_norm(q.reshape(B, S, N_HEADS, HEAD_DIM), q_gain)
    k = rms_norm(k.reshape(B, S, N_HEADS, HEAD_DIM), k_gain)
    v = v.reshape(B, S, N_HEADS, HEAD_DIM)
    q, k, v = (t.transpose(0, 2, 1, 3) for t in (q, k, v))
    scale = 1.0 / math.sqrt(HEAD_DIM)
    outs = []
    for blk in range(S // BLOCK_Q):
        t0 = blk * BLOCK_Q
        t1 = t0 + BLOCK_Q
        qb = q[:, :, t0:t1]
        kb = k[:, :, :t1]
        vb = v[:, :, :t1]
        z = jnp.einsum('bhqd,bhkd->bhqk', qb, kb).astype(jnp.float32) * scale
        qpos = t0 + jnp.arange(BLOCK_Q)
        kpos = jnp.arange(t1)
        causal = kpos[None, :] < qpos[:, None]
        log_stay = jnp.where(causal, jax.nn.log_sigmoid(-z), 0.0)
        log_after = lax.cumsum(log_stay, axis=3, reverse=True) - log_stay
        weights = jnp.where(causal, jnp.exp(jax.nn.log_sigmoid(z) + log_after), 0.0)
        outs.append(jnp.einsum('bhqk,bhkd->bhqd', weights.astype(vb.dtype), vb))
    o = jnp.concatenate(outs, axis=2)
    o = o.transpose(0, 2, 1, 3).reshape(B, S, D_MODEL)
    return o @ w_o

def multiscale_pool_mixer(h, w_in, w_grp, scale):
    B, S, _ = h.shape
    u = (h @ w_in).reshape(B, S, N_POOL_GROUPS, POOL_GROUP)
    uf = u.astype(jnp.float32)
    c = jnp.cumsum(uf, axis=1)
    pos = jnp.arange(S)
    outs = []
    for gi, w in enumerate(POOL_WINDOWS):
        cg = c[:, :, gi]
        cpad = jnp.pad(cg, ((0, 0), (w, 0), (0, 0)))
        wsum = cpad[:, w:] - cpad[:, :S]
        cnt = jnp.minimum(pos + 1, w).astype(jnp.float32)
        outs.append(wsum / cnt[None, :, None] - uf[:, :, gi])
    pooled = jnp.stack(outs, axis=2).astype(h.dtype)
    y = jnp.einsum('bsgc,gcd->bsgd', pooled, w_grp).reshape(B, S, D_MODEL)
    return y * scale

def first_inputs(seed: int = 0) -> dict:
    key = jax.random.key(seed)
    ks = iter(jax.random.split(key, 32))
    n_a = (DEPTH + 1) // 2
    n_b = DEPTH // 2
    f32 = jnp.float32

    def w(shape, fan_in):
        return jax.random.normal(next(ks), shape, f32) * fan_in ** -0.5

    def gain(shape):
        return 1.0 + 0.05 * jax.random.normal(next(ks), shape, f32)

    return {
        "x": jax.random.normal(next(ks), (BATCH, SEQ, D_MODEL), f32),
        "p": jax.random.normal(next(ks), (DEPTH, BATCH, SEQ, PLE_DIM), f32),
        "norm_ffn1": gain((DEPTH, D_MODEL)),
        "w_ffn1_gu": w((DEPTH, D_MODEL, 2 * D_FF), D_MODEL),
        "w_ffn1_down": w((DEPTH, D_FF, D_MODEL), D_FF),
        "norm_mix": gain((DEPTH, D_MODEL)),
        "w_qkv": w((n_a, D_MODEL, 3 * D_MODEL), D_MODEL),
        "q_norm": gain((n_a, HEAD_DIM)),
        "k_norm": gain((n_a, HEAD_DIM)),
        "w_o": w((n_a, D_MODEL, D_MODEL), D_MODEL),
        "w_pool_in": w((n_b, D_MODEL, D_MODEL), D_MODEL),
        "w_pool_grp": w((n_b, N_POOL_GROUPS, POOL_GROUP, POOL_GROUP), POOL_GROUP),
        "pool_scale": gain((n_b, D_MODEL)),
        "norm_ffn2": gain((DEPTH, D_MODEL)),
        "w_ffn2_gu": w((DEPTH, D_MODEL, 2 * D_FF), D_MODEL),
        "w_ffn2_down": w((DEPTH, D_FF, D_MODEL), D_FF),
        "norm_ple": gain((DEPTH, D_MODEL)),
        "w_ple_gate": w((DEPTH, D_MODEL, D_MODEL), D_MODEL),
        "w_ple_proj": w((DEPTH, PLE_DIM, D_MODEL), PLE_DIM),
    }

def first_block(x, p, norm_ffn1, w_ffn1_gu, w_ffn1_down, norm_mix, w_qkv, q_norm,
              k_norm, w_o, w_pool_in, w_pool_grp, pool_scale, norm_ffn2,
              w_ffn2_gu, w_ffn2_down, norm_ple, w_ple_gate, w_ple_proj):
    for i in range(DEPTH):
        x = x + 0.5 * swiglu(rms_norm(x, norm_ffn1[i]), w_ffn1_gu[i], w_ffn1_down[i])
        h = rms_norm(x, norm_mix[i])
        j = i // N_MIXERS
        if i % N_MIXERS == 0:
            mix = stick_breaking_attention(h, w_qkv[j], q_norm[j], k_norm[j], w_o[j])
        else:
            mix = multiscale_pool_mixer(h, w_pool_in[j], w_pool_grp[j], pool_scale[j])
        x = x + mix
        x = x + 0.5 * swiglu(rms_norm(x, norm_ffn2[i]), w_ffn2_gu[i], w_ffn2_down[i])
        gate = jax.nn.sigmoid(rms_norm(x, norm_ple[i]) @ w_ple_gate[i])
        x = x + gate * (p[i] @ w_ple_proj[i])
    return x


N_MIXERS_2 = 3
HEAD_DIM_2 = 64
N_HEADS_2 = D_MODEL // HEAD_DIM_2
D_FF_2 = 4 * D_MODEL
ROPE_THETA = 10000.0
NORM_EPS = 1e-6
NEG_INF = -1e30
NSA_KV_GROUPS = 4
NSA_CMP_LEN = 32
NSA_CMP_STRIDE = 16
NSA_CMP_HIDDEN = 4 * HEAD_DIM_2
NSA_SEL_LEN = 64
NSA_TOP_N = 16
NSA_WINDOW = 512
NSA_SEL_QBLOCK = 32
NSA_FORCE_BONUS = 1000.0
FOX_QBLOCK = 128
SWA_KV_HEADS = 2
SWA_WINDOW = 128
BAND_QBLOCK = 128
N_LAYERS_A = len(range(0, DEPTH, N_MIXERS_2))
N_LAYERS_B = len(range(1, DEPTH, N_MIXERS_2))
N_LAYERS_C = len(range(2, DEPTH, N_MIXERS_2))


def rms_norm_2(x, g):
    xf = x.astype(jnp.float32)
    y = xf * lax.rsqrt(jnp.mean(xf * xf, axis=-1, keepdims=True) + NORM_EPS)
    return (y * g.astype(jnp.float32)).astype(x.dtype)

def rope_tables(seq):
    inv = ROPE_THETA ** (-jnp.arange(0, HEAD_DIM_2, 2, dtype=jnp.float32) / HEAD_DIM_2)
    ang = jnp.arange(seq, dtype=jnp.float32)[:, None] * inv[None, :]
    return jnp.cos(ang), jnp.sin(ang)

def apply_rope(x, cos, sin):
    xf = x.astype(jnp.float32)
    x1, x2 = jnp.split(xf, 2, axis=-1)
    c = cos[None, :, None, :]
    s = sin[None, :, None, :]
    return jnp.concatenate([x1 * c - x2 * s, x2 * c + x1 * s], axis=-1).astype(x.dtype)

def banded_attention(q, k, v, window, sinks=None):
    B, T, H, dh = q.shape
    G = k.shape[2]
    rep = H // G
    blk = BAND_QBLOCK
    nb = T // blk
    span = blk + window
    scale = dh ** -0.5
    kp = jnp.pad(k, ((0, 0), (window, 0), (0, 0), (0, 0)))
    vp = jnp.pad(v, ((0, 0), (window, 0), (0, 0), (0, 0)))
    qc = q.reshape(B, nb, blk, G, rep, dh).transpose(1, 0, 2, 3, 4, 5)
    offs_q = jnp.arange(blk)
    offs_k = jnp.arange(span) - window

    def one(args):
        i, qi = args
        start = i * blk
        kc = lax.dynamic_slice_in_dim(kp, start, span, axis=1)
        vc = lax.dynamic_slice_in_dim(vp, start, span, axis=1)
        qpos = start + offs_q
        kpos = start + offs_k
        dist = qpos[:, None] - kpos[None, :]
        valid = (kpos[None, :] >= 0) & (dist >= 0) & (dist < window)
        s = jnp.einsum('bqgrd,bkgd->bgrqk', qi, kc).astype(jnp.float32) * scale
        s = jnp.where(valid, s, NEG_INF)
        if sinks is None:
            p = jax.nn.softmax(s, axis=-1)
        else:
            sink = jnp.broadcast_to(sinks.astype(jnp.float32).reshape(G, rep)[None, :, :, None, None],
                                    (B, G, rep, blk, 1))
            p = jax.nn.softmax(jnp.concatenate([s, sink], axis=-1), axis=-1)[..., :-1]
        return jnp.einsum('bgrqk,bkgd->bqgrd', p.astype(vc.dtype), vc)

    out = lax.map(one, (jnp.arange(nb), qc))
    return out.transpose(1, 0, 2, 3, 4, 5).reshape(B, T, H, dh)

def nsa_compress(tok, pos, w1, w2):
    B, T, G, dh = tok.shape
    nc = (T - NSA_CMP_LEN) // NSA_CMP_STRIDE + 1
    idx = np.arange(nc)[:, None] * NSA_CMP_STRIDE + np.arange(NSA_CMP_LEN)[None, :]
    win = tok[:, idx] + pos[:, None, :].astype(tok.dtype)
    win = win.transpose(0, 1, 3, 2, 4).reshape(B, nc, G, NSA_CMP_LEN * dh)
    return jax.nn.silu(win @ w1) @ w2

def nsa_selected_attention(qg, k, v, sel):
    B, T, G, rep, dh = qg.shape
    ns = T // NSA_SEL_LEN
    n = sel.shape[-1]
    qb = NSA_SEL_QBLOCK
    nq = T // qb
    scale = dh ** -0.5
    kb = k.reshape(B, ns, NSA_SEL_LEN, G, dh).transpose(0, 3, 1, 2, 4)
    vb = v.reshape(B, ns, NSA_SEL_LEN, G, dh).transpose(0, 3, 1, 2, 4)
    qc = qg.reshape(B, nq, qb, G, rep, dh).transpose(1, 0, 2, 3, 4, 5)
    sc = sel.reshape(B, G, nq, qb, n).transpose(2, 0, 1, 3, 4)
    gather = jax.vmap(jax.vmap(lambda tab, ix: tab[ix]))
    offs = jnp.arange(NSA_SEL_LEN)

    def one(args):
        i, qi, si = args
        gk = gather(kb, si).reshape(B, G, qb, n * NSA_SEL_LEN, dh)
        gv = gather(vb, si).reshape(B, G, qb, n * NSA_SEL_LEN, dh)
        kpos = (si[..., None] * NSA_SEL_LEN + offs).reshape(B, G, qb, n * NSA_SEL_LEN)
        qpos = i * qb + jnp.arange(qb)
        valid = kpos <= qpos[None, None, :, None]
        s = jnp.einsum('bqgrd,bgqkd->bgrqk', qi, gk).astype(jnp.float32) * scale
        s = jnp.where(valid[:, :, None], s, NEG_INF)
        p = jax.nn.softmax(s, axis=-1)
        return jnp.einsum('bgrqk,bgqkd->bqgrd', p.astype(gv.dtype), gv)

    out = lax.map(one, (jnp.arange(nq), qc, sc))
    return out.transpose(1, 0, 2, 3, 4, 5).reshape(B, T, G * rep, dh)

def nsa_mixer(h, w_in, cmp_pos, cmp_w1, cmp_w2, w_out, cos, sin):
    B, T, _ = h.shape
    H, G, dh = N_HEADS_2, NSA_KV_GROUPS, HEAD_DIM_2
    rep = H // G
    kvw = G * dh
    scale = dh ** -0.5
    proj = h @ w_in
    sizes = [H * dh, kvw, kvw, kvw, kvw, kvw, kvw, 3 * H]
    cuts = np.cumsum(sizes)[:-1].tolist()
    q, kc_t, vc_t, ks, vs, kw, vw, gate = jnp.split(proj, cuts, axis=-1)
    q = apply_rope(q.reshape(B, T, H, dh), cos, sin)
    kc_t = apply_rope(kc_t.reshape(B, T, G, dh), cos, sin)
    ks = apply_rope(ks.reshape(B, T, G, dh), cos, sin)
    kw = apply_rope(kw.reshape(B, T, G, dh), cos, sin)
    vc_t = vc_t.reshape(B, T, G, dh)
    vs = vs.reshape(B, T, G, dh)
    vw = vw.reshape(B, T, G, dh)
    qg = q.reshape(B, T, G, rep, dh)
    tpos = jnp.arange(T)

    kcmp = nsa_compress(kc_t, cmp_pos[0], cmp_w1[0], cmp_w2[0])
    vcmp = nsa_compress(vc_t, cmp_pos[1], cmp_w1[1], cmp_w2[1])
    nc = kcmp.shape[1]
    s = jnp.einsum('btgrd,bcgd->bgrtc', qg, kcmp).astype(jnp.float32) * scale
    cend = jnp.arange(nc) * NSA_CMP_STRIDE + NSA_CMP_LEN - 1
    cvalid = cend[None, :] <= tpos[:, None]
    p_cmp = jax.nn.softmax(jnp.where(cvalid, s, NEG_INF), axis=-1)
    p_cmp = jnp.where((tpos >= NSA_CMP_LEN - 1)[:, None], p_cmp, 0.0)
    o_cmp = jnp.einsum('bgrtc,bcgd->btgrd', p_cmp.astype(vcmp.dtype), vcmp).reshape(B, T, H, dh)

    ns = T // NSA_SEL_LEN
    c_lo = np.arange(nc)[:, None] * NSA_CMP_STRIDE
    s_lo = np.arange(ns)[None, :] * NSA_SEL_LEN
    ov = np.clip(np.minimum(c_lo + NSA_CMP_LEN, s_lo + NSA_SEL_LEN) - np.maximum(c_lo, s_lo), 0, None)
    overlap = jnp.asarray(ov.astype(np.float32) / NSA_CMP_LEN)
    imp = jnp.einsum('bgrtc,cn->bgtn', p_cmp, overlap)
    tblk = tpos // NSA_SEL_LEN
    j = jnp.arange(ns)
    forced = (j[None, :] == 0) | (j[None, :] == tblk[:, None]) | (j[None, :] == tblk[:, None] - 1)
    bvalid = j[None, :] <= tblk[:, None]
    score = jnp.where(bvalid, imp + jnp.where(forced, NSA_FORCE_BONUS, 0.0), -1.0)
    n_top = min(NSA_TOP_N, ns)
    _, sel = lax.top_k(score, n_top)

    o_slc = nsa_selected_attention(qg, ks, vs, sel)
    o_win = banded_attention(q, kw, vw, NSA_WINDOW)

    g = jax.nn.sigmoid(gate.astype(jnp.float32)).reshape(B, T, H, 3)
    o = g[..., 0:1] * o_cmp + g[..., 1:2] * o_slc + g[..., 2:3] * o_win
    return o.astype(h.dtype).reshape(B, T, H * dh) @ w_out

def fox_attention(q, k, v, logf):
    B, T, H, dh = q.shape
    blk = FOX_QBLOCK
    nb = T // blk
    scale = dh ** -0.5
    c = jnp.cumsum(logf, axis=1).transpose(0, 2, 1)
    outs = []
    for i in range(nb):
        lo, hi = i * blk, (i + 1) * blk
        s = jnp.einsum('bqhd,bkhd->bhqk', q[:, lo:hi], k[:, :hi]).astype(jnp.float32) * scale
        s = s + c[:, :, lo:hi, None] - c[:, :, None, :hi]
        causal = jnp.arange(lo, hi)[:, None] >= jnp.arange(hi)[None, :]
        p = jax.nn.softmax(jnp.where(causal, s, NEG_INF), axis=-1)
        outs.append(jnp.einsum('bhqk,bkhd->bqhd', p.astype(v.dtype), v[:, :hi]))
    return jnp.concatenate(outs, axis=1)

def fox_mixer(h, w_in, b_f, w_out):
    B, T, _ = h.shape
    H, dh = N_HEADS_2, HEAD_DIM_2
    proj = h @ w_in
    q, k, v, fl = jnp.split(proj, [H * dh, 2 * H * dh, 3 * H * dh], axis=-1)
    logf = jax.nn.log_sigmoid(fl.astype(jnp.float32) + b_f.astype(jnp.float32))
    o = fox_attention(q.reshape(B, T, H, dh), k.reshape(B, T, H, dh), v.reshape(B, T, H, dh), logf)
    return o.reshape(B, T, H * dh) @ w_out

def swa_mixer(h, w_in, b_in, sinks, w_out, b_out, cos, sin):
    B, T, _ = h.shape
    H, G, dh = N_HEADS_2, SWA_KV_HEADS, HEAD_DIM_2
    proj = h @ w_in + b_in
    q, k, v = jnp.split(proj, [H * dh, H * dh + G * dh], axis=-1)
    q = apply_rope(q.reshape(B, T, H, dh), cos, sin)
    k = apply_rope(k.reshape(B, T, G, dh), cos, sin)
    o = banded_attention(q, k, v.reshape(B, T, G, dh), SWA_WINDOW, sinks)
    return o.reshape(B, T, H * dh) @ w_out + b_out

def squared_relu_mlp(h, w_up, w_down):
    return jnp.square(jax.nn.relu(h @ w_up)) @ w_down

def second_inputs(seed: int = 0) -> dict:
    key = jax.random.key(seed)
    ks = jax.random.split(key, 20)
    D, H, dh = D_MODEL, N_HEADS_2, HEAD_DIM_2
    f32 = jnp.float32
    nsa_in_w = H * dh + 6 * NSA_KV_GROUPS * dh + 3 * H
    fox_in_w = 3 * H * dh + H
    swa_in_w = H * dh + 2 * SWA_KV_HEADS * dh
    cmp_in = NSA_CMP_LEN * dh
    nrm = lambda k, shape, fan: jax.random.normal(k, shape, f32) * (fan ** -0.5)
    return {
        'x': jax.random.normal(ks[0], (BATCH, SEQ, D), f32),
        'norm_g': 1.0 + 0.02 * jax.random.normal(ks[1], (DEPTH, 4, D), f32),
        'mlp_w_up': nrm(ks[2], (DEPTH, D, D_FF_2), D),
        'mlp_w_down': nrm(ks[3], (DEPTH, D_FF_2, D), D_FF_2),
        'nsa_w_in': nrm(ks[4], (N_LAYERS_A, D, nsa_in_w), D),
        'nsa_cmp_pos': 0.2 * jax.random.normal(ks[5], (N_LAYERS_A, 2, NSA_CMP_LEN, dh), f32),
        'nsa_cmp_w1': nrm(ks[6], (N_LAYERS_A, 2, cmp_in, NSA_CMP_HIDDEN), cmp_in),
        'nsa_cmp_w2': nrm(ks[7], (N_LAYERS_A, 2, NSA_CMP_HIDDEN, dh), NSA_CMP_HIDDEN),
        'nsa_w_out': nrm(ks[8], (N_LAYERS_A, H * dh, D), H * dh),
        'fox_w_in': nrm(ks[9], (N_LAYERS_B, D, fox_in_w), D),
        'fox_b_f': jax.random.uniform(ks[10], (N_LAYERS_B, H), f32, 1.0, 5.0),
        'fox_w_out': nrm(ks[11], (N_LAYERS_B, H * dh, D), H * dh),
        'swa_w_in': nrm(ks[12], (N_LAYERS_C, D, swa_in_w), D),
        'swa_b_in': 0.02 * jax.random.normal(ks[13], (N_LAYERS_C, swa_in_w), f32),
        'swa_sinks': jax.random.normal(ks[14], (N_LAYERS_C, H), f32),
        'swa_w_out': nrm(ks[15], (N_LAYERS_C, H * dh, D), H * dh),
        'swa_b_out': 0.02 * jax.random.normal(ks[16], (N_LAYERS_C, D), f32),
    }

def second_block(x, norm_g, mlp_w_up, mlp_w_down, nsa_w_in, nsa_cmp_pos, nsa_cmp_w1, nsa_cmp_w2, nsa_w_out,
              fox_w_in, fox_b_f, fox_w_out, swa_w_in, swa_b_in, swa_sinks, swa_w_out, swa_b_out):
    T = x.shape[1]
    cos, sin = rope_tables(T)
    for i in range(DEPTH):
        kind = i % N_MIXERS_2
        slot = i // N_MIXERS_2
        h = rms_norm_2(x, norm_g[i, 0])
        if kind == 0:
            m = nsa_mixer(h, nsa_w_in[slot], nsa_cmp_pos[slot], nsa_cmp_w1[slot], nsa_cmp_w2[slot],
                          nsa_w_out[slot], cos, sin)
        elif kind == 1:
            m = fox_mixer(h, fox_w_in[slot], fox_b_f[slot], fox_w_out[slot])
        else:
            m = swa_mixer(h, swa_w_in[slot], swa_b_in[slot], swa_sinks[slot], swa_w_out[slot],
                          swa_b_out[slot], cos, sin)
        x = x + rms_norm_2(m, norm_g[i, 1])
        h = rms_norm_2(x, norm_g[i, 2])
        x = x + rms_norm_2(squared_relu_mlp(h, mlp_w_up[i], mlp_w_down[i]), norm_g[i, 3])
    return x


def setup_inputs(seed=0):
    out = dict(first_inputs(seed))
    for name, value in second_inputs(seed + 1).items():
        if name != "x":
            out[name + "_2"] = value
    return out


def reference(
    x, p, norm_ffn1, w_ffn1_gu, w_ffn1_down, norm_mix, w_qkv, q_norm, k_norm, w_o, w_pool_in,
    w_pool_grp, pool_scale, norm_ffn2, w_ffn2_gu, w_ffn2_down, norm_ple, w_ple_gate, w_ple_proj,
    norm_g_2, mlp_w_up_2, mlp_w_down_2, nsa_w_in_2, nsa_cmp_pos_2, nsa_cmp_w1_2, nsa_cmp_w2_2,
    nsa_w_out_2, fox_w_in_2, fox_b_f_2, fox_w_out_2, swa_w_in_2, swa_b_in_2, swa_sinks_2,
    swa_w_out_2, swa_b_out_2,
):
    x = first_block(
        x, p, norm_ffn1, w_ffn1_gu, w_ffn1_down, norm_mix, w_qkv, q_norm, k_norm, w_o,
        w_pool_in, w_pool_grp, pool_scale, norm_ffn2, w_ffn2_gu, w_ffn2_down, norm_ple,
        w_ple_gate, w_ple_proj,
    )
    return second_block(
        x, norm_g_2, mlp_w_up_2, mlp_w_down_2, nsa_w_in_2, nsa_cmp_pos_2, nsa_cmp_w1_2,
        nsa_cmp_w2_2, nsa_w_out_2, fox_w_in_2, fox_b_f_2, fox_w_out_2, swa_w_in_2, swa_b_in_2,
        swa_sinks_2, swa_w_out_2, swa_b_out_2,
    )


_drawn_inputs = setup_inputs


def setup_inputs(seed=0):
    import zlib

    import numpy as np

    out = dict(_drawn_inputs(seed))
    spreads = {}
    factors = {'q_norm': 4.208, 'k_norm': 4.619, 'norm_ple': 5.321}
    for name, (base, spread) in spreads.items():
        noise = np.random.default_rng([zlib.crc32(name.encode()), seed]).standard_normal(out[name].shape)
        drawn = base * np.exp(spread * noise) if base else spread * noise
        out[name] = jnp.asarray(drawn.astype(out[name].dtype))
    for name, factor in factors.items():
        out[name] = (out[name] * factor).astype(out[name].dtype)
    return out
```

```python
from contextlib import ExitStack

import numpy as np

import concourse.bass as bass
from concourse import mybir

P = 128
TOKENS, DM = 256, 1024
TT = TOKENS // P
KC = DM // P
HEADS, DH = 16, 64
PAIRS = HEADS // 2
SLOT_HEAD = (0, 2, 1, 3)
GROUPS = 4
HG = HEADS // GROUPS
PLE = 256
D_FF, D_MLP = 2816, 4096
FFN_BLOCKS = D_FF // 256
MLP_BLOCKS = D_MLP // 512
WINDOWS = (2, 4, 8, 16)
CMP_LEN, CMP_STRIDE = 32, 16
NCMP = (TOKENS - CMP_LEN) // CMP_STRIDE + 1
CPAD = 32
CMP_HID = 256
EPS = 1e-6
QSCALE = DH ** -0.5
NEG = -1e30

UNIT = 2048
RAW, RING = 3, 6

FFN_U = 3 * FFN_BLOCKS
MLP_U = 4 * MLP_BLOCKS
STAGES = [
    ("ffn", FFN_U), ("stick", 16), ("ffn", FFN_U), ("ple", 5),
    ("ffn", FFN_U), ("pool", 6), ("ffn", FFN_U), ("ple", 5),
    ("nsa", 19), ("mlp", MLP_U), ("fox", 17), ("mlp", MLP_U),
]

PAD_UNITS = RAW

CONST = {}
_at = 0
for _name, _n in [("ident", P), ("after_neg", P), ("ones_neg", P), ("upto", P), ("ones", P),
                  ("mask", 2 * P), ("cos", TT * 32), ("sin", TT * 32), ("cmp_mask", TT * CPAD),
                  ("cmp_valid", TT), ("head_block", HG)]:
    CONST[_name] = (_at, _n)
    _at += _n
NCONST = _at
COLS = {}
_at = 0
for _name, _n in [("gains", 12 * KC), ("q_gain", 1), ("k_gain", 1), ("cmp_pos", 2 * CMP_LEN // 2),
                  ("cmp_w2", 2 * 2 * DH), ("b_f", HEADS)]:
    COLS[_name] = (_at, _n)
    _at += _n
NCOLS = _at

QKV = 0
QT, KT = 6144, 8192
ACT_AT = 10240
NARENA = 11264


class Signal:

    def __init__(self, nc, ctx, name, free=0):
        self.sem = ctx.enter_context(nc.semaphore(name))
        self.free = free
        self.seen = {}

    def due(self, who, step=1, turn=None):
        v = self.seen.get(who, 0 if who == "pe" else self.free) + step
        self.seen[who] = v
        if turn is not None:
            v = v + turn.i * turn.each[self]
        return self.sem, v


class Turn:

    def __init__(self, i, each, units):
        self.i, self.each, self.units = i, each, units


def network_kernel(nc, stream, x_in, consts_in, cols_in, p_in, rows_in, count_in, out):
    f32, f32r = mybir.dt.float32, mybir.dt.float32r
    ALU, ACT, AX = mybir.AluOpType, mybir.ActivationFunctionType, mybir.AxisListType
    stages = STAGES
    starts, units_total = [], 0
    for _, n in stages:
        starts.append(units_total)
        units_total += n
    units_total += PAD_UNITS

    ctx = ExitStack()
    with ctx:
        def sb(name, cols, dt=f32):
            return ctx.enter_context(nc.sbuf_tensor(name, [P, cols], dt))

        raw = sb("raw", RAW * UNIT)
        w_hi, w_lo = sb("w_hi", RING * UNIT, f32r), sb("w_lo", RING * UNIT, f32r)
        X = sb("X", TT * DM)
        hT_hi, hT_lo = sb("hT_hi", KC * TOKENS, f32r), sb("hT_lo", KC * TOKENS, f32r)
        hid_hi, hid_lo = sb("hid_hi", 4 * TOKENS, f32r), sb("hid_lo", 4 * TOKENS, f32r)
        arena = sb("arena", NARENA)
        sil = sb("sil", TT * 512)
        const = sb("const", NCONST)
        cols = sb("cols", NCOLS)
        stat = sb("stat", 312)
        ps = ctx.enter_context(nc.psum_tensor("ps", [P, 8 * 512], f32))

        def bank(b, a=0, n=512):
            return ps[:, b * 512 + a:b * 512 + a + n]

        def at(off, n):
            return arena[:, off:off + n]

        def K(name, a=0, n=None):
            o, m = CONST[name]
            return const[:, o + a:o + a + (m - a if n is None else n)]

        def C(name, a=0, n=None):
            o, m = COLS[name]
            return cols[:, o + a:o + a + (m - a if n is None else n)]

        def xs(tok, a=0, n=DM):
            return X[:, tok * DM + a:tok * DM + a + n]

        def f(ap):
            return ap.bitcast(f32)

        def chunk(t, c, n=1):
            return t[:, c * TOKENS:(c + n) * TOKENS]

        def lhs(t, c, tok):
            return t[:, c * TOKENS + tok * P:c * TOKENS + (tok + 1) * P]

        def unit_cols(t, u, a, n):
            s = (u % RING) * UNIT
            return t[:, s + a:s + a + n]

        ident = K("ident")
        ss, var, rstd = stat[:, 0:4], stat[:, 4:8], stat[:, 8:12]
        nhalf = stat[:, 12:44]
        ssq, varq, rstdq = stat[:, 44:76], stat[:, 76:108], stat[:, 108:140]
        q_gain8 = stat[:, 140:141]
        nmax, rsum, rinv = stat[:, 144:160], stat[:, 160:176], stat[:, 176:192]
        cmax, csum, ccoef = stat[:, 192:200], stat[:, 200:208], stat[:, 208:216]
        fl, cq = stat[:, 224:256], stat[:, 256:288]
        coefs = stat[:, 288:312]

        def S(name, free=0):
            return Signal(nc, ctx, name, free)

        const_in, x_in_done, row_in, out_done = S("const_in"), S("x_in_done"), S("row_in"), S("out_done")
        raw_in = [S(f"raw_in{r}") for r in range(RAW)]
        hi_done, lo_done, unit_used = S("hi_done"), S("lo_done"), S("unit_used")
        x_ready, ss_ready, rstd_ready, xn_ready = S("x_ready"), S("ss_ready"), S("rstd_ready"), S("xn_ready")
        hT_full, hT_hi_done, hT_ready = S("hT_full"), S("hT_hi_done"), S("hT_ready")
        gu_full, silu_done = S("gu_full"), S("silu_done")
        hid_ready, hidT_full, hidT_hi, hidT_ready = S("hid_ready"), S("hidT_full"), S("hidT_hi"), S("hidT_ready")
        quarter_full = S("quarter_full")
        proj_full, proj_free = S("proj_full"), [S("proj_free0", 1), S("proj_free1", 1)]
        p_hi_done, p_ready, sg_ready = S("p_hi_done"), S("p_ready"), S("sg_ready")
        u_hi_done, u_ready, pool_full, pooled = S("u_hi_done"), S("u_ready"), S("pool_full"), S("pooled")
        sq_ready, ssq_ready, rstdq_ready, qn_ready = S("sq_ready"), S("ssq_ready"), S("rstdq_ready"), S("qn_ready")
        qk_full, tr_act, tr_dve = S("qk_full"), S("tr_act"), S("tr_dve")
        z_full, z_used, l_ready, nst_raw, nst_ready = S("z_full"), S("z_used"), S("l_ready"), S("nst_raw"), S("nst_ready")
        after_full, warg_ready, w_raw, w_ready = S("after_full"), S("warg_ready"), S("w_raw"), S("w_ready")
        s_full, s_used, max_ready, p_done = S("s_full"), S("s_used"), S("max_ready"), S("p_done")
        t_full, tA_done, tB_done, pv_full, sums_used = S("t_full"), S("tA_done"), S("tB_done"), S("pv_full"), S("sums_used")
        zeros_ready = S("zeros_ready")
        gates_ready, win_tmp, win_hi, win_ready = S("gates_ready"), S("win_tmp"), S("win_hi"), S("win_ready")
        hidc_ready, cmp_full, cmp_kv = S("hidc_ready"), S("cmp_full"), S("cmp_kv")
        cs_full, cs_ready, cp_exp, cpT_full, cpT_ready, cpv_full = (
            S("cs_full"), S("cs_ready"), S("cp_exp"), S("cpT_full"), S("cpT_ready"), S("cpv_full"))
        fl_soft, logf_ready, c_full, c_ready = S("fl_soft"), S("logf_ready"), S("c_full"), S("c_ready")
        act_step, dve_step, pool_step, even_done = S("act_step"), S("dve_step"), S("pool_step"), S("even_done")

        split = {"act": 0, "dve": 0}

        def all_of(who, sigs, n):
            for s in sigs:
                s.due(who, n)

        block = ctx.enter_context(nc.Block())

        @block.sync
        def _(sp):
            sp.dma_start(const[:], consts_in).then_inc(const_in.sem, 16)
            sp.dma_start(cols[:], cols_in).then_inc(const_in.sem, 16)
            sp.dma_start(X[:].rearrange("p (t d) -> p t d", t=TT), x_in).then_inc(x_in_done.sem, 16)
            view = stream.rearrange("(n r) p c -> n r p c", r=RAW)
            for r in range(RAW):
                sp.dma_start(raw[:, r * UNIT:(r + 1) * UNIT], view[0, r]).then_inc(raw_in[r].sem, 16)
            with sp.Fori(1, units_total // RAW) as n:
                for r in range(RAW):
                    sp.wait_ge(lo_done.sem, n * RAW + (r - RAW + 1))
                    sp.dma_start(raw[:, r * UNIT:(r + 1) * UNIT], view[n, r]).then_inc(raw_in[r].sem, 16)
            for tok in range(TT):
                sp.wait_ge(x_ready.sem, 2 * len(stages) - 1 + tok)
                sp.dma_start(out[tok], xs(tok)).then_inc(out_done.sem, 16)
            sp.wait_ge(out_done.sem, 16 * TT)

        @block.tensor
        def _(pe):
            me = "pe"

            def unit_ready(u, t=None):
                pe.wait_ge(lo_done.sem, u + 1 + (t.i * t.units if t else 0))

            def three(dst, a_hi, a_lo, b_hi, b_lo, start, stop):
                nc.tensor.matmul(dst, a_hi, b_hi, start=start, stop=False, skip_group_check=True)
                nc.tensor.matmul(dst, a_hi, b_lo, start=False, stop=False, skip_group_check=True)
                return nc.tensor.matmul(dst, a_lo, b_hi, start=False, stop=stop, skip_group_check=True)

            def half_block(dst, tok, us, width, fresh, t, first):
                per = UNIT // width if len(us) == 2 else KC
                per = min(per, KC // len(us))
                for k in range(KC):
                    u = us[k // per]
                    if first and k % per == 0:
                        unit_ready(u, t)
                    if fresh and k % 2 == 0:
                        pe.wait_ge(*hT_ready.due(me))
                    a = (k % per) * width
                    yield k, three(dst, lhs(hT_hi, k, tok), lhs(hT_lo, k, tok), unit_cols(w_hi, u, a, width),
                                   unit_cols(w_lo, u, a, width), k == 0, k == KC - 1)

            def columns(us, free, full, width=512, fresh=False, t=None, between=None):
                for tok in range(TT):
                    if free is not None:
                        pe.wait_ge(*free[tok].due(me, turn=t))
                    for k, mm in half_block(bank(tok, 0, width), tok, us, width, fresh and tok == 0, t, tok == 0):
                        if tok == 0 and k == KC - 1:
                            mm.then_inc(full.sem, 1)
                        if tok == 1 and k % (KC // len(us)) == KC // len(us) - 1:
                            mm.then_inc(unit_used.sem, 1)
                    if tok == 0 and between:
                        between()

            def quarters(u, fresh, b0=4):
                for tok in range(TT):
                    for half in range(2):
                        us = [u + 2 * half, u + 2 * half + 1]
                        go = half_block(bank(b0 + 2 * tok + half), tok, us, 512, fresh and tok + half == 0, None, tok == 0)
                        for k, mm in go:
                            if k == KC - 1 and (tok, half) != (1, 1):
                                mm.then_inc(quarter_full.sem, 1)
                            elif tok == 1 and (k in (3, 7) or (half, k) == (1, 0)):
                                mm.then_inc(unit_used.sem, 1)

            def norm_transpose():
                for tok in range(TT):
                    pe.wait_ge(*xn_ready.due(me))
                    for c in range(KC):
                        mm = nc.tensor.transpose(bank(c // 2, (c % 2) * TOKENS + tok * P, P), at(tok * DM + c * P, P), ident)
                        if tok == 1 and c % 2 == 1:
                            mm.then_inc(hT_full.sem, 1)

            def mlp(u0, blocks, hc, turns, per_turn):
                step = 2 + hc // 2
                banks_t = hc // 2

                def hidden_transpose(t=None):
                    pe.wait_ge(*hid_ready.due(me, turn=t))
                    for tok in range(TT):
                        for c in range(hc):
                            mm = nc.tensor.transpose(bank(2 + c // 2, (c % 2) * TOKENS + tok * P, P),
                                                     at(ACT_AT + tok * 512 + c * P, P), ident)
                            if tok == 1 and c % 2 == 1:
                                mm.then_inc(hidT_full.sem, 1)

                def down(us, first, last, t=None):
                    for u in us:
                        unit_ready(u, t)
                    for _ in range(banks_t):
                        pe.wait_ge(*hidT_ready.due(me, turn=t))
                    for tok in range(TT):
                        for half in range(2):
                            for c in range(hc):
                                u, a = us[c // 2], (c % 2) * DM + half * 512
                                mm = three(bank(4 + 2 * tok + half), lhs(hid_hi, c, tok), lhs(hid_lo, c, tok),
                                           unit_cols(w_hi, u, a, 512), unit_cols(w_lo, u, a, 512),
                                           first and c == 0, last and c == hc - 1)
                                if (tok, half) == (1, 1):
                                    if c % 2 == 1:
                                        mm.then_inc(unit_used.sem, 1)
                                elif last and c == hc - 1:
                                    mm.then_inc(quarter_full.sem, 1)

                def one(j, u, t=None):
                    if j:
                        pe.wait_ge(*hid_ready.due(me, turn=t))
                    columns([u, u + 1], None, gu_full, fresh=j == 0, t=t,
                            between=(lambda: hidden_transpose(t)) if j else None)
                    if j:
                        down(list(range(u + 2, u + step)), j == 1, False, t)

                one(0, u0)
                one(1, u0 + 2)
                u = u0 + 2 + step
                each = {hid_ready: 2 * per_turn, hidT_ready: banks_t * per_turn}
                with pe.Fori(0, turns) as i:
                    t = Turn(i, each, per_turn * step)
                    for b in range(per_turn):
                        one(2 + b, u + b * step, t)
                for s, n in each.items():
                    s.due(me, n * (turns - 1))
                u += turns * per_turn * step
                for j in range(2 + turns * per_turn, blocks):
                    one(j, u)
                    u += step
                pe.wait_ge(*hid_ready.due(me))
                hidden_transpose()
                down(list(range(u, u + hc // 2)), False, True)

            def qkv(u0):
                each = {proj_free[0]: 3, proj_free[1]: 3}
                for _ in range(4):
                    pe.wait_ge(*hT_ready.due(me))
                with pe.Fori(0, 2) as i:
                    t = Turn(i, each, 6)
                    for b in range(3):
                        columns([u0 + 2 * b, u0 + 2 * b + 1], proj_free, proj_full, t=t)
                for s, n in each.items():
                    s.due(me, n)

            def transpose_pairs(section, b0):
                for tok in range(TT):
                    pe.wait_ge(*qn_ready.due(me))
                    for p in range(PAIRS):
                        mm = nc.tensor.transpose(bank(b0 + p // 2, (p % 2) * TOKENS + tok * P, P),
                                                 at(section + tok * DM + p * P, P), ident)
                        if tok == 1 and p % 2 == 1:
                            mm.then_inc(qk_full.sem, 1)

            def head(off, h, a=0, n=TOKENS):
                r = DH * (h % 2)
                return arena[r:r + DH, off + (h // 2) * TOKENS + a:off + (h // 2) * TOKENS + a + n]

            def group_head(off, h, a=0, n=TOKENS):
                r, g = DH * (h % 2), h // HG
                return arena[r:r + DH, off + g * TOKENS + a:off + g * TOKENS + a + n]

            def A(b0, h, a, n):
                return ps[:, b0 * 512 + h * 256 + a:b0 * 512 + h * 256 + a + n]

            def stick(u0):
                qkv(u0)
                for sec in range(2):
                    for tok in range(TT):
                        if sec == 0:
                            pe.wait_ge(*qn_ready.due(me))
                        for p in range(PAIRS):
                            mm = nc.tensor.transpose(bank(4 * sec + p // 2, (p % 2) * TOKENS + tok * P, P),
                                                     at(QKV + sec * 2048 + tok * DM + p * P, P), ident)
                            if tok == 1 and p % 2 == 1:
                                mm.then_inc(qk_full.sem, 1)
                for _ in range(4):
                    pe.wait_ge(*tr_act.due(me))
                    pe.wait_ge(*tr_dve.due(me))

                def scores(g):
                    if g:
                        pe.wait_ge(*z_used.due(me))
                    for s in range(HG):
                        h = HG * g + SLOT_HEAD[s]
                        nc.tensor.matmul(A(0, s, 0, 256), head(KT, h, 0, P), head(QT, h), start=True, stop=True)
                        if s == 2:
                            pe.wait_ge(*even_done.due(me))
                        mm = nc.tensor.matmul(bank(2, s * P, P), head(KT, h, P, P), head(QT, h, P, P), start=True, stop=True)
                        if s == 1:
                            mm.then_inc(even_done.sem, 1)
                    mm.then_inc(z_full.sem, 1)

                def weigh(g):
                    pe.wait_ge(*nst_ready.due(me))
                    nA, nB = at(3072, 1024), at(ACT_AT, 512)
                    for b in range(2):
                        nc.tensor.matmul(bank(3 + b), K("after_neg"), nA[:, b * 512:(b + 1) * 512], start=True, stop=False, skip_group_check=True)
                        for s in (2 * b, 2 * b + 1):
                            nc.tensor.matmul(A(3, s, P, P), K("ones_neg"), nB[:, s * P:(s + 1) * P], start=False, stop=True, skip_group_check=True)
                    nc.tensor.matmul(bank(5), K("after_neg"), nB, start=True, stop=True).then_inc(after_full.sem, 1)
                    pe.wait_ge(*w_ready.due(me))
                    wA, wB = at(1536, 1024), at(2560, 512)
                    o = 6 + g % 2
                    for s in range(HG):
                        j = SLOT_HEAD[s]
                        h = HG * g + j
                        r, p = DH * (h % 2), (j // 2) * TOKENS
                        v0, v1 = at(QKV + 4096 + h * DH, DH), at(QKV + 4096 + DM + h * DH, DH)
                        nc.tensor.matmul(ps[r:r + DH, o * 512 + p:o * 512 + p + 256], v0, wA[:, s * 256:(s + 1) * 256], start=True, stop=False, skip_group_check=True)
                        mm = nc.tensor.matmul(ps[r:r + DH, o * 512 + p + P:o * 512 + p + 256], v1, wB[:, s * P:(s + 1) * P], start=False, stop=True, skip_group_check=True)
                    mm.then_inc(hT_full.sem, 1)

                for n in range(GROUPS + 1):
                    if n < GROUPS:
                        scores(n)
                    if n:
                        weigh(n - 1)
                quarters(u0 + 12, True)

            sums = [0]

            def bank6():
                if sums[0]:
                    pe.wait_ge(sums_used.sem, sums[0])
                sums[0] += 1

            def softmax_attention(jobs, q_of, k_of, v_of, extra, before, after):
                for n in range(len(jobs) + 1):
                    if n < len(jobs):
                        g, br = jobs[n]
                        if n:
                            pe.wait_ge(*s_used.due(me))
                        elif s_used.seen.get(me):
                            s_used.due(me)
                        for s in range(HG):
                            h = HG * g + SLOT_HEAD[s]
                            last = br != "fox"
                            nc.tensor.matmul(A(0, s, 0, 256), q_of(h, P, P), k_of(br, h, 0, 256), start=True, stop=last, skip_group_check=True)
                            if not last:
                                nc.tensor.matmul(A(0, s, 0, 256), extra(h), sil[0:HEADS, 0:TOKENS], start=False, stop=True, skip_group_check=True)
                            if s == 2:
                                pe.wait_ge(*even_done.due(me))
                            mm = nc.tensor.matmul(bank(2, s * P, P), q_of(h, 0, P), k_of(br, h, 0, P), start=True, stop=last, skip_group_check=True)
                            if not last:
                                mm = nc.tensor.matmul(bank(2, s * P, P), extra(h), sil[0:HEADS, 0:P], start=False, stop=True, skip_group_check=True)
                            if s == 1:
                                mm.then_inc(even_done.sem, 1)
                        mm.then_inc(s_full.sem, 1)
                        if before:
                            before(g, br)
                    if n:
                        g, br = jobs[n - 1]
                        if after:
                            after(g, br)
                        pe.wait_ge(*p_done.due(me))
                        s0 = ((n - 1) % 2) * 1536
                        for s in range(HG):
                            sA, sB = at(s0 + s * 256, 256), at(s0 + 1024 + s * P, P)
                            nc.tensor.transpose(A(3, s, 0, P), sB, ident)
                            nc.tensor.transpose(A(3, s, P, P), sA[:, 0:P], ident)
                            mm = nc.tensor.transpose(bank(5, s * P, P), sA[:, P:256], ident)
                        mm.then_inc(t_full.sem, 1)
                        pe.wait_ge(*tA_done.due(me))
                        pe.wait_ge(*tB_done.due(me))
                        bank6()
                        tA, tB = at(3072, 1024), at(ACT_AT, 512)
                        for s in range(HG):
                            j = SLOT_HEAD[s]
                            h = HG * g + j
                            nc.tensor.matmul(bank(6, j * DH, DH), tA[:, s * 256:s * 256 + P], v_of(br, h, 0), start=True, stop=True, skip_group_check=True)
                            nc.tensor.matmul(bank(6, 256 + j * DH, DH), tA[:, s * 256 + P:(s + 1) * 256], v_of(br, h, 0), start=True, stop=False, skip_group_check=True)
                            mm = nc.tensor.matmul(bank(6, 256 + j * DH, DH), tB[:, s * P:(s + 1) * P], v_of(br, h, 1), start=False, stop=True, skip_group_check=True)
                        mm.then_inc(pv_full.sem, 1)
                        if br != "slc":
                            pe.wait_ge(sums_used.sem, sums[0])
                            for tok in range(TT):
                                for c in range(2):
                                    mm = nc.tensor.transpose(bank(7, c * TOKENS + tok * P, P), at(ACT_AT + 512 + tok * 256 + c * P, P), ident)
                            mm.then_inc(hT_full.sem, 1)

            def fox(u0):
                for _ in range(4):
                    pe.wait_ge(*hT_ready.due(me))
                columns([u0], proj_free, proj_full, width=HEADS)
                each = {proj_free[0]: 3, proj_free[1]: 3}
                with pe.Fori(0, 2) as i:
                    t = Turn(i, each, 6)
                    for b in range(3):
                        columns([u0 + 1 + 2 * b, u0 + 2 + 2 * b], proj_free, proj_full, t=t)
                for s, n in each.items():
                    s.due(me, n)
                pe.wait_ge(*logf_ready.due(me))
                lf = [fl[:, 0:HEADS], fl[:, HEADS:2 * HEADS]]
                nc.tensor.matmul(bank(2, 0, HEADS), K("upto"), lf[0], start=True, stop=True, skip_group_check=True)
                nc.tensor.matmul(bank(2, HEADS, HEADS), K("ones"), lf[0], start=True, stop=False, skip_group_check=True)
                nc.tensor.matmul(bank(2, HEADS, HEADS), K("upto"), lf[1], start=False, stop=True, skip_group_check=True)
                rows = ps[0:HEADS, 3 * 512:3 * 512 + TOKENS]
                nc.tensor.matmul(rows[:, 0:P], lf[0], K("upto"), start=True, stop=True, skip_group_check=True)
                nc.tensor.matmul(rows[:, P:TOKENS], lf[0], K("ones"), start=True, stop=False, skip_group_check=True)
                nc.tensor.matmul(rows[:, P:TOKENS], lf[1], K("upto"), start=False, stop=True, skip_group_check=True).then_inc(c_full.sem, 1)
                pe.wait_ge(*c_ready.due(me))
                for sec in range(2):
                    for tok in range(TT):
                        if sec == 0:
                            pe.wait_ge(*proj_free[tok].due("pe_all", 21))
                        for p in range(PAIRS):
                            mm = nc.tensor.transpose(bank(4 * sec + p // 2, (p % 2) * TOKENS + tok * P, P),
                                                     at(QKV + sec * 2048 + tok * DM + p * P, P), ident)
                            if tok == 1 and p % 2 == 1:
                                mm.then_inc(qk_full.sem, 1)
                for _ in range(4):
                    pe.wait_ge(*tr_act.due(me))
                    pe.wait_ge(*tr_dve.due(me))
                softmax_attention(
                    [(g, "fox") for g in range(GROUPS)],
                    lambda h, a, n: head(QT, h, a, n), lambda br, h, a, n: head(KT, h, a, n),
                    lambda br, h, tok: at(QKV + 4096 + tok * DM + h * DH, DH),
                    lambda h: const[0:HEADS, CONST["ident"][0] + h:CONST["ident"][0] + h + 1].broadcast_to((HEADS, P)),
                    None, None)
                quarters(u0 + 13, True)

            def nsa(u0):
                for _ in range(4):
                    pe.wait_ge(*hT_ready.due(me))
                for b in range(5):
                    columns([u0 + 2 * b, u0 + 2 * b + 1], proj_free, proj_full)
                columns([u0 + 10], proj_free, proj_full, width=3 * HEADS)
                transpose_pairs(0, 0)

                def group_keys(sec, b0):
                    for tok in range(TT):
                        for g in range(GROUPS):
                            for half in range(2):
                                c = (g % 2) * TOKENS + tok * P
                                dst = ps[DH * half:DH * half + DH, (b0 + g // 2) * 512 + c:(b0 + g // 2) * 512 + c + P]
                                mm = nc.tensor.matmul(dst, at(sec + tok * 256 + g * DH, DH), ident, start=True, stop=True, skip_group_check=True)
                            if tok == 1 and g % 2 == 1:
                                mm.then_inc(qk_full.sem, 1)

                for _ in range(TT):
                    pe.wait_ge(*qn_ready.due(me))
                group_keys(3072, 4)
                group_keys(3584, 6)
                for _ in range(2):
                    pe.wait_ge(*tr_act.due(me))
                    pe.wait_ge(*tr_dve.due(me))
                group_keys(2048, 0)
                group_keys(2560, 2)
                pe.wait_ge(*win_ready.due(me))
                for kv in range(2):
                    us = [u0 + 11 + 2 * kv, u0 + 12 + 2 * kv]
                    for u in us:
                        unit_ready(u)
                    for fc in range(2):
                        for jj in range(CMP_LEN // 2):
                            u, a = us[jj // 8], (jj % 8) * CMP_HID + fc * P
                            w = kv * 960 + jj * 60
                            dst = bank(4 + 2 * kv + fc, 0, 60)
                            nc.tensor.matmul(dst, unit_cols(w_hi, u, a, P), hT_hi[:, w:w + 60], start=jj == 0, stop=False, skip_group_check=True)
                            nc.tensor.matmul(dst, unit_cols(w_hi, u, a, P), hT_lo[:, w:w + 60], start=False, stop=False, skip_group_check=True)
                            mm = nc.tensor.matmul(dst, unit_cols(w_lo, u, a, P), hT_hi[:, w:w + 60], start=False, stop=jj == 15, skip_group_check=True)
                            if fc == 1 and jj % 8 == 7:
                                mm.then_inc(unit_used.sem, 1)
                for _ in range(2):
                    pe.wait_ge(*hidc_ready.due(me))
                def hidc(kv, fc, a, n):
                    return at(5216 + (kv * 2 + fc) * 128 + a, n)
                for half in range(2):
                    for fc in range(2):
                        nc.tensor.matmul(ps[DH * half:DH * half + DH, 0:128], C("cmp_w2", fc * DH, DH), hidc(0, fc, 0, 128),
                                         start=fc == 0, stop=fc == 1, skip_group_check=True)
                for g in range(GROUPS):
                    for r in range(HG):
                        for fc in range(2):
                            mm = nc.tensor.matmul(ps[CPAD * r:CPAD * r + CPAD, 512 + g * DH:512 + (g + 1) * DH], hidc(1, fc, g * CPAD, CPAD),
                                                  C("cmp_w2", 128 + fc * DH, DH), start=fc == 0, stop=fc == 1, skip_group_check=True)
                mm.then_inc(cmp_full.sem, 1)
                pe.wait_ge(*cmp_kv.due(me))
                for _ in range(4):
                    pe.wait_ge(*tr_dve.due(me))
                    pe.wait_ge(*tr_act.due(me))

                split_before = hT_ready.seen[me]

                def cmp_scores(g, br):
                    if br != "slc":
                        return
                    for s in range(HG):
                        h = HG * g + SLOT_HEAD[s]
                        r = DH * (h % 2)
                        if s == 2:
                            pe.wait_ge(*even_done.due(me))
                        for qt in range(TT):
                            mm = nc.tensor.matmul(bank(7, (qt * HG + SLOT_HEAD[s]) * CPAD, CPAD), head(QT, h, qt * P, P),
                                                  arena[r:r + DH, 5728 + g * CPAD:5728 + (g + 1) * CPAD], start=True, stop=True, skip_group_check=True)
                        if s == 1:
                            mm.then_inc(even_done.sem, 1)
                    mm.then_inc(cs_full.sem, 1)

                def cmp_sums(g, br):
                    if br != "slc":
                        return
                    pe.wait_ge(*cp_exp.due(me))
                    if g:
                        pe.wait_ge(hT_ready.sem, split_before + g)
                    for qt in range(TT):
                        mm = nc.tensor.transpose(bank(7, 256 + qt * P, P), at(5856 + qt * P, P), ident)
                    mm.then_inc(cpT_full.sem, 1)
                    pe.wait_ge(*cpT_ready.due(me))
                    bank6()
                    for qt in range(TT):
                        mm = nc.tensor.matmul(bank(6, qt * 256, 256), sil[:, 256 + qt * P:256 + (qt + 1) * P], sil[:, 768:1024], start=True, stop=True, skip_group_check=True)
                    mm.then_inc(cpv_full.sem, 1)

                softmax_attention(
                    [(g, br) for g in range(GROUPS) for br in ("slc", "win")],
                    lambda h, a, n: head(QT, h, a, n),
                    lambda br, h, a, n: group_head(KT + (0 if br == "slc" else 1024), h, a, n),
                    lambda br, h, tok: at((4096 if br == "slc" else 4608) + tok * 256 + (h // HG) * DH, DH),
                    None, cmp_scores, cmp_sums)
                quarters(u0 + 15, True)

            def pool(u0):
                columns([u0, u0 + 1], proj_free, proj_full, fresh=True)
                columns([u0 + 2, u0 + 3], proj_free, proj_full)
                ub = u0 + 4
                unit_ready(ub)
                for _ in range(TT):
                    pe.wait_ge(*u_ready.due(me))
                for c in range(KC):
                    for tt in range(TT):
                        rhs = unit_cols(w_hi, ub, (tt * 4 + c // 2) * TOKENS, TOKENS)
                        a = tt * DM + c * P
                        nc.tensor.matmul(bank(c // 2, (c % 2) * TOKENS, TOKENS), hT_hi[:, a:a + P], rhs, start=tt == 0, stop=False, skip_group_check=True)
                        mm = nc.tensor.matmul(bank(c // 2, (c % 2) * TOKENS, TOKENS), hT_lo[:, a:a + P], rhs, start=False, stop=tt == 1, skip_group_check=True)
                    if c == KC - 1:
                        mm.then_inc(unit_used.sem, 1)
                    elif c % 2 == 1:
                        mm.then_inc(pool_full.sem, 1)
                ug = u0 + 5
                unit_ready(ug)
                for tok in range(TT):
                    for g in range(4):
                        if tok == 0:
                            pe.wait_ge(*hT_ready.due(me))
                        for c in range(2):
                            a = (g * 2 + c) * 256
                            mm = three(bank(4 + 2 * tok + g // 2, (g % 2) * 256, 256), lhs(hT_hi, 2 * g + c, tok), lhs(hT_lo, 2 * g + c, tok),
                                       unit_cols(w_hi, ug, a, 256), unit_cols(w_lo, ug, a, 256), c == 0, c == 1)
                        if (tok, g) == (1, 3):
                            mm.then_inc(unit_used.sem, 1)
                        elif g % 2 == 1:
                            mm.then_inc(quarter_full.sem, 1)

            def ple(u0):
                unit_ready(u0)
                pe.wait_ge(*p_ready.due(me))
                for tok in range(TT):
                    for half in range(2):
                        for c in range(2):
                            a = c * DM + half * 512
                            mm = three(bank(4 + 2 * tok + half), lhs(hid_hi, c, tok), lhs(hid_lo, c, tok),
                                       unit_cols(w_hi, u0, a, 512), unit_cols(w_lo, u0, a, 512), c == 0, c == 1)
                mm.then_inc(unit_used.sem, 1)
                for _ in range(4):
                    pe.wait_ge(*hT_ready.due(me))
                quarters(u0 + 1, False, b0=0)

            pe.wait_ge(const_in.sem, 32)
            for (kind, _), u0 in zip(stages, starts):
                norm_transpose()
                if kind == "ffn":
                    mlp(u0, FFN_BLOCKS, 2, 4, 2)
                elif kind == "mlp":
                    mlp(u0, MLP_BLOCKS, 4, 2, 3)
                else:
                    {"stick": stick, "ple": ple, "pool": pool, "nsa": nsa, "fox": fox}[kind](u0)

        @block.scalar
        def _(act):
            me = "act"

            def split_to(n, t=None):
                n = min(n, units_total)
                while split[me] < n:
                    u = split[me]
                    split[me] += 1
                    more = t.i * t.units if t else 0
                    act.wait_ge(raw_in[u % RAW].sem, 16 * (u // RAW + 1) + (t.i * (16 * t.units // RAW) if t else 0))
                    if u >= RING:
                        act.wait_ge(unit_used.sem, u - RING + 1 + more)
                    r = u % RAW
                    nc.scalar.activation(unit_cols(w_hi, u, 0, UNIT), raw[:, r * UNIT:(r + 1) * UNIT], ACT.Copy).then_inc(hi_done.sem, 1)

            def step(ins):
                ins.then_inc(act_step.sem, 1)
                act.wait_ge(*act_step.due(me))

            def square_x(s):
                for tok in range(TT):
                    if s > 0:
                        act.wait_ge(*x_ready.due(me))
                    nc.scalar.activation(at(4096 + tok * DM, DM), xs(tok), ACT.Square, accum_out=ss[:, tok:tok + 1]).then_inc(ss_ready.sem, 1)

            def h_high(n):
                for b in range(4):
                    act.wait_ge(*hT_full.due(me))
                    for c in (2 * b, 2 * b + 1):
                        ins = nc.scalar.activation(chunk(hT_hi, c), bank(b, (c % 2) * TOKENS, TOKENS), ACT.Copy, scale=C("gains", n * KC + c, 1))
                    ins.then_inc(hT_hi_done.sem, 1)

            def mlp(u0, blocks, hc, turns, per_turn, relu):
                step_u = 2 + hc // 2
                w = 512 if relu else 256

                def activate(tok, done, t):
                    if tok == 0:
                        act.wait_ge(*gu_full.due(me, turn=t))
                    else:
                        act.wait_ge(unit_used.sem, done + (t.i * t.units if t else 0))
                    nc.scalar.activation(sil[:, tok * 512:tok * 512 + w], bank(tok, 0, w), ACT.Relu if relu else ACT.Silu).then_inc(silu_done.sem, 1)

                def hidden_high(t=None):
                    for b in range(hc // 2):
                        act.wait_ge(*hidT_full.due(me, turn=t))
                        nc.scalar.activation(chunk(hid_hi, 2 * b, 2), bank(2 + b), ACT.Copy).then_inc(hidT_hi.sem, 1)

                def one(j, u, ahead, t=None):
                    activate(0, None, t)
                    if j:
                        hidden_high(t)
                    split_to(ahead - step_u // 2, t)
                    activate(1, u + 2, t)
                    split_to(ahead, t)

                one(0, u0, u0 + 2 + step_u)
                one(1, u0 + 2, u0 + 2 + 2 * step_u)
                u = u0 + 2 + step_u
                each = {gu_full: per_turn, hidT_full: per_turn * (hc // 2)}
                with act.Fori(0, turns) as i:
                    t = Turn(i, each, per_turn * step_u)
                    for b in range(per_turn):
                        one(2 + b, u + b * step_u, u + (b + 2) * step_u, t)
                for s, n in each.items():
                    s.due(me, n * (turns - 1))
                split[me] += (turns - 1) * per_turn * step_u
                u += turns * per_turn * step_u
                for j in range(2 + turns * per_turn, blocks):
                    one(j, u, u + 2 * step_u)
                    u += step_u
                hidden_high()

            def square_acc(end):
                for tok in range(TT):
                    if tok == 0:
                        act.wait_ge(*quarter_full.due(me, 2))
                    else:
                        quarter_full.due(me)
                        act.wait_ge(unit_used.sem, end)
                    nc.scalar.activation(at(8192 + tok * DM, DM), ps[:, (4 + 2 * tok) * 512:(6 + 2 * tok) * 512], ACT.Square,
                                         accum_out=ss[:, 2 + tok:3 + tok]).then_inc(ss_ready.sem, 1)

            def evacuate(dst, src, t=None):
                act.wait_ge(*proj_full.due(me, turn=t))
                nc.scalar.activation(dst, src, ACT.Copy).then_inc(proj_free[0].sem, 1)

            def qkv(u0):
                each = {proj_full: 3}
                with act.Fori(0, 2) as i:
                    t = Turn(i, each, 6)
                    for b in range(3):
                        evacuate(arena[:, bass.ds(i * 512 + (QKV + b * 2048), 512)], bank(0), t)
                        split_to(u0 + 5 + 2 * (b + 1), t)
                split[me] += 6
                proj_full.due(me, 3)

            def transposed_high(n):
                act.wait_ge(*hT_full.due(me))
                nc.scalar.activation(chunk(hT_hi, 2 * n, 2), bank(6 + n % 2), ACT.Copy).then_inc(hT_hi_done.sem, 1)

            def stick(u0):
                qkv(u0)
                split_to(u0 + 16)
                sec = at(QKV, 4096).rearrange("p (s t d) -> p s t d", s=2, t=TT)
                for tok in range(TT):
                    act.wait_ge(*proj_free[tok].due(me, 6))
                    dst = at(6144 + tok * 2048, 2048).rearrange("p (s d) -> p s d", s=2)
                    nc.scalar.activation(dst, sec[:, :, tok, :], ACT.Square).then_inc(sq_ready.sem, 1)
                nc.scalar.preload_act_table_set("natural_log_exp_and_others")
                for b in range(4):
                    act.wait_ge(*qk_full.due(me))
                    nc.scalar.activation(at(QT + b * 512, 512), bank(b), ACT.Copy, scale=q_gain8).then_inc(tr_act.sem, 1)
                qk_full.due(me, 4)
                for n in range(GROUPS + 1):
                    if n < GROUPS:
                        act.wait_ge(*z_full.due(me))
                        if n:
                            act.wait_ge(*z_used.due(me))
                        L = at(0, 1536)
                        step(nc.scalar.activation(L, ps[:, 0:1536], ACT.Abs))
                        step(nc.scalar.activation(L, L, ACT.Exp, scale=-1.0))
                        nc.scalar.activation(L, L, ACT.Ln, bias=1.0).then_inc(l_ready.sem, 1)
                    if n:
                        act.wait_ge(*warg_ready.due(me))
                        nc.scalar.activation(at(1536, 1536), at(1536, 1536), ACT.Exp).then_inc(w_raw.sem, 1)
                        transposed_high(n - 1)
                z_used.due(me)

            def exponentials(n):
                act.wait_ge(*max_ready.due(me))
                s0, m0 = (n % 2) * 1536, (n % 2) * 8
                for s in range(HG):
                    for qt in range(TT):
                        e = at(s0 + s * 256, 256) if qt else at(s0 + 1024 + s * P, P)
                        c, to = m0 + qt * HG + s, m0 + qt * HG + SLOT_HEAD[s]
                        ins = nc.scalar.activation(e, e, ACT.Exp, bias=nmax[:, c:c + 1], accum_out=rsum[:, to:to + 1])
                ins.then_inc(p_done.sem, 1)

            def softmax_attention(jobs):
                for n in range(len(jobs) + 1):
                    if n < len(jobs):
                        g, br = jobs[n]
                        if br == "slc":
                            act.wait_ge(*cs_ready.due(me))
                            nc.scalar.activation(at(5856, 256), at(5856, 256), ACT.Exp).then_inc(cp_exp.sem, 1)
                        exponentials(n)
                    if n:
                        g, br = jobs[n - 1]
                        act.wait_ge(*t_full.due(me))
                        nc.scalar.activation(at(3072, 1024), ps[:, 3 * 512:5 * 512], ACT.Copy).then_inc(tA_done.sem, 1)
                        if br != "slc":
                            act.wait_ge(*hT_full.due(me))
                            nc.scalar.activation(chunk(hT_hi, 2 * g, 2), bank(7), ACT.Copy).then_inc(hT_hi_done.sem, 1)

            def fox(u0):
                nc.scalar.preload_act_table_set("natural_log_exp_and_others")
                act.wait_ge(*proj_full.due(me))
                nc.scalar.activation(fl[:, 0:HEADS], bank(0, 0, HEADS), ACT.Copy).then_inc(proj_free[0].sem, 1)
                split_to(u0 + 6)
                act.wait_ge(*fl_soft.due(me))
                tmp = at(6144, 2 * HEADS)
                step(nc.scalar.activation(tmp, fl, ACT.Abs))
                step(nc.scalar.activation(tmp, tmp, ACT.Exp, scale=-1.0))
                nc.scalar.activation(tmp, tmp, ACT.Ln, bias=1.0).then_inc(l_ready.sem, 1)
                qkv(u0 + 1)
                split_to(u0 + 17)
                for b in range(4):
                    act.wait_ge(*qk_full.due(me))
                    nc.scalar.activation(at(QT + b * 512, 512), bank(b), ACT.Copy, scale=QSCALE).then_inc(tr_act.sem, 1)
                qk_full.due(me, 4)
                softmax_attention([(g, "fox") for g in range(GROUPS)])

            def nsa(u0):
                for b in range(5):
                    if b < 2:
                        dst = at(b * 512, 512)
                    else:
                        off, stride = [(2048, 512), (3072, 1024), (3584, 1024)][b - 2]
                        dst = at(off, 2 * stride).rearrange("p (s d) -> p s d", s=2)[:, :, 0:256]
                    evacuate(dst, bank(0) if b < 2 else bank(0).rearrange("p (s d) -> p s d", s=2))
                    split_to(u0 + 5 + 2 * (b + 1))
                evacuate(at(5120, 48), bank(0, 0, 48))
                split_to(u0 + 17)
                act.wait_ge(*proj_free[0].due(me, 6))
                act.wait_ge(*proj_free[1].due(me, 6))
                nc.scalar.activation(at(5120, 96), at(5120, 96), ACT.Sigmoid).then_inc(gates_ready.sem, 1)
                for b in range(2):
                    act.wait_ge(*qk_full.due(me))
                    nc.scalar.activation(at(QT + b * 512, 512), bank(b), ACT.Copy, scale=QSCALE).then_inc(tr_act.sem, 1)
                qk_full.due(me, 2)
                for b in range(2):
                    act.wait_ge(*qk_full.due(me))
                    nc.scalar.activation(at(KT + b * 512, 512), bank(4 + b), ACT.Copy).then_inc(tr_act.sem, 1)
                qk_full.due(me, 2)
                for b in range(2):
                    act.wait_ge(*qk_full.due(me))
                    src, dst = bank(b).rearrange("p (g t) -> p g t", g=2), at(b * 512, 512).rearrange("p (g t) -> p g t", g=2)
                    nc.scalar.activation(dst[0:DH], src[0:DH], ACT.Copy)
                    nc.scalar.activation(dst[DH:P, :, 0:TOKENS - 1], src[DH:P, :, 1:TOKENS], ACT.Copy).then_inc(tr_act.sem, 1)
                qk_full.due(me, 2)
                act.wait_ge(*win_tmp.due(me))
                nc.scalar.activation(hT_hi[:, 0:1920], at(2048, 1920), ACT.Copy).then_inc(win_hi.sem, 1)
                nc.scalar.preload_act_table(ACT.Silu)
                act.wait_ge(*zeros_ready.due(me))
                for kv in range(2):
                    act.wait_ge(unit_used.sem, u0 + 13 + 2 * kv)
                    for fc in range(2):
                        dst = at(5216 + (kv * 2 + fc) * 128, 128).rearrange("p (g c) -> p g c", g=GROUPS)[:, :, 0:NCMP]
                        src = bank(4 + 2 * kv + fc, 0, 60).rearrange("p (g c) -> p g c", g=GROUPS)
                        ins = nc.scalar.activation(dst, src, ACT.Silu)
                    ins.then_inc(hidc_ready.sem, 1)
                split_to(u0 + 19)
                nc.scalar.preload_act_table(ACT.Exp)
                softmax_attention([(g, br) for g in range(GROUPS) for br in ("slc", "win")])

            def pool(u0):
                for b in range(2):
                    evacuate(at(b * 512, 512), bank(0))
                    split_to(u0 + 5 + 2 * (b + 1))
                act.wait_ge(*proj_free[0].due(me, 2))
                act.wait_ge(unit_used.sem, u0 + 4)
                nc.scalar.activation(hT_hi[:, 0:DM], at(0, DM), ACT.Copy).then_inc(u_hi_done.sem, 1)
                act.wait_ge(*proj_free[1].due(me, 2))
                nc.scalar.activation(hT_hi[:, DM:2 * DM], at(DM, DM), ACT.Copy).then_inc(u_hi_done.sem, 1)
                act.wait_ge(unit_used.sem, u0 + 5)
                for b in range(4):
                    act.wait_ge(*pooled.due(me))
                    nc.scalar.activation(chunk(hT_hi, 2 * b, 2), at(2048 + b * 512, 512), ACT.Copy).then_inc(hT_hi_done.sem, 1)

            def ple(u0):
                nc.scalar.preload_act_table(ACT.Sigmoid)
                for q in range(4):
                    if q < 3:
                        act.wait_ge(*quarter_full.due(me))
                    else:
                        act.wait_ge(unit_used.sem, u0 + 5)
                    nc.scalar.activation(at(q * 512, 512), bank(q), ACT.Sigmoid).then_inc(sg_ready.sem, 1)

            act.wait_ge(const_in.sem, 32)
            act.wait_ge(x_in_done.sem, 16)
            nc.scalar.activation(q_gain8, C("q_gain"), ACT.Copy, scale=QSCALE).then_inc(proj_free[0].sem, 1)
            norms = 0
            for s, ((kind, n), u0) in enumerate(zip(stages, starts)):
                square_x(s)
                if kind == "ple":
                    act.wait_ge(*row_in.due(me, 16))
                    nc.scalar.activation(chunk(hid_hi, 0, 2), at(9216, 512), ACT.Copy).then_inc(p_hi_done.sem, 1)
                if kind == "ffn":
                    nc.scalar.preload_act_table(ACT.Silu)
                split_to(u0 + 5)
                h_high(norms)
                norms += 1
                if kind == "ffn":
                    mlp(u0, FFN_BLOCKS, 2, 4, 2, False)
                    quarter_full.due(me, 3)
                elif kind == "mlp":
                    mlp(u0, MLP_BLOCKS, 4, 2, 3, True)
                    row_in.due(me, 16)
                    square_acc(u0 + n)
                else:
                    {"stick": stick, "ple": ple, "pool": pool, "nsa": nsa, "fox": fox}[kind](u0)
                    if kind in ("nsa", "fox"):
                        row_in.due(me, 16)
                        square_acc(u0 + n)
                    elif kind == "pool":
                        row_in.due(me, 32)
                        quarter_full.due(me, 3)
                    elif kind == "stick":
                        quarter_full.due(me, 3)

        @block.vector
        def _(dve):
            me = "dve"

            def split_to(n, t=None):
                n = min(n, units_total)
                while split[me] < n:
                    u = split[me]
                    split[me] += 1
                    dve.wait_ge(hi_done.sem, u + 1 + (t.i * t.units if t else 0))
                    r = u % RAW
                    nc.vector.tensor_tensor(unit_cols(w_lo, u, 0, UNIT), raw[:, r * UNIT:(r + 1) * UNIT], f(unit_cols(w_hi, u, 0, UNIT)),
                                            ALU.subtract).then_inc(lo_done.sem, 1)

            def step(ins):
                ins.then_inc(dve_step.sem, 1)
                dve.wait_ge(*dve_step.due(me))

            def normalise():
                for tok in range(TT):
                    dve.wait_ge(*rstd_ready.due(me))
                    nc.vector.tensor_scalar(at(tok * DM, DM), xs(tok), rstd[:, tok:tok + 1], None, ALU.mult).then_inc(xn_ready.sem, 1)

            def h_low(n):
                for b in range(4):
                    dve.wait_ge(*hT_hi_done.due(me))
                    for c in (2 * b, 2 * b + 1):
                        ins = nc.vector.scalar_tensor_tensor(chunk(hT_lo, c), bank(b, (c % 2) * TOKENS, TOKENS), C("gains", n * KC + c, 1),
                                                             f(chunk(hT_hi, c)), ALU.mult, ALU.subtract)
                    ins.then_inc(hT_ready.sem, 1)

            def mlp(u0, blocks, hc, turns, per_turn, relu):
                step_u = 2 + hc // 2

                def combine(tok, t):
                    dve.wait_ge(*silu_done.due(me, turn=t))
                    dst = at(ACT_AT + tok * 512, 512 if relu else 256)
                    a = sil[:, tok * 512:tok * 512 + (512 if relu else 256)]
                    nc.vector.tensor_tensor(dst, a, a if relu else bank(tok, 256, 256), ALU.mult).then_inc(hid_ready.sem, 1)

                def hidden_low(t=None):
                    for b in range(hc // 2):
                        dve.wait_ge(*hidT_hi.due(me, turn=t))
                        nc.vector.tensor_tensor(chunk(hid_lo, 2 * b, 2), bank(2 + b), f(chunk(hid_hi, 2 * b, 2)), ALU.subtract).then_inc(hidT_ready.sem, 1)

                def one(j, u, ahead, t=None):
                    if j:
                        hidden_low(t)
                    combine(0, t)
                    split_to(ahead - step_u // 2, t)
                    combine(1, t)
                    split_to(ahead, t)

                one(0, u0, u0 + 2 + step_u)
                one(1, u0 + 2, u0 + 2 + 2 * step_u)
                u = u0 + 2 + step_u
                each = {silu_done: 2 * per_turn, hidT_hi: per_turn * (hc // 2)}
                with dve.Fori(0, turns) as i:
                    t = Turn(i, each, per_turn * step_u)
                    for b in range(per_turn):
                        one(2 + b, u + b * step_u, u + (b + 2) * step_u, t)
                for s, n in each.items():
                    s.due(me, n * (turns - 1))
                split[me] += (turns - 1) * per_turn * step_u
                u += turns * per_turn * step_u
                for j in range(2 + turns * per_turn, blocks):
                    one(j, u, u + 2 * step_u)
                    u += step_u
                hidden_low()

            def add_to_x(kind, end, row):
                for tok in range(TT):
                    if kind in ("nsa", "fox", "mlp"):
                        dve.wait_ge(*rstd_ready.due(me))
                        if tok == 0:
                            dve.wait_ge(*row_in.due(me, 16))
                            quarter_full.due(me, 3)
                        acc = ps[:, (4 + 2 * tok) * 512:(6 + 2 * tok) * 512]
                        step(nc.vector.scalar_tensor_tensor(at(tok * DM, DM), acc, rstd[:, 2 + tok:3 + tok], at(row, DM), ALU.mult, ALU.mult))
                        nc.vector.tensor_tensor(xs(tok), xs(tok), at(tok * DM, DM), ALU.add).then_inc(x_ready.sem, 1)
                        continue
                    for half in range(2):
                        q = 2 * tok + half
                        a, xq = bank(4 + q), xs(tok, half * 512, 512)
                        if kind == "ple":
                            dve.wait_ge(*sg_ready.due(me))
                            step(nc.vector.tensor_tensor(at(q * 512, 512), at(q * 512, 512), a, ALU.mult))
                            ins = nc.vector.tensor_tensor(xq, xq, at(q * 512, 512), ALU.add)
                        else:
                            if q < 3:
                                dve.wait_ge(*quarter_full.due(me))
                            else:
                                dve.wait_ge(unit_used.sem, end)
                            if kind == "ffn":
                                ins = nc.vector.scalar_tensor_tensor(xq, a, 0.5, xq, ALU.mult, ALU.add)
                            elif kind == "stick":
                                ins = nc.vector.tensor_tensor(xq, a, xq, ALU.add)
                            else:
                                step(nc.vector.tensor_tensor(at(q * 512, 512), a, at(row + half * 512, 512), ALU.mult))
                                ins = nc.vector.tensor_tensor(xq, xq, at(q * 512, 512), ALU.add)
                        if half == 1:
                            ins.then_inc(x_ready.sem, 1)
                if kind == "ple":
                    quarter_full.due(me, 3)

            def evacuate(dst, src, done, t=None):
                dve.wait_ge(unit_used.sem, done + (t.i * t.units if t else 0))
                nc.vector.tensor_copy(dst, src).then_inc(proj_free[1].sem, 1)

            def qkv(u0):
                with dve.Fori(0, 2) as i:
                    t = Turn(i, {}, 6)
                    for b in range(3):
                        evacuate(arena[:, bass.ds(i * 512 + (QKV + b * 2048 + DM), 512)], bank(1), u0 + 2 * b + 2, t)
                        split_to(u0 + 5 + 2 * (b + 1), t)
                split[me] += 6

            def stick(u0):
                qkv(u0)
                split_to(u0 + 16)
                secs = at(QKV, 4096).rearrange("p (s t d) -> p s t d", s=2, t=TT)
                for tok in range(TT):
                    dve.wait_ge(*sq_ready.due(me))
                    nc.vector.tensor_reduce(ssq, at(6144 + tok * 2048, 2048).rearrange("p (h d) -> p h d", d=DH), AX.X, ALU.add).then_inc(ssq_ready.sem, 1)
                    dve.wait_ge(*rstdq_ready.due(me))
                    v = secs[:, :, tok, :].rearrange("p s (h d) -> p s h d", d=DH)
                    r = rstdq.rearrange("p (s h) -> p s h", s=2)
                    for s in range(2):
                        ins = nc.vector.tensor_tensor(v[:, s], v[:, s], r[:, s].unsqueeze(2).broadcast_to((P, HEADS, DH)), ALU.mult)
                    ins.then_inc(qn_ready.sem, 1)
                qk_full.due(me, 4)
                for b in range(4):
                    dve.wait_ge(*qk_full.due(me))
                    nc.vector.tensor_scalar(at(KT + b * 512, 512), bank(4 + b), C("k_gain"), None, ALU.mult).then_inc(tr_dve.sem, 1)

                for n in range(GROUPS + 1):
                    if n:
                        dve.wait_ge(*after_full.due(me))
                        dve.wait_ge(*z_used.due(me))
                        ls = at(1536, 1536)
                        nc.vector.tensor_tensor(ls, ls, ps[:, 3 * 512:6 * 512], ALU.add).then_inc(warg_ready.sem, 1)
                    if n < GROUPS:
                        dve.wait_ge(*l_ready.due(me))
                        nc.vector.scalar_tensor_tensor(at(3072, 1024), ps[:, 0:1024], 0.0, at(0, 1024), ALU.max, ALU.add)
                        nc.vector.scalar_tensor_tensor(at(ACT_AT, 512), ps[:, 1024:1536], 0.0, at(1024, 512), ALU.max, ALU.add).then_inc(nst_raw.sem, 1)
                    if n:
                        dve.wait_ge(*hT_hi_done.due(me))
                        b = 6 + (n - 1) % 2
                        nc.vector.tensor_tensor(chunk(hT_lo, 2 * (n - 1), 2), bank(b), f(chunk(hT_hi, 2 * (n - 1), 2)), ALU.subtract).then_inc(hT_ready.sem, 1)
                    if n < GROUPS:
                        nc.vector.scalar_tensor_tensor(at(1536, 1536), ps[:, 0:1536], 0.0, at(0, 1536), ALU.min, ALU.subtract).then_inc(z_used.sem, 1)

            def masked_scores(n, fox_group=None):
                dve.wait_ge(*s_full.due(me))
                s0, m0 = (n % 2) * 1536, (n % 2) * 8
                sA, sB = at(s0, 1024).rearrange("p (h k) -> p h k", h=HG), at(s0 + 1024, 512).rearrange("p (h k) -> p h k", h=HG)
                if fox_group is None:
                    nc.vector.tensor_tensor(sA, ps[:, 0:1024].rearrange("p (h k) -> p h k", h=HG),
                                            K("mask").unsqueeze(1).broadcast_to((P, HG, 2 * P)), ALU.add)
                    ins = nc.vector.tensor_tensor(sB, bank(2).rearrange("p (h k) -> p h k", h=HG),
                                                  K("mask", P, P).unsqueeze(1).broadcast_to((P, HG, P)), ALU.add)
                else:
                    for s in range(HG):
                        h = HG * fox_group + SLOT_HEAD[s]
                        nc.vector.scalar_tensor_tensor(sA[:, s], ps[:, s * 256:(s + 1) * 256], cq[:, HEADS + h:HEADS + h + 1], K("mask"), ALU.add, ALU.add)
                        ins = nc.vector.scalar_tensor_tensor(sB[:, s], bank(2, s * P, P), cq[:, h:h + 1], K("mask", P, P), ALU.add, ALU.add)
                ins.then_inc(s_used.sem, 1)
                dve.wait_ge(*s_used.due(me))
                nc.vector.tensor_reduce(nmax[:, m0:m0 + HG], sB, AX.X, ALU.max, negate=True)
                nc.vector.tensor_reduce(nmax[:, m0 + HG:m0 + 2 * HG], sA, AX.X, ALU.max, negate=True).then_inc(max_ready.sem, 1)

            def weights_down():
                dve.wait_ge(*t_full.due(me))
                nc.vector.tensor_copy(at(ACT_AT, 512), bank(5)).then_inc(tB_done.sem, 1)

            def group_low(g):
                dve.wait_ge(*hT_hi_done.due(me))
                nc.vector.tensor_tensor(chunk(hT_lo, 2 * g, 2), bank(7), f(chunk(hT_hi, 2 * g, 2)), ALU.subtract).then_inc(hT_ready.sem, 1)

            rows = TT * HG

            def by_row(ap):
                return ap.rearrange("p (a d) -> p a d", a=rows)

            def per_row(c, d=DH):
                return c.unsqueeze(2).broadcast_to((P, rows, d))

            O = by_row(at(ACT_AT + 512, 512))

            def fox(u0):
                evacuate(fl[:, HEADS:2 * HEADS], bank(1, 0, HEADS), u0 + 1)
                dve.wait_ge(*proj_free[0].due(me))
                dve.wait_ge(*proj_free[1].due(me))
                fl3 = fl.rearrange("p (t h) -> p t h", t=TT)
                nc.vector.tensor_tensor(fl3, fl3, C("b_f").unsqueeze(1).broadcast_to((P, TT, HEADS)), ALU.add).then_inc(fl_soft.sem, 1)
                split_to(u0 + 6)
                dve.wait_ge(*l_ready.due(me))
                nc.vector.scalar_tensor_tensor(fl, fl, 0.0, at(6144, 2 * HEADS), ALU.min, ALU.subtract).then_inc(logf_ready.sem, 1)
                qkv(u0 + 1)
                split_to(u0 + 17)
                dve.wait_ge(*c_full.due(me))
                nc.vector.tensor_copy(cq, bank(2, 0, 2 * HEADS))
                nc.vector.tensor_scalar(sil[0:HEADS, 0:TOKENS], ps[0:HEADS, 3 * 512:3 * 512 + TOKENS], -1.0, None, ALU.mult).then_inc(c_ready.sem, 1)
                qk_full.due(me, 4)
                for b in range(4):
                    dve.wait_ge(*qk_full.due(me))
                    nc.vector.tensor_copy(at(KT + b * 512, 512), bank(4 + b)).then_inc(tr_dve.sem, 1)
                for n in range(GROUPS + 1):
                    if n < GROUPS:
                        masked_scores(n, n)
                    if n:
                        g, m0 = n - 1, ((n - 1) % 2) * 8
                        weights_down()
                        dve.wait_ge(*pv_full.due(me))
                        step(nc.vector.reciprocal(rinv[:, m0:m0 + 8], rsum[:, m0:m0 + 8]))
                        nc.vector.tensor_tensor(O, by_row(bank(6)), per_row(rinv[:, m0:m0 + 8]), ALU.mult).then_inc(sums_used.sem, 1)
                        group_low(g)

            def rotate(x, tok, heads, turn, last):
                x1, x2 = x[:, :, 0:32], x[:, :, 32:64]
                c = K("cos", tok * 32, 32).unsqueeze(1).broadcast_to((P, heads, 32))
                s = K("sin", tok * 32, 32).unsqueeze(1).broadcast_to((P, heads, 32))
                t = [at(KT + turn % 2 * 1536 + i * 512, heads * 32).rearrange("p (h d) -> p h d", h=heads) for i in range(3)]
                nc.vector.tensor_tensor(t[0], x1, c, ALU.mult)
                nc.vector.tensor_tensor(t[1], x2, s, ALU.mult)
                nc.vector.tensor_tensor(t[2], x1, s, ALU.mult)
                step(nc.vector.tensor_tensor(x2, x2, c, ALU.mult))
                nc.vector.tensor_tensor(x1, t[0], t[1], ALU.subtract)
                ins = nc.vector.tensor_tensor(x2, x2, t[2], ALU.add)
                if last:
                    ins.then_inc(qn_ready.sem, 1)

            def nsa(u0):
                for b in range(5):
                    if b < 2:
                        dst, src = at(DM + b * 512, 512), bank(1)
                    else:
                        off, stride = [(2048, 512), (3072, 1024), (3584, 1024)][b - 2]
                        dst = at(off, 2 * stride).rearrange("p (s d) -> p s d", s=2)[:, :, 256:512]
                        src = bank(1).rearrange("p (s d) -> p s d", s=2)
                    evacuate(dst, src, u0 + 2 * b + 2)
                    split_to(u0 + 5 + 2 * (b + 1))
                evacuate(at(5168, 48), bank(1, 0, 48), u0 + 11)
                split_to(u0 + 17)
                for tok in range(TT):
                    dve.wait_ge(*proj_free[tok].due(me, 14))
                for tok in range(TT):
                    rotate(at(tok * DM, DM).rearrange("p (h d) -> p h d", d=DH), tok, HEADS, tok, True)
                for tok in range(TT):
                    for i, sec in enumerate((2048, 3072, 3584)):
                        rotate(at(sec + tok * 256, 256).rearrange("p (h d) -> p h d", d=DH), tok, GROUPS, TT + 3 * tok + i, sec == 3584)
                qk_full.due(me, 2)
                for b in (2, 3):
                    dve.wait_ge(*qk_full.due(me))
                    nc.vector.tensor_scalar(at(QT + b * 512, 512), bank(b), QSCALE, None, ALU.mult).then_inc(tr_dve.sem, 1)
                qk_full.due(me, 2)
                for b in range(2):
                    dve.wait_ge(*qk_full.due(me))
                    nc.vector.tensor_copy(at(KT + 1024 + b * 512, 512), bank(6 + b)).then_inc(tr_dve.sem, 1)
                qk_full.due(me, 2)
                for b in range(2):
                    dve.wait_ge(*qk_full.due(me))
                    src = bank(2 + b).rearrange("p (g t) -> p g t", g=2)
                    dst = at(1024 + b * 512, 512).rearrange("p (g t) -> p g t", g=2)
                    nc.vector.tensor_copy(dst[0:DH], src[0:DH])
                    nc.vector.tensor_copy(dst[DH:P, :, 0:TOKENS - 1], src[DH:P, :, 1:TOKENS]).then_inc(tr_dve.sem, 1)
                dve.wait_ge(*tr_act.due(me, 10))
                dve.wait_ge(*tr_dve.due(me, 10))
                half = CMP_LEN // 2
                for kv in range(2):
                    pos = C("cmp_pos", kv * half, half).unsqueeze(2).broadcast_to((P, half, NCMP))
                    for g in range(GROUPS):
                        tokens = at(kv * 1024 + g * TOKENS, TOKENS)
                        src = tokens.rearrange("p (b j) -> p j b", j=CMP_STRIDE)
                        dst = at(2048 + kv * 960, 960).rearrange("p (j g b) -> p j g b", j=half, g=GROUPS)[:, :, g, :]
                        q = half // 2
                        nc.vector.tensor_tensor(dst[:, 0:q], src[:, 0:CMP_STRIDE:2, 0:NCMP], pos[:, 0:q], ALU.add)
                        ins = nc.vector.tensor_tensor(dst[:, q:half], src[:, 0:CMP_STRIDE:2, 1:NCMP + 1], pos[:, q:half], ALU.add)
                ins.then_inc(win_tmp.sem, 1)
                dve.wait_ge(*win_hi.due(me))
                nc.vector.tensor_tensor(hT_lo[:, 0:1920], at(2048, 1920), f(hT_hi[:, 0:1920]), ALU.subtract).then_inc(win_ready.sem, 1)
                split_to(u0 + 19)
                dve.wait_ge(*cmp_full.due(me))
                nc.vector.tensor_copy(at(5728, 128), bank(0, 0, 128))
                nc.vector.tensor_copy(sil[:, 512:768], bank(1, 0, 256)).then_inc(cmp_kv.sem, 1)
                dve.wait_ge(*cmp_kv.due(me))
                dve.wait_ge(*gates_ready.due(me))
                gates = at(5120, 96).rearrange("p (t h x) -> p t h x", t=TT, x=3)

                def coefficients(sums_of, g, x):
                    coef = coefs[:, x * 8:(x + 1) * 8]
                    step(nc.vector.reciprocal(coef, sums_of))
                    c3 = coef.rearrange("p (t h) -> p t h", t=TT)
                    step(nc.vector.tensor_tensor(c3, c3, gates[:, :, HG * g:HG * (g + 1), x], ALU.mult))
                    return coef

                scores = at(5856, 256)
                jobs = [(g, x) for g in range(GROUPS) for x in (1, 2)]
                for n in range(len(jobs) + 1):
                    if n < len(jobs):
                        g, x = jobs[n]
                        masked_scores(n)
                        if x == 1:
                            dve.wait_ge(*cs_full.due(me))
                            s4 = scores.rearrange("p (t h c) -> p t h c", t=TT, h=HG)
                            c4 = bank(7, 0, 256).rearrange("p (t h c) -> p t h c", t=TT, h=HG)
                            m3 = K("cmp_mask").rearrange("p (t c) -> p t c", t=TT)
                            for t in range(TT):
                                ins = nc.vector.tensor_tensor(s4[:, t], c4[:, t], m3[:, t].unsqueeze(1).broadcast_to((P, HG, CPAD)), ALU.add)
                            step(ins)
                            step(nc.vector.tensor_reduce(cmax, by_row(scores), AX.X, ALU.max))
                            nc.vector.tensor_tensor(by_row(scores), by_row(scores), per_row(cmax, CPAD), ALU.subtract).then_inc(cs_ready.sem, 1)
                    if n:
                        g, x = jobs[n - 1]
                        if x == 1:
                            dve.wait_ge(*cpT_full.due(me))
                            nc.vector.tensor_copy(sil[:, 256:512], bank(7, 256, 256))
                            nc.vector.tensor_tensor(sil[:, 768:1024].rearrange("p (h d) -> p h d", h=HG),
                                                    sil[:, 512 + g * DH:512 + (g + 1) * DH].unsqueeze(1).broadcast_to((P, HG, DH)),
                                                    K("head_block").unsqueeze(2).broadcast_to((P, HG, DH)), ALU.mult).then_inc(cpT_ready.sem, 1)
                            step(nc.vector.tensor_reduce(csum, by_row(scores), AX.X, ALU.add))
                            coef = coefficients(csum, g, 0)
                            c3 = coef.rearrange("p (t h) -> p t h", t=TT)
                            step(nc.vector.tensor_tensor(c3, c3, K("cmp_valid").unsqueeze(2).broadcast_to((P, TT, HG)), ALU.mult))
                            dve.wait_ge(*cpv_full.due(me))
                            nc.vector.tensor_tensor(O, by_row(bank(6)), per_row(coef), ALU.mult).then_inc(sums_used.sem, 1)
                        weights_down()
                        m0 = ((n - 1) % 2) * 8
                        coef = coefficients(rsum[:, m0:m0 + 8], g, x)
                        dve.wait_ge(*pv_full.due(me))
                        tmp = by_row(sil[:, 0:512])
                        step(nc.vector.tensor_tensor(tmp, by_row(bank(6)), per_row(coef), ALU.mult))
                        nc.vector.tensor_tensor(O, O, tmp, ALU.add).then_inc(sums_used.sem, 1)
                        if x == 2:
                            group_low(g)

            def pool(u0):
                for b in range(2):
                    evacuate(at(DM + b * 512, 512), bank(1), u0 + 2 * b + 2)
                    split_to(u0 + 5 + 2 * (b + 1))
                for tok in range(TT):
                    dve.wait_ge(*u_hi_done.due(me))
                    nc.vector.tensor_tensor(hT_lo[:, tok * DM:(tok + 1) * DM], at(tok * DM, DM), f(hT_hi[:, tok * DM:(tok + 1) * DM]),
                                            ALU.subtract).then_inc(u_ready.sem, 1)
                dve.wait_ge(*row_in.due(me, 32))
                for b in range(4):
                    if b < 3:
                        dve.wait_ge(*pool_full.due(me))
                    else:
                        dve.wait_ge(unit_used.sem, u0 + 5)
                    inv = at(7168 + b * TOKENS, TOKENS).unsqueeze(1).broadcast_to((P, 2, TOKENS))
                    nc.vector.tensor_tensor(at(2048 + b * 512, 512).rearrange("p (c t) -> p c t", c=2),
                                            bank(b).rearrange("p (c t) -> p c t", c=2), inv, ALU.mult).then_inc(pooled.sem, 1)
                for b in range(4):
                    dve.wait_ge(*hT_hi_done.due(me))
                    nc.vector.tensor_tensor(chunk(hT_lo, 2 * b, 2), at(2048 + b * 512, 512), f(chunk(hT_hi, 2 * b, 2)), ALU.subtract).then_inc(hT_ready.sem, 1)

            nc.vector.memset(nhalf, -0.5).then_inc(proj_free[1].sem, 1)
            dve.wait_ge(const_in.sem, 32)
            dve.wait_ge(x_in_done.sem, 16)
            norms = 0
            for (kind, n), u0 in zip(stages, starts):
                if kind == "ple":
                    dve.wait_ge(*p_hi_done.due(me))
                    row_in.due(me, 16)
                    nc.vector.tensor_tensor(chunk(hid_lo, 0, 2), at(9216, 512), f(chunk(hid_hi, 0, 2)), ALU.subtract).then_inc(p_ready.sem, 1)
                normalise()
                split_to(u0 + 5)
                h_low(norms)
                norms += 1
                if kind == "ffn":
                    mlp(u0, FFN_BLOCKS, 2, 4, 2, False)
                elif kind == "mlp":
                    mlp(u0, MLP_BLOCKS, 4, 2, 3, True)
                elif kind != "ple":
                    {"stick": stick, "pool": pool, "nsa": nsa, "fox": fox}[kind](u0)
                add_to_x(kind, u0 + n, ACT_AT if kind in ("nsa", "fox") else 6144)

        @block.gpsimd
        def _(pool):
            me = "pool"

            def step(ins):
                ins.then_inc(pool_step.sem, 1)
                pool.wait_ge(*pool_step.due(me))

            def inverse_rms(sums, tmp, dst, n, width):
                step(nc.gpsimd.tensor_scalar(tmp, sums, 1.0 / width, EPS, ALU.mult, ALU.add))
                return nc.gpsimd.tensor_tensor(dst, tmp, nhalf[:, 0:n], ALU.pow)

            def rows_rms(first):
                for tok in range(TT):
                    c = first + tok
                    pool.wait_ge(*ss_ready.due(me))
                    inverse_rms(ss[:, c:c + 1], var[:, c:c + 1], rstd[:, c:c + 1], 1, DM).then_inc(rstd_ready.sem, 1)

            def causal_zero(z, heads):
                return nc.gpsimd.affine_select(out=z, in_=z, compare_op=ALU.is_gt, fill=0.0, base=0,
                                               pattern=[[0, heads], [1, P]], channel_multiplier=-1)

            def diagonal_zero(a, b):
                causal_zero(a.rearrange("p (h q) -> p h q", h=HG)[:, :, 0:P], HG)
                return causal_zero(b.rearrange("p (h q) -> p h q", h=HG), HG)

            pool.wait_ge(proj_free[1].sem, 1)
            layer, row = 0, 0
            for (kind, _), nxt in zip(stages, stages[1:] + [("", 0)]):
                rows_rms(0)
                if kind == "stick":
                    for tok in range(TT):
                        pool.wait_ge(*ssq_ready.due(me))
                        inverse_rms(ssq, varq, rstdq, 2 * HEADS, DH).then_inc(rstdq_ready.sem, 1)
                    for n in range(GROUPS + 1):
                        if n < GROUPS:
                            pool.wait_ge(*nst_raw.due(me))
                            diagonal_zero(at(3072, 1024), at(ACT_AT, 512)).then_inc(nst_ready.sem, 1)
                        if n:
                            pool.wait_ge(*w_raw.due(me))
                            diagonal_zero(at(1536, 1024), at(2560, 512)).then_inc(w_ready.sem, 1)
                    hT_ready.due(me, 8)
                elif kind == "pool":
                    pool.wait_ge(*hT_ready.due(me, 4))
                    pool.dma_start(at(6144, DM), rows_in[row]).then_inc(row_in.sem, 16)
                    pool.dma_start(at(7168, 4 * TOKENS), count_in).then_inc(row_in.sem, 16)
                    row += 1
                    hT_ready.due(me, 4)
                elif kind == "ffn":
                    pool.wait_ge(*hT_ready.due(me, 4))
                    if nxt[0] == "ple":
                        pool.dma_start(at(9216, 2 * TOKENS), p_in[layer]).then_inc(row_in.sem, 16)
                        layer += 1
                elif kind == "ple":
                    hT_ready.due(me, 4)
                else:
                    if kind == "nsa":
                        nc.gpsimd.memset(at(5216, 512), 0.0).then_inc(zeros_ready.sem, 1)
                    pool.wait_ge(*hT_ready.due(me, 4 if kind == "mlp" else 8))
                    pool.dma_start(at(6144 if kind == "mlp" else ACT_AT, DM), rows_in[row]).then_inc(row_in.sem, 16)
                    row += 1
                    rows_rms(2)



def chunks(w):
    k, n = w.shape[0] // P, w.shape[1]
    return w.reshape(k, P, n).transpose(1, 0, 2).reshape(P, k * n)


def as_units(a):
    n = -(-a.shape[1] // UNIT)
    if a.shape[1] != n * UNIT:
        a = np.concatenate([a, np.zeros((P, n * UNIT - a.shape[1]), a.dtype)], axis=1)
    return [a[:, i * UNIT:(i + 1) * UNIT] for i in range(n)]


def interleave(up, down):
    out = list(up[0])
    for j in range(1, len(up)):
        out += up[j] + down[j - 1]
    return out + down[-1]


def ffn_units(gu, down):
    up = [as_units(chunks(np.concatenate([gu[:, 256 * j:256 * (j + 1)], gu[:, D_FF + 256 * j:D_FF + 256 * (j + 1)]], axis=1)))
          for j in range(FFN_BLOCKS)]
    return interleave(up, [as_units(chunks(down[256 * j:256 * (j + 1)])) for j in range(FFN_BLOCKS)])


def mlp_units(w_up, w_down):
    return interleave([as_units(chunks(w_up[:, 512 * j:512 * (j + 1)])) for j in range(MLP_BLOCKS)],
                      [as_units(chunks(w_down[512 * j:512 * (j + 1)])) for j in range(MLP_BLOCKS)])


def block_units(w, order):
    return [u for b in order for u in as_units(chunks(w[:, 512 * b:512 * (b + 1)]))]


QKV_ORDER = [0, 2, 4, 1, 3, 5]


def band():
    out = np.zeros((TT, P, len(WINDOWS), TOKENS), np.float32)
    t = np.arange(TOKENS)
    for i, w in enumerate(WINDOWS):
        full = ((t[:, None] <= t[None, :]) & (t[:, None] > t[None, :] - w)).astype(np.float32)
        full[t, t] -= np.minimum(t + 1, w)
        out[:, :, i, :] = full.reshape(TT, P, TOKENS)
    return out.transpose(1, 0, 2, 3).reshape(P, -1)


def constants():
    out = np.zeros((P, NCONST), np.float32)

    def put(name, a):
        o, n = CONST[name]
        out[:, o:o + n] = np.asarray(a, np.float32).reshape(P, n)

    i = np.arange(P)
    put("ident", np.eye(P))
    put("after_neg", -(i[:, None] > i[None, :]).astype(np.float32))
    put("ones_neg", -np.ones((P, P)))
    put("upto", i[:, None] <= i[None, :])
    put("ones", np.ones((P, P)))
    put("mask", np.concatenate([np.zeros((P, P)), np.where(i[None, :] <= i[:, None], 0.0, NEG)], axis=1))
    inv = np.float32(10000.0) ** (-np.arange(0, DH, 2, dtype=np.float32) / np.float32(DH))
    angle = (np.arange(TOKENS, dtype=np.float32)[:, None] * inv[None, :]).astype(np.float32)
    put("cos", np.cos(angle).reshape(TT, P, 32).transpose(1, 0, 2))
    put("sin", np.sin(angle).reshape(TT, P, 32).transpose(1, 0, 2))
    t, c = np.arange(TOKENS), np.arange(CPAD)
    seen = (c[None, :] < NCMP) & (c[None, :] * CMP_STRIDE + CMP_LEN - 1 <= t[:, None])
    put("cmp_mask", np.where(seen, 0.0, NEG).reshape(TT, P, CPAD).transpose(1, 0, 2))
    put("cmp_valid", (t >= CMP_LEN - 1).astype(np.float32).reshape(TT, P).T)
    put("head_block", i[:, None] // CPAD == np.arange(HG)[None, :])
    return out


def small_parameters(v):
    out = np.zeros((P, NCOLS), np.float32)

    def put(name, a):
        o, n = COLS[name]
        out[:, o:o + n] = a.reshape(P, n)

    gains = [g[i] for i in range(2) for g in (v["norm_ffn1"], v["norm_mix"], v["norm_ffn2"], v["norm_ple"])]
    gains += [v["norm_g_2"][i, j] for i in range(2) for j in (0, 2)]
    put("gains", np.stack(gains).reshape(12, KC, P).transpose(2, 0, 1))
    put("q_gain", np.concatenate([v["q_norm"][0], v["q_norm"][0]]))
    put("k_gain", np.concatenate([v["k_norm"][0], v["k_norm"][0]]))
    put("cmp_pos", v["nsa_cmp_pos_2"][0].reshape(2, CMP_LEN // 2, 2, DH).transpose(2, 3, 0, 1))
    put("cmp_w2", v["nsa_cmp_w2_2"][0].reshape(2, 2, P, DH).transpose(2, 0, 1, 3))
    put("b_f", np.broadcast_to(v["fox_b_f_2"][0], (P, HEADS)))
    return out


def kernel(**inputs):
    import concourse.bacc as bacc
    from concourse.bass_utils import run_bass_kernel_spmd

    v = {k: np.asarray(a) for k, a in inputs.items()}
    units = []
    for i in range(2):
        units += ffn_units(v["w_ffn1_gu"][i], v["w_ffn1_down"][i])
        if i == 0:
            units += block_units(v["w_qkv"][0], QKV_ORDER) + block_units(v["w_o"][0], range(2))
        else:
            units += block_units(v["w_pool_in"][0], range(2)) + as_units(band())
            units += as_units(v["w_pool_grp"][0].reshape(4, 2, P, 256).transpose(2, 0, 1, 3).reshape(P, -1))
        units += ffn_units(v["w_ffn2_gu"][i], v["w_ffn2_down"][i])
        units += as_units(chunks(v["w_ple_proj"][i])) + block_units(v["w_ple_gate"][i], range(2))
    w = v["nsa_w_in_2"][0]
    units += block_units(w[:, :2560], range(5)) + as_units(chunks(w[:, 2560:]))
    for kv in range(2):
        units += as_units(chunks(v["nsa_cmp_w1_2"][0, kv]))
    units += block_units(v["nsa_w_out_2"][0], range(2)) + mlp_units(v["mlp_w_up_2"][0], v["mlp_w_down_2"][0])
    w = v["fox_w_in_2"][0]
    units += as_units(chunks(w[:, 3072:])) + block_units(w[:, :3072], QKV_ORDER)
    units += block_units(v["fox_w_out_2"][0], range(2)) + mlp_units(v["mlp_w_up_2"][1], v["mlp_w_down_2"][1])

    rows = [v["pool_scale"][0], v["norm_g_2"][0, 1], v["norm_g_2"][0, 3], v["norm_g_2"][1, 1], v["norm_g_2"][1, 3]]
    t = np.arange(TOKENS)
    counts = np.stack([np.float32(1) / np.minimum(t + 1, w).astype(np.float32) for w in WINDOWS])
    arrays = {
        "weights": np.stack(units + PAD_UNITS * [np.zeros((P, UNIT), np.float32)]),
        "x": np.ascontiguousarray(v["x"][0].reshape(TT, P, DM).transpose(1, 0, 2)),
        "constants": constants(),
        "parameters": small_parameters(v),
        "p": np.ascontiguousarray(v["p"][:, 0].transpose(0, 2, 1).reshape(2, 2, P, TOKENS).transpose(0, 2, 1, 3).reshape(2, P, 2 * TOKENS)),
        "rows": np.stack([np.broadcast_to(r, (P, DM)) for r in rows]),
        "counts": np.ascontiguousarray(np.broadcast_to(counts.reshape(1, -1), (P, 4 * TOKENS))),
    }
    nc = bacc.Bacc("TRN2", target_bir_lowering=False, num_devices=1)
    args = [nc.dram_tensor(n, a.shape, mybir.dt.float32, kind="ExternalInput").ap() for n, a in arrays.items()]
    out = nc.dram_tensor("out", (TT, P, DM), mybir.dt.float32, kind="ExternalOutput").ap()
    network_kernel(nc, *args, out)
    got = run_bass_kernel_spmd(nc, [arrays], core_ids=[0]).results[0]["out"]
    return got.reshape(1, TOKENS, DM)
```

```python
from contextlib import ExitStack

import numpy as np

import concourse.bass as bass
from concourse import mybir

P = 128
TOKENS, DM = 256, 1024
TT = TOKENS // P
KC = DM // P
HEADS, DH = 16, 64
PAIRS = HEADS // 2
SLOT_HEAD = (0, 2, 1, 3)
GROUPS = 4
HG = HEADS // GROUPS
PLE = 256
D_FF, D_MLP = 2816, 4096
FFN_BLOCKS = D_FF // 256
MLP_BLOCKS = D_MLP // 256
HC = 2
WINDOWS = (2, 4, 8, 16)
CMP_LEN, CMP_STRIDE = 32, 16
NCMP = (TOKENS - CMP_LEN) // CMP_STRIDE + 1
CPAD = 32
CMP_HID = 256
EPS = 1e-6
QSCALE = DH ** -0.5
NEG = -1e30

UNIT = 2048
RAW, RING = 3, 6

FFN_U = 3 * FFN_BLOCKS
MLP_U = 2 * MLP_BLOCKS
STAGES = [
    ("ffn", FFN_U), ("stick", 16), ("ffn", FFN_U), ("ple", 5),
    ("ffn", FFN_U), ("pool", 6), ("ffn", FFN_U), ("ple", 5),
    ("nsa", 19), ("mlp", MLP_U), ("fox", 17), ("mlp", MLP_U),
]

CONST = {}
_at = 0
for _name, _n in [("ident", P), ("after_neg", P), ("ones_neg", P), ("upto", P), ("ones", P),
                  ("mask", 2 * P), ("cos", TT * 32), ("sin", TT * 32), ("cmp_mask", TT * CPAD),
                  ("cmp_valid", TT), ("head_block", HG), ("parity", 2)]:
    CONST[_name] = (_at, _n)
    _at += _n
NCONST = _at
COLS = {}
_at = 0
for _name, _n in [("gains", 12 * KC), ("post_gains", 4 * KC), ("pool_scale", KC), ("q_gain", 1), ("k_gain", 1), ("cmp_pos", 2 * CMP_LEN // 2),
                  ("cmp_w2", 2 * 2 * DH), ("b_f", HEADS)]:
    COLS[_name] = (_at, _n)
    _at += _n
NCOLS = _at

QKV = 0
QT, KT = 6144, 8192
SQUARES = 4096
ACT_AT = 10240
CMP_K = 5728
NARENA = 11264

FOX_JOBS = [(g, "fox") for g in range(GROUPS)]
NSA_JOBS = [(g, b) for g in range(GROUPS) for b in ("cmp", "slc", "win")]


class Signal:

    def __init__(self, nc, ctx, name, free=0):
        self.sem = ctx.enter_context(nc.semaphore(name))
        self.free = free
        self.seen = {}

    def due(self, who, step=1, turn=None):
        v = self.seen.get(who, 0 if who == "pe" else self.free) + step
        self.seen[who] = v
        if turn is not None:
            v = v + turn.i * turn.each[self]
        return self.sem, v


class Turn:

    def __init__(self, i, each, units):
        self.i, self.each, self.units = i, each, units


def network_kernel(nc, stream, x_in, consts_in, cols_in, p_in, count_in, out):
    f32, f32r = mybir.dt.float32, mybir.dt.float32r
    ALU, ACT, AX = mybir.AluOpType, mybir.ActivationFunctionType, mybir.AxisListType
    stages = STAGES
    starts, units_total = [], 0
    for _, n in stages:
        starts.append(units_total)
        units_total += n

    ctx = ExitStack()
    with ctx:
        def sb(name, cols, dt=f32):
            return ctx.enter_context(nc.sbuf_tensor(name, [P, cols], dt))

        raw = sb("raw", RAW * UNIT)
        w_hi, w_lo = sb("w_hi", RING * UNIT, f32r), sb("w_lo", RING * UNIT, f32r)
        X = sb("X", KC * TOKENS)
        hT_hi, hT_lo = sb("hT_hi", KC * TOKENS, f32r), sb("hT_lo", KC * TOKENS, f32r)
        hid_hi, hid_lo = sb("hid_hi", 4 * TOKENS, f32r), sb("hid_lo", 4 * TOKENS, f32r)
        arena = sb("arena", NARENA)
        sil = sb("sil", TT * 512)
        const = sb("const", NCONST)
        cols = sb("cols", NCOLS)
        stat = sb("stat", 288)
        ps = ctx.enter_context(nc.psum_tensor("ps", [P, 8 * 512], f32))

        def bank(b, a=0, n=512):
            return ps[:, b * 512 + a:b * 512 + a + n]

        def at(off, n):
            return arena[:, off:off + n]

        NST = sil[:, 0:1024], at(ACT_AT, 512)
        LOGW = [(at(1536, 1024), at(2560, 512)), (at(3072, 1024), at(ACT_AT + 512, 512))]

        def K(name, a=0, n=None):
            o, m = CONST[name]
            return const[:, o + a:o + a + (m - a if n is None else n)]

        def C(name, a=0, n=None):
            o, m = COLS[name]
            return cols[:, o + a:o + a + (m - a if n is None else n)]

        def xs(c, n=1):
            return X[:, c * TOKENS:(c + n) * TOKENS]

        def f(ap):
            return ap.bitcast(f32)

        def chunk(t, c, n=1):
            return t[:, c * TOKENS:(c + n) * TOKENS]

        def lhs(t, c, tok):
            return t[:, c * TOKENS + tok * P:c * TOKENS + (tok + 1) * P]

        def unit_cols(t, u, a, n):
            s = (u % RING) * UNIT
            return t[:, s + a:s + a + n]

        ident = K("ident")
        var, rstd = stat[:, 0:TT], stat[:, 4:4 + TT]
        nhalf = stat[:, 12:44]
        ssq, varq, rstdq = stat[:, 44:60], stat[:, 76:92], stat[:, 108:124]
        q_gain8 = stat[:, 140:141]
        nmax, rsum, coefs = stat[:, 144:160], stat[:, 160:176], stat[:, 176:192]
        fl, cq = stat[:, 224:256], stat[:, 256:288]

        def S(name, free=0):
            return Signal(nc, ctx, name, free)

        const_in, x_in_done, row_in, out_done = S("const_in"), S("x_in_done"), S("row_in"), S("out_done")
        raw_in = [S(f"raw_in{r}") for r in range(RAW)]
        hi_done, lo_done, unit_used = S("hi_done"), S("lo_done"), S("unit_used")
        x_ready, squares_ready, sums_full, h_ready = S("x_ready"), S("squares_ready"), S("sums_full"), S("h_ready")
        var_ready, rstd_ready, rstd_full = S("var_ready"), S("rstd_ready"), S("rstd_full")
        hT_full, hT_hi_done, hT_ready = S("hT_full"), S("hT_hi_done"), S("hT_ready")
        gu_full, silu_done = S("gu_full"), S("silu_done")
        hid_ready, hid_hi_done, hid_split = S("hid_ready"), S("hid_hi_done"), S("hid_split")
        acc_full = S("acc_full")
        proj_full, proj_free = S("proj_full"), [S("proj_free0", 3), S("proj_free1", 3)]
        p_hi_done, p_ready, sg_ready = S("p_hi_done"), S("p_ready"), S("sg_ready")
        u_hi_done, u_ready, pool_full, pooled = S("u_hi_done"), S("u_ready"), S("pool_full"), S("pooled")
        sq_ready, ssq_ready, rstdq_ready, qn_ready = S("sq_ready"), S("ssq_ready"), S("rstdq_ready"), S("qn_ready")
        qk_full, tr_act, tr_dve = S("qk_full"), S("tr_act"), S("tr_dve")
        z_full, z_used, l_ready, nst_raw, nst_ready = S("z_full"), S("z_used"), S("l_ready"), S("nst_raw"), S("nst_ready")
        after_full, warg_ready, w_raw, w_ready = S("after_full"), S("warg_ready"), S("w_raw"), S("w_ready")
        s_full, s_used, max_ready, p_done = S("s_full"), S("s_used"), S("max_ready"), S("p_done")
        t_full, tA_done, tB_done = S("t_full"), S("tA_done"), S("tB_done")
        coef_ready, pA_ready, pB_ready = S("coef_ready"), S("pA_ready"), S("pB_ready")
        zeros_ready = S("zeros_ready")
        gates_ready, win_tmp, win_hi, win_ready = S("gates_ready"), S("win_tmp"), S("win_hi"), S("win_ready")
        hidc_ready, cmp_full, cmp_kv = S("hidc_ready"), S("cmp_full"), S("cmp_kv")
        fl_soft, logf_ready, c_full, c_ready = S("fl_soft"), S("logf_ready"), S("c_full"), S("c_ready")
        act_step, dve_step, pool_step, even_done = S("act_step"), S("dve_step"), S("pool_step"), S("even_done")

        split = {"act": 0, "dve": 0}
        blocks_done = {"pe": 0, "act": 0, "dve": 0}

        def all_of(who, sigs, n):
            for s in sigs:
                s.due(who, n)

        block = ctx.enter_context(nc.Block())

        @block.sync
        def _(sp):
            sp.dma_start(const[:], consts_in).then_inc(const_in.sem, 16)
            sp.dma_start(cols[:], cols_in).then_inc(const_in.sem, 16)
            sp.dma_start(X[:], x_in).then_inc(x_in_done.sem, 16)
            view = stream.rearrange("(n r) p c -> n r p c", r=RAW)
            for r in range(RAW):
                sp.dma_start(raw[:, r * UNIT:(r + 1) * UNIT], view[0, r]).then_inc(raw_in[r].sem, 16)
            with sp.Fori(1, units_total // RAW) as n:
                for r in range(RAW):
                    sp.wait_ge(lo_done.sem, n * RAW + (r - RAW + 1))
                    sp.dma_start(raw[:, r * UNIT:(r + 1) * UNIT], view[n, r]).then_inc(raw_in[r].sem, 16)
            for b in range(4):
                sp.wait_ge(x_ready.sem, 4 * (len(stages) - 1) + b + 1)
                sp.dma_start(out[b], xs(2 * b, 2)).then_inc(out_done.sem, 16)
            sp.wait_ge(out_done.sem, 16 * 4)

        @block.tensor
        def _(pe):
            me = "pe"

            def unit_ready(u, t=None):
                pe.wait_ge(lo_done.sem, u + 1 + (t.i * t.units if t else 0))

            def three(dst, a_hi, a_lo, b_hi, b_lo, start, stop):
                nc.tensor.matmul(dst, a_hi, b_hi, start=start, stop=False, skip_group_check=True)
                nc.tensor.matmul(dst, a_hi, b_lo, start=False, stop=False, skip_group_check=True)
                return nc.tensor.matmul(dst, a_lo, b_hi, start=False, stop=stop, skip_group_check=True)

            def columns(us, width=512, fresh=False, t=None):
                per = KC // len(us)
                b0 = 2 * (blocks_done[me] % 3)
                blocks_done[me] += 1
                for tok in range(TT):
                    pe.wait_ge(*proj_free[tok].due(me, turn=t))
                for k in range(KC):
                    u = us[k // per]
                    if k % per == 0:
                        unit_ready(u, t)
                    if fresh:
                        pe.wait_ge(*hT_ready.due(me))
                    a = (k % per) * width
                    for tok in range(TT):
                        mm = three(bank(b0 + tok, 0, width), lhs(hT_hi, k, tok), lhs(hT_lo, k, tok), unit_cols(w_hi, u, a, width),
                                   unit_cols(w_lo, u, a, width), k == 0, k == KC - 1)
                        if (k, tok) == (KC - 1, 0):
                            mm.then_inc(proj_full.sem, 1)
                    if k % per == per - 1:
                        mm.then_inc(unit_used.sem, 1)

            def tile3(dst, u, a, b_hi, b_lo, start, stop):
                return three(dst, unit_cols(w_hi, u, a, P), unit_cols(w_lo, u, a, P), b_hi, b_lo, start, stop)

            def half(b0, m):
                return bank(b0 + m // 2, (m % 2) * TOKENS, TOKENS)

            def up(us, b0, tiles, full, fresh, t=None):
                per = KC // len(us)
                for k in range(KC):
                    u = us[k // per]
                    if k % per == 0:
                        unit_ready(u, t)
                    if fresh:
                        pe.wait_ge(*hT_ready.due(me))
                    for m in range(tiles):
                        mm = tile3(half(b0, m), u, ((k % per) * tiles + m) * P, chunk(hT_hi, k), chunk(hT_lo, k),
                                   k == 0 and m % 2 == 0, k == KC - 1)
                        if full and (k, m) == (KC - 1, 1):
                            mm.then_inc(full.sem, 1)
                    if k % per == per - 1:
                        mm.then_inc(unit_used.sem, 1)

            def project(u):
                pe.wait_ge(*hT_ready.due(me, GROUPS))
                for v in range(4):
                    unit_ready(u + v)
                for k in range(KC):
                    for m in range(KC):
                        v = u + 2 * (m // 4) + k // 4
                        mm = tile3(half(4, m), v, ((k % 4) * 4 + m % 4) * P, chunk(hT_hi, k), chunk(hT_lo, k),
                                   k == 0 and m % 2 == 0, k == KC - 1)
                        if (k, m) in ((4, 0), (KC - 1, 4), (KC - 1, 6), (KC - 1, 7)):
                            mm.then_inc(unit_used.sem, 1)
                        elif k == KC - 1 and m % 2 == 1:
                            mm.then_inc(acc_full.sem, 1)

            def sum_squares(pairs):
                for b in pairs:
                    pe.wait_ge(*squares_ready.due(me))
                    for c in (2 * b, 2 * b + 1):
                        for tok in range(TT):
                            mm = nc.tensor.matmul(bank(2, tok * P, P), at(SQUARES + c * TOKENS + tok * P, P), K("ones"),
                                                  start=c + tok == 0, stop=c == KC - 1, skip_group_check=True)
                if pairs[-1] == 3:
                    mm.then_inc(sums_full.sem, 1)

            def norm(first=0):
                sum_squares(range(first, 4))
                pe.wait_ge(*rstd_ready.due(me))
                for tok in range(TT):
                    mm = nc.tensor.matmul(bank(3, tok * P, P), rstd[:, tok:tok + 1].broadcast_to((P, P)), ident, start=True, stop=True, skip_group_check=True)
                mm.then_inc(rstd_full.sem, 1)

            def mlp(u0, blocks, ups, banks, turns, per_turn):
                step = ups + 1

                def down(u, first, last, t=None):
                    h = HC if last else 0
                    unit_ready(u, t)
                    pe.wait_ge(*hid_split.due(me, turn=t))
                    for b in range(4):
                        if last and b == 3:
                            sum_squares([0])
                        for c in range(HC):
                            for m in (2 * b, 2 * b + 1):
                                mm = tile3(half(4, m), u, c * DM + m * P, chunk(hid_hi, h + c), chunk(hid_lo, h + c),
                                           first and c == 0 and m % 2 == 0, last and c == HC - 1)
                        if b == 3:
                            mm.then_inc(unit_used.sem, 1)
                        elif last:
                            mm.then_inc(acc_full.sem, 1)

                def one(j, u, t=None):
                    up(list(range(u, u + ups)), ups * (j % banks), 2 * ups, gu_full if ups == 2 else None, j == 0, t)
                    if j:
                        down(u + ups, j == 1, False, t)

                one(0, u0)
                one(1, u0 + ups)
                u = u0 + ups + step
                with pe.Fori(0, turns) as i:
                    t = Turn(i, {hid_split: per_turn}, per_turn * step)
                    for b in range(per_turn):
                        one(2 + b, u + b * step, t)
                hid_split.due(me, per_turn * (turns - 1))
                u += turns * per_turn * step
                for j in range(2 + turns * per_turn, blocks):
                    one(j, u)
                    u += step
                down(u, False, True)

            def columns_t(us, t):
                b0 = 2 * (blocks_done[me] % 3)
                blocks_done[me] += 1
                for tok in range(TT):
                    pe.wait_ge(*proj_free[tok].due(me, turn=t))
                up(us, b0, 4, proj_full, False, t)

            def transpose_pairs(section, b0):
                for tok in range(TT):
                    pe.wait_ge(*qn_ready.due(me))
                    for p in range(PAIRS):
                        mm = nc.tensor.transpose(bank(b0 + p // 2, (p % 2) * TOKENS + tok * P, P),
                                                 at(section + tok * DM + p * P, P), ident)
                        if tok == 1 and p % 2 == 1:
                            mm.then_inc(qk_full.sem, 1)

            def head(off, h, a=0, n=TOKENS):
                r = DH * (h % 2)
                return arena[r:r + DH, off + (h // 2) * TOKENS + a:off + (h // 2) * TOKENS + a + n]

            def group_head(off, h, a=0, n=TOKENS):
                r, g = DH * (h % 2), h // HG
                return arena[r:r + DH, off + g * TOKENS + a:off + g * TOKENS + a + n]

            def A(b0, h, a, n):
                return ps[:, b0 * 512 + h * 256 + a:b0 * 512 + h * 256 + a + n]

            def stick(u0):
                each = {proj_free[0]: 3, proj_free[1]: 3, qn_ready: 2}

                def transpose_half(off, t):
                    pe.wait_ge(*qn_ready.due(me, turn=t))
                    for p in range(PAIRS // 2):
                        for tok in range(TT):
                            mm = nc.tensor.transpose(bank(6 + p // 2, (p % 2) * TOKENS + tok * P, P), at(off + tok * 512 + p * P, P), ident)
                        if p % 2 == 1:
                            mm.then_inc(qk_full.sem, 1)

                with pe.Fori(0, 2) as i:
                    t = Turn(i, each, 6)
                    columns([u0, u0 + 1], fresh=True, t=t)
                    columns([u0 + 2, u0 + 3], t=t)
                    transpose_half(0, t)
                    columns([u0 + 4, u0 + 5], t=t)
                    transpose_half(DM, t)
                for sig, n in each.items():
                    sig.due(me, n)
                pe.wait_ge(*tr_act.due(me, 4))
                pe.wait_ge(*tr_dve.due(me, 2))

                def scores(g):
                    if g:
                        pe.wait_ge(*z_used.due(me))
                    if g == GROUPS // 2:
                        pe.wait_ge(*tr_dve.due(me, 2))
                    for s in range(HG):
                        h = HG * g + SLOT_HEAD[s]
                        nc.tensor.matmul(A(0, s, 0, 256), head(KT, h, 0, P), head(QT, h), start=True, stop=True)
                        if s == 2:
                            pe.wait_ge(*even_done.due(me))
                        mm = nc.tensor.matmul(bank(2, s * P, P), head(KT, h, P, P), head(QT, h, P, P), start=True, stop=True)
                        if s == 1:
                            mm.then_inc(even_done.sem, 1)
                    mm.then_inc(z_full.sem, 1)

                def after(g):
                    pe.wait_ge(*nst_ready.due(me))
                    for b in range(2):
                        nc.tensor.matmul(bank(3 + b), K("after_neg"), NST[0][:, b * 512:(b + 1) * 512], start=True, stop=False, skip_group_check=True)
                        for s in (2 * b, 2 * b + 1):
                            nc.tensor.matmul(A(3, s, P, P), K("ones_neg"), NST[1][:, s * P:(s + 1) * P], start=False, stop=True, skip_group_check=True)
                    nc.tensor.matmul(bank(5), K("after_neg"), NST[1], start=True, stop=True).then_inc(after_full.sem, 1)

                def weighted(g):
                    pe.wait_ge(*w_ready.due(me))
                    wA, wB = LOGW[g % 2]
                    for s in range(HG):
                        j = SLOT_HEAD[s]
                        h = HG * g + j
                        r, o = DH * (h % 2), (6 + g % 2) * 512 + (j // 2) * TOKENS
                        v0, v1 = at(QKV + 4096 + h * DH, DH), at(QKV + 4096 + DM + h * DH, DH)
                        nc.tensor.matmul(ps[r:r + DH, o:o + 256], v0, wA[:, s * 256:(s + 1) * 256], start=True, stop=False, skip_group_check=True)
                        mm = nc.tensor.matmul(ps[r:r + DH, o + P:o + 256], v1, wB[:, s * P:(s + 1) * P], start=False, stop=True, skip_group_check=True)
                    mm.then_inc(hT_full.sem, 1)

                scores(0)
                for n in range(GROUPS + 1):
                    if n + 1 < GROUPS:
                        scores(n + 1)
                    if n < GROUPS:
                        after(n)
                    if n:
                        weighted(n - 1)
                z_used.due(me)
                project(u0 + 12)

            def softmax_attention(jobs, k_of, v_of, bias_of=None):
                heads_before = hT_ready.seen[me]

                def scores(n):
                    g, br = jobs[n]
                    if n:
                        pe.wait_ge(*s_used.due(me))
                    if br == "cmp":
                        for qt in range(TT):
                            for p in range(HG // 2):
                                c = (g * HG // 2 + p) * TOKENS + qt * P
                                mm = nc.tensor.matmul(bank(0, (qt * HG + 2 * p) * CPAD, 2 * CPAD), at(QT + c, P), at(CMP_K + g * 2 * CPAD, 2 * CPAD), start=True, stop=True, skip_group_check=True)
                        mm.then_inc(s_full.sem, 1)
                        return
                    one = bias_of is None
                    for s in range(HG):
                        h = HG * g + SLOT_HEAD[s]
                        nc.tensor.matmul(A(0, s, 0, 256), head(QT, h, P, P), k_of(br, h, 0, 256), start=True, stop=one, skip_group_check=True)
                        if not one:
                            nc.tensor.matmul(A(0, s, 0, 256), bias_of(h), sil[0:HEADS, 0:TOKENS], start=False, stop=True, skip_group_check=True)
                        if s == 2:
                            pe.wait_ge(*even_done.due(me))
                        mm = nc.tensor.matmul(bank(2, s * P, P), head(QT, h, 0, P), k_of(br, h, 0, P), start=True, stop=one, skip_group_check=True)
                        if not one:
                            mm = nc.tensor.matmul(bank(2, s * P, P), bias_of(h), sil[0:HEADS, 0:P], start=False, stop=True, skip_group_check=True)
                        if s == 1:
                            mm.then_inc(even_done.sem, 1)
                    mm.then_inc(s_full.sem, 1)

                def transposed(n):
                    g, br = jobs[n]
                    s0 = (n % 2) * 1536
                    pe.wait_ge(*pB_ready.due(me))
                    if br == "cmp":
                        for qt in range(TT):
                            mm = nc.tensor.transpose(bank(3, qt * P, P), at(s0 + qt * P, P), ident)
                    else:
                        pe.wait_ge(*pA_ready.due(me))
                        for s in range(HG):
                            sA, sB = at(s0 + s * 256, 256), at(s0 + 1024 + s * P, P)
                            nc.tensor.transpose(A(3, s, 0, P), sB, ident)
                            nc.tensor.transpose(A(3, s, P, P), sA[:, 0:P], ident)
                            mm = nc.tensor.transpose(bank(5, s * P, P), sA[:, P:256], ident)
                    mm.then_inc(t_full.sem, 1)

                def weighted(n):
                    g, br = jobs[n]
                    first = n == 0 or jobs[n - 1][0] != g
                    last = n == len(jobs) - 1 or jobs[n + 1][0] != g
                    pe.wait_ge(*tA_done.due(me))
                    if br != "cmp":
                        pe.wait_ge(*tB_done.due(me))
                    if first and g >= 2:
                        pe.wait_ge(hT_ready.sem, heads_before + g - 1)
                    tA, tB = at(3072, 1024), at(ACT_AT, 512)
                    for s in range(HG):
                        j = SLOT_HEAD[s]
                        h = HG * g + j
                        r, o = DH * (h % 2), (6 + g % 2) * 512 + (j // 2) * TOKENS
                        if br == "cmp":
                            mm = nc.tensor.matmul(ps[r:r + DH, o:o + TOKENS], sil[:, h * DH:(h + 1) * DH], tA[:, 0:TOKENS], start=first and j < 2, stop=last, skip_group_check=True)
                        else:
                            nc.tensor.matmul(ps[r:r + DH, o:o + TOKENS], v_of(br, h, 0), tA[:, s * 256:(s + 1) * 256], start=first and j < 2, stop=False, skip_group_check=True)
                            mm = nc.tensor.matmul(ps[r:r + DH, o + P:o + TOKENS], v_of(br, h, 1), tB[:, s * P:(s + 1) * P], start=False, stop=last, skip_group_check=True)
                    if last:
                        mm.then_inc(hT_full.sem, 1)

                scores(0)
                scores(1)
                for n in range(len(jobs)):
                    transposed(n)
                    if n + 2 < len(jobs):
                        scores(n + 2)
                    weighted(n)
                s_used.due(me)

            def fox(u0):
                columns([u0], width=HEADS, fresh=True)
                each = {proj_free[0]: 3, proj_free[1]: 3}
                with pe.Fori(0, 2) as i:
                    t = Turn(i, each, 6)
                    columns_t([u0 + 1, u0 + 2], t)
                    columns_t([u0 + 3, u0 + 4], t)
                    columns([u0 + 5, u0 + 6], t=t)
                for sig, n in each.items():
                    sig.due(me, n)
                pe.wait_ge(*logf_ready.due(me))
                lf = [fl[:, 0:HEADS], fl[:, HEADS:2 * HEADS]]
                nc.tensor.matmul(bank(6, 0, HEADS), K("upto"), lf[0], start=True, stop=True, skip_group_check=True)
                nc.tensor.matmul(bank(6, HEADS, HEADS), K("ones"), lf[0], start=True, stop=False, skip_group_check=True)
                nc.tensor.matmul(bank(6, HEADS, HEADS), K("upto"), lf[1], start=False, stop=True, skip_group_check=True)
                rows = ps[0:HEADS, 7 * 512:7 * 512 + TOKENS]
                nc.tensor.matmul(rows[:, 0:P], lf[0], K("upto"), start=True, stop=True, skip_group_check=True)
                nc.tensor.matmul(rows[:, P:TOKENS], lf[0], K("ones"), start=True, stop=False, skip_group_check=True)
                nc.tensor.matmul(rows[:, P:TOKENS], lf[1], K("upto"), start=False, stop=True, skip_group_check=True).then_inc(c_full.sem, 1)
                pe.wait_ge(*c_ready.due(me))
                for tok in range(TT):
                    pe.wait_ge(*proj_free[tok].due("pe_all", 21))
                softmax_attention(
                    FOX_JOBS, lambda br, h, a, n: head(KT, h, a, n),
                    lambda br, h, tok: at(QKV + 4096 + tok * DM + h * DH, DH),
                    lambda h: const[0:HEADS, CONST["ident"][0] + h:CONST["ident"][0] + h + 1].broadcast_to((HEADS, P)))
                project(u0 + 13)

            def nsa(u0):
                for b in range(5):
                    columns([u0 + 2 * b, u0 + 2 * b + 1], fresh=b == 0)
                columns([u0 + 10], width=3 * HEADS)
                transpose_pairs(0, 0)

                def group_keys(sec, b0):
                    for tok in range(TT):
                        for g in range(GROUPS):
                            for half in range(2):
                                c = (g % 2) * TOKENS + tok * P
                                dst = ps[DH * half:DH * half + DH, (b0 + g // 2) * 512 + c:(b0 + g // 2) * 512 + c + P]
                                mm = nc.tensor.matmul(dst, at(sec + tok * 256 + g * DH, DH), ident, start=True, stop=True, skip_group_check=True)
                            if tok == 1 and g % 2 == 1:
                                mm.then_inc(qk_full.sem, 1)

                for _ in range(TT):
                    pe.wait_ge(*qn_ready.due(me))
                group_keys(3072, 4)
                group_keys(3584, 6)
                for _ in range(2):
                    pe.wait_ge(*tr_act.due(me))
                    pe.wait_ge(*tr_dve.due(me))
                group_keys(2048, 0)
                group_keys(2560, 2)
                pe.wait_ge(*win_ready.due(me))
                for kv in range(2):
                    us = [u0 + 11 + 2 * kv, u0 + 12 + 2 * kv]
                    for u in us:
                        unit_ready(u)
                    for fc in range(2):
                        for jj in range(CMP_LEN // 2):
                            u, a = us[jj // 8], (jj % 8) * CMP_HID + fc * P
                            w = kv * 960 + jj * 60
                            dst = bank(4 + 2 * kv + fc, 0, 60)
                            nc.tensor.matmul(dst, unit_cols(w_hi, u, a, P), hT_hi[:, w:w + 60], start=jj == 0, stop=False, skip_group_check=True)
                            nc.tensor.matmul(dst, unit_cols(w_hi, u, a, P), hT_lo[:, w:w + 60], start=False, stop=False, skip_group_check=True)
                            mm = nc.tensor.matmul(dst, unit_cols(w_lo, u, a, P), hT_hi[:, w:w + 60], start=False, stop=jj == 15, skip_group_check=True)
                            if fc == 1 and jj % 8 == 7:
                                mm.then_inc(unit_used.sem, 1)
                for _ in range(2):
                    pe.wait_ge(*hidc_ready.due(me))
                def hidc(kv, fc, a, n):
                    return at(5216 + (kv * 2 + fc) * 128 + a, n)
                for half in range(2):
                    for fc in range(2):
                        nc.tensor.matmul(ps[DH * half:DH * half + DH, 0:128], C("cmp_w2", fc * DH, DH), hidc(0, fc, 0, 128),
                                         start=fc == 0, stop=fc == 1, skip_group_check=True)
                for g in range(GROUPS):
                    for r in range(HG):
                        for fc in range(2):
                            mm = nc.tensor.matmul(ps[CPAD * r:CPAD * r + CPAD, 512 + g * DH:512 + (g + 1) * DH], hidc(1, fc, g * CPAD, CPAD),
                                                  C("cmp_w2", 128 + fc * DH, DH), start=fc == 0, stop=fc == 1, skip_group_check=True)
                mm.then_inc(cmp_full.sem, 1)
                pe.wait_ge(*cmp_kv.due(me))
                for _ in range(4):
                    pe.wait_ge(*tr_dve.due(me))
                    pe.wait_ge(*tr_act.due(me))

                softmax_attention(
                    NSA_JOBS, lambda br, h, a, n: group_head(KT + (0 if br == "slc" else 1024), h, a, n),
                    lambda br, h, tok: at((4096 if br == "slc" else 4608) + tok * 256 + (h // HG) * DH, DH))
                project(u0 + 15)

            def pool(u0):
                columns([u0, u0 + 1], fresh=True)
                columns([u0 + 2, u0 + 3])
                ub = u0 + 4
                unit_ready(ub)
                for _ in range(TT):
                    pe.wait_ge(*u_ready.due(me))
                for c in range(KC):
                    for tt in range(TT):
                        rhs = unit_cols(w_hi, ub, (tt * 4 + c // 2) * TOKENS, TOKENS)
                        a = tt * DM + c * P
                        nc.tensor.matmul(bank(c // 2, (c % 2) * TOKENS, TOKENS), hT_hi[:, a:a + P], rhs, start=tt == 0, stop=False, skip_group_check=True)
                        mm = nc.tensor.matmul(bank(c // 2, (c % 2) * TOKENS, TOKENS), hT_lo[:, a:a + P], rhs, start=False, stop=tt == 1, skip_group_check=True)
                    if c == KC - 1:
                        mm.then_inc(unit_used.sem, 1)
                    elif c % 2 == 1:
                        mm.then_inc(pool_full.sem, 1)
                ug = u0 + 5
                unit_ready(ug)
                for g in range(4):
                    pe.wait_ge(*hT_ready.due(me))
                    for m in (2 * g, 2 * g + 1):
                        for c in range(2):
                            mm = tile3(half(4, m), ug, (g * 2 + c) * 256 + (m % 2) * P, chunk(hT_hi, 2 * g + c), chunk(hT_lo, 2 * g + c),
                                       c == 0 and m % 2 == 0, c == 1)
                    mm.then_inc((acc_full if g < 3 else unit_used).sem, 1)

            def ple(u0):
                unit_ready(u0)
                pe.wait_ge(*p_ready.due(me))
                for m in range(KC):
                    for c in range(2):
                        mm = tile3(half(4, m), u0, c * DM + m * P, chunk(hid_hi, c), chunk(hid_lo, c),
                                   c == 0 and m % 2 == 0, c == 1)
                mm.then_inc(unit_used.sem, 1)
                up([u0 + 1, u0 + 2], 0, 4, gu_full, True)
                up([u0 + 3, u0 + 4], 2, 4, gu_full, False)

            pe.wait_ge(const_in.sem, 32)
            before = None
            for (kind, _), u0 in zip(stages, starts):
                norm(1 if before == "ffn" else 0)
                if kind == "ffn":
                    mlp(u0, FFN_BLOCKS, 2, 2, 4, 2)
                elif kind == "mlp":
                    mlp(u0, MLP_BLOCKS, 1, 3, 4, 3)
                else:
                    {"stick": stick, "ple": ple, "pool": pool, "nsa": nsa, "fox": fox}[kind](u0)
                if kind in ("nsa", "fox", "mlp"):
                    norm(1 if kind == "mlp" else 0)
                before = kind

        @block.scalar
        def _(act):
            me = "act"

            def split_to(n, t=None):
                n = min(n, units_total)
                while split[me] < n:
                    u = split[me]
                    split[me] += 1
                    more = t.i * t.units if t else 0
                    act.wait_ge(raw_in[u % RAW].sem, 16 * (u // RAW + 1) + (t.i * (16 * t.units // RAW) if t else 0))
                    if u >= RING:
                        act.wait_ge(unit_used.sem, u - RING + 1 + more)
                    r = u % RAW
                    nc.scalar.activation(unit_cols(w_hi, u, 0, UNIT), raw[:, r * UNIT:(r + 1) * UNIT], ACT.Copy).then_inc(hi_done.sem, 1)

            def step(ins):
                ins.then_inc(act_step.sem, 1)
                act.wait_ge(*act_step.due(me))

            def square_x(s):
                for b in range(4):
                    if s > 0:
                        act.wait_ge(*x_ready.due(me))
                    nc.scalar.activation(at(SQUARES + b * 512, 512), xs(2 * b, 2), ACT.Square).then_inc(squares_ready.sem, 1)

            def square_acc(end):
                for b in range(4):
                    if b < 3:
                        act.wait_ge(*acc_full.due(me))
                    else:
                        act.wait_ge(unit_used.sem, end)
                    nc.scalar.activation(at(SQUARES + b * 512, 512), bank(4 + b), ACT.Square).then_inc(squares_ready.sem, 1)

            def h_high():
                for c in range(KC):
                    act.wait_ge(*h_ready.due(me))
                    nc.scalar.activation(chunk(hT_hi, c), at(c * TOKENS, TOKENS), ACT.Copy).then_inc(hT_hi_done.sem, 1)

            def mlp(u0, blocks, ups, banks, turns, per_turn):
                step_u = ups + 1

                def one(j, u, t=None):
                    more = t.i * t.units if t else 0
                    if ups == 2:
                        act.wait_ge(*gu_full.due(me, turn=t))
                    else:
                        act.wait_ge(unit_used.sem, u + 1 + more)
                    nc.scalar.activation(sil[:, 0:512], bank(ups * (j % banks)), ACT.Silu if ups == 2 else ACT.Relu).then_inc(silu_done.sem, 1)
                    last = j == blocks - 1
                    ahead = u + ups + RING
                    if not last:
                        split_to(ahead - 1, t)
                    act.wait_ge(*hid_ready.due(me, turn=t))
                    if j and not last:
                        act.wait_ge(unit_used.sem, u + step_u + more)
                    nc.scalar.activation(chunk(hid_hi, HC if last else 0, HC), at(ACT_AT, 512), ACT.Copy).then_inc(hid_hi_done.sem, 1)
                    split_to(ahead - 1 if last else ahead, t)

                one(0, u0)
                one(1, u0 + ups)
                u = u0 + ups + step_u
                each = {gu_full: per_turn, hid_ready: per_turn}
                with act.Fori(0, turns) as i:
                    t = Turn(i, each, per_turn * step_u)
                    for b in range(per_turn):
                        one(2 + b, u + b * step_u, t)
                if ups == 2:
                    gu_full.due(me, per_turn * (turns - 1))
                hid_ready.due(me, per_turn * (turns - 1))
                split[me] += (turns - 1) * per_turn * step_u
                u += turns * per_turn * step_u
                for j in range(2 + turns * per_turn, blocks):
                    one(j, u)
                    u += step_u

            def evacuate(dst, width=512, parts=1, t=None, scale=1.0):
                act.wait_ge(*proj_full.due(me, turn=t))
                src = bank(2 * (blocks_done[me] % 3), 0, width)
                blocks_done[me] += 1
                nc.scalar.activation(dst, src if parts == 1 else src.rearrange("p (s d) -> p s d", s=parts), ACT.Copy, scale=scale).then_inc(proj_free[0].sem, 1)

            def transposed_high(n):
                act.wait_ge(*hT_full.due(me))
                nc.scalar.activation(chunk(hT_hi, 2 * n, 2), bank(6 + n % 2), ACT.Copy).then_inc(hT_hi_done.sem, 1)

            def stick(u0):
                each = {proj_full: 3, proj_free[0]: 3, proj_free[1]: 3, qk_full: 4}
                with act.Fori(0, 2) as i:
                    t = Turn(i, each, 6)
                    for b, off in enumerate((0, DM)):
                        evacuate(at(off, 512), t=t)
                        if b == 1:
                            for half in range(2):
                                act.wait_ge(*qk_full.due(me, turn=t))
                                nc.scalar.activation(arena[:, bass.ds(i * DM + (QT + half * 512), 512)], bank(6 + half), ACT.Copy, scale=q_gain8).then_inc(tr_act.sem, 1)
                        for tok in range(TT):
                            act.wait_ge(*proj_free[tok].due(me, turn=t))
                        nc.scalar.activation(at(ACT_AT, DM), at(off, DM), ACT.Square).then_inc(sq_ready.sem, 1)
                        split_to(u0 + 5 + 2 * (b + 1), t)
                    evacuate(arena[:, bass.ds(i * 512 + (QKV + 4096), 512)], t=t)
                    split_to(u0 + 5 + 6, t)
                    qk_full.due(me, 2)
                    for tok in range(TT):
                        proj_free[tok].due(me)
                split[me] += 6
                for sig, n in each.items():
                    sig.due(me, n)
                nc.scalar.preload_act_table_set("natural_log_exp_and_others")

                def logs(n):
                    act.wait_ge(*z_full.due(me))
                    if n:
                        act.wait_ge(*z_used.due(me))
                    L = at(0, 1536)
                    step(nc.scalar.activation(L, ps[:, 0:1536], ACT.Abs))
                    step(nc.scalar.activation(L, L, ACT.Exp, scale=-1.0))
                    nc.scalar.activation(L, L, ACT.Ln, bias=1.0).then_inc(l_ready.sem, 1)

                logs(0)
                split_to(u0 + 16)
                for n in range(GROUPS + 1):
                    if n + 1 < GROUPS:
                        logs(n + 1)
                    if n < GROUPS:
                        act.wait_ge(*warg_ready.due(me))
                        nc.scalar.activation(LOGW[n % 2][0], LOGW[n % 2][0], ACT.Exp)
                        nc.scalar.activation(LOGW[n % 2][1], LOGW[n % 2][1], ACT.Exp).then_inc(w_raw.sem, 1)
                    if n:
                        transposed_high(n - 1)
                z_used.due(me)

            def softmax_attention(jobs):
                def exponentials(n):
                    act.wait_ge(*max_ready.due(me))
                    s0, m0 = (n % 2) * 1536, (n % 2) * 8
                    if jobs[n][1] == "cmp":
                        nc.scalar.activation(at(s0, 256), at(s0, 256), ACT.Exp).then_inc(p_done.sem, 1)
                        return
                    for s in range(HG):
                        for qt in range(TT):
                            e = at(s0 + s * 256, 256) if qt else at(s0 + 1024 + s * P, P)
                            c, to = m0 + qt * HG + s, m0 + qt * HG + SLOT_HEAD[s]
                            ins = nc.scalar.activation(e, e, ACT.Exp, bias=nmax[:, c:c + 1], accum_out=rsum[:, to:to + 1])
                    ins.then_inc(p_done.sem, 1)

                exponentials(0)
                for n in range(len(jobs) + 1):
                    if n + 1 < len(jobs):
                        exponentials(n + 1)
                    if n < len(jobs):
                        act.wait_ge(*t_full.due(me))
                        w = 256 if jobs[n][1] == "cmp" else 1024
                        nc.scalar.activation(at(3072, w), ps[:, 3 * 512:3 * 512 + w], ACT.Copy).then_inc(tA_done.sem, 1)
                    if n == len(jobs) or n and jobs[n][0] != jobs[n - 1][0]:
                        transposed_high(jobs[n - 1][0])

            def fox(u0):
                nc.scalar.preload_act_table_set("natural_log_exp_and_others")
                evacuate(fl[:, 0:HEADS], HEADS)
                split_to(u0 + 6)
                act.wait_ge(*fl_soft.due(me))
                tmp = at(ACT_AT, 2 * HEADS)
                step(nc.scalar.activation(tmp, fl, ACT.Abs))
                step(nc.scalar.activation(tmp, tmp, ACT.Exp, scale=-1.0))
                nc.scalar.activation(tmp, tmp, ACT.Ln, bias=1.0).then_inc(l_ready.sem, 1)
                with act.Fori(0, 2) as i:
                    t = Turn(i, {proj_full: 3}, 6)
                    for b, off in enumerate((QT, KT)):
                        evacuate(arena[:, bass.ds(i * DM + off, 512)], t=t, scale=QSCALE if b == 0 else 1.0)
                        split_to(u0 + 6 + 2 * (b + 1), t)
                    evacuate(arena[:, bass.ds(i * 512 + (QKV + 4096), 512)], t=t)
                    split_to(u0 + 6 + 6, t)
                split[me] += 6
                proj_full.due(me, 3)
                split_to(u0 + 17)
                softmax_attention(FOX_JOBS)

            def nsa(u0):
                for b in range(5):
                    if b < 2:
                        dst = at(b * 512, 512)
                    else:
                        off, stride = [(2048, 512), (3072, 1024), (3584, 1024)][b - 2]
                        dst = at(off, 2 * stride).rearrange("p (s d) -> p s d", s=2)[:, :, 0:256]
                    evacuate(dst, parts=1 if b < 2 else 2)
                    split_to(u0 + 5 + 2 * (b + 1))
                evacuate(at(5120, 48), 48)
                split_to(u0 + 17)
                act.wait_ge(*proj_free[0].due(me, 6))
                act.wait_ge(*proj_free[1].due(me, 6))
                nc.scalar.activation(at(5120, 96), at(5120, 96), ACT.Sigmoid).then_inc(gates_ready.sem, 1)
                for b in range(2):
                    act.wait_ge(*qk_full.due(me))
                    nc.scalar.activation(at(QT + b * 512, 512), bank(b), ACT.Copy, scale=QSCALE).then_inc(tr_act.sem, 1)
                qk_full.due(me, 2)
                for b in range(2):
                    act.wait_ge(*qk_full.due(me))
                    nc.scalar.activation(at(KT + b * 512, 512), bank(4 + b), ACT.Copy).then_inc(tr_act.sem, 1)
                qk_full.due(me, 2)
                for b in range(2):
                    act.wait_ge(*qk_full.due(me))
                    src, dst = bank(b).rearrange("p (g t) -> p g t", g=2), at(b * 512, 512).rearrange("p (g t) -> p g t", g=2)
                    nc.scalar.activation(dst[0:DH], src[0:DH], ACT.Copy)
                    nc.scalar.activation(dst[DH:P, :, 0:TOKENS - 1], src[DH:P, :, 1:TOKENS], ACT.Copy).then_inc(tr_act.sem, 1)
                qk_full.due(me, 2)
                act.wait_ge(*win_tmp.due(me))
                nc.scalar.activation(hT_hi[:, 0:1920], at(2048, 1920), ACT.Copy).then_inc(win_hi.sem, 1)
                nc.scalar.preload_act_table(ACT.Silu)
                act.wait_ge(*zeros_ready.due(me))
                for kv in range(2):
                    act.wait_ge(unit_used.sem, u0 + 13 + 2 * kv)
                    for fc in range(2):
                        dst = at(5216 + (kv * 2 + fc) * 128, 128).rearrange("p (g c) -> p g c", g=GROUPS)[:, :, 0:NCMP]
                        src = bank(4 + 2 * kv + fc, 0, 60).rearrange("p (g c) -> p g c", g=GROUPS)
                        ins = nc.scalar.activation(dst, src, ACT.Silu)
                    ins.then_inc(hidc_ready.sem, 1)
                split_to(u0 + 19)
                nc.scalar.preload_act_table(ACT.Exp)
                softmax_attention(NSA_JOBS)

            def pool(u0):
                for b in range(2):
                    evacuate(at(b * 512, 512))
                    split_to(u0 + 5 + 2 * (b + 1))
                act.wait_ge(*proj_free[0].due(me, 2))
                act.wait_ge(unit_used.sem, u0 + 4)
                nc.scalar.activation(hT_hi[:, 0:DM], at(0, DM), ACT.Copy).then_inc(u_hi_done.sem, 1)
                act.wait_ge(*proj_free[1].due(me, 2))
                nc.scalar.activation(hT_hi[:, DM:2 * DM], at(DM, DM), ACT.Copy).then_inc(u_hi_done.sem, 1)
                act.wait_ge(unit_used.sem, u0 + 5)
                for b in range(4):
                    act.wait_ge(*pooled.due(me))
                    nc.scalar.activation(chunk(hT_hi, 2 * b, 2), at(2048 + b * 512, 512), ACT.Copy).then_inc(hT_hi_done.sem, 1)

            def ple(u0):
                nc.scalar.preload_act_table(ACT.Sigmoid)
                for q in range(4):
                    if q % 2 == 0:
                        act.wait_ge(*gu_full.due(me))
                    else:
                        act.wait_ge(unit_used.sem, u0 + 2 + q)
                    nc.scalar.activation(at(q * 512, 512), bank(q), ACT.Sigmoid).then_inc(sg_ready.sem, 1)

            act.wait_ge(const_in.sem, 32)
            act.wait_ge(x_in_done.sem, 16)
            nc.scalar.activation(q_gain8, C("q_gain"), ACT.Copy, scale=QSCALE).then_inc(proj_free[0].sem, 3)
            for s, ((kind, n), u0) in enumerate(zip(stages, starts)):
                if kind == "ple":
                    act.wait_ge(*row_in.due(me, 16))
                    act.wait_ge(unit_used.sem, u0 - 1)
                    nc.scalar.activation(chunk(hid_hi, 0, 2), at(9216, 512), ACT.Copy).then_inc(p_hi_done.sem, 1)
                square_x(s)
                h_high()
                if kind == "ffn":
                    nc.scalar.preload_act_table(ACT.Silu)
                split_to(u0 + 5)
                if kind == "ffn":
                    mlp(u0, FFN_BLOCKS, 2, 2, 4, 2)
                elif kind == "mlp":
                    mlp(u0, MLP_BLOCKS, 1, 3, 4, 3)
                else:
                    {"stick": stick, "ple": ple, "pool": pool, "nsa": nsa, "fox": fox}[kind](u0)
                if kind in ("nsa", "fox", "mlp"):
                    square_acc(u0 + n)
                elif kind != "ple":
                    acc_full.due(me, 3)
                if kind == "pool":
                    row_in.due(me, 16)

        @block.vector
        def _(dve):
            me = "dve"

            def split_to(n, t=None):
                n = min(n, units_total)
                while split[me] < n:
                    u = split[me]
                    split[me] += 1
                    dve.wait_ge(hi_done.sem, u + 1 + (t.i * t.units if t else 0))
                    r = u % RAW
                    nc.vector.tensor_tensor(unit_cols(w_lo, u, 0, UNIT), raw[:, r * UNIT:(r + 1) * UNIT], f(unit_cols(w_hi, u, 0, UNIT)),
                                            ALU.subtract).then_inc(lo_done.sem, 1)

            def step(ins):
                ins.then_inc(dve_step.sem, 1)
                dve.wait_ge(*dve_step.due(me))

            def normalise(gain):
                inverse_rms()
                for c in range(KC + 1):
                    if c < KC:
                        nc.vector.scalar_tensor_tensor(at(c * TOKENS, TOKENS), xs(c), C("gains", gain * KC + c, 1), bank(3, 0, TOKENS),
                                                       ALU.mult, ALU.mult).then_inc(h_ready.sem, 1)
                    if c:
                        dve.wait_ge(*hT_hi_done.due(me))
                        nc.vector.tensor_tensor(chunk(hT_lo, c - 1), at((c - 1) * TOKENS, TOKENS), f(chunk(hT_hi, c - 1)), ALU.subtract).then_inc(hT_ready.sem, 1)

            def inverse_rms():
                dve.wait_ge(*sums_full.due(me))
                mean = ps[:, 2 * 512:2 * 512 + TT * P:P]
                nc.vector.tensor_scalar(var, mean, 1.0 / DM, EPS, ALU.mult, ALU.add).then_inc(var_ready.sem, 1)
                dve.wait_ge(*rstd_full.due(me))

            def mlp(u0, blocks, ups, banks, turns, per_turn):
                step_u = ups + 1

                def one(j, u, t=None):
                    dve.wait_ge(*silu_done.due(me, turn=t))
                    if ups == 2:
                        dve.wait_ge(unit_used.sem, u + 2 + (t.i * t.units if t else 0))
                        other = bank(ups * (j % banks) + 1)
                    else:
                        other = sil[:, 0:512]
                    if j:
                        dve.wait_ge(*hid_split.due(me, turn=t))
                    nc.vector.tensor_tensor(at(ACT_AT, 512), sil[:, 0:512], other, ALU.mult).then_inc(hid_ready.sem, 1)
                    last = j == blocks - 1
                    ahead = u + ups + RING
                    if not last:
                        split_to(ahead - 1, t)
                    dve.wait_ge(*hid_hi_done.due(me, turn=t))
                    h = HC if last else 0
                    nc.vector.tensor_tensor(chunk(hid_lo, h, HC), at(ACT_AT, 512), f(chunk(hid_hi, h, HC)), ALU.subtract).then_inc(hid_split.sem, 1)
                    split_to(ahead - 1 if last else ahead, t)

                one(0, u0)
                one(1, u0 + ups)
                u = u0 + ups + step_u
                each = {silu_done: per_turn, hid_hi_done: per_turn, hid_split: per_turn}
                with dve.Fori(0, turns) as i:
                    t = Turn(i, each, per_turn * step_u)
                    for b in range(per_turn):
                        one(2 + b, u + b * step_u, t)
                for s, n in each.items():
                    s.due(me, n * (turns - 1))
                split[me] += (turns - 1) * per_turn * step_u
                u += turns * per_turn * step_u
                for j in range(2 + turns * per_turn, blocks):
                    one(j, u)
                    u += step_u
                hid_split.due(me)

            def add_to_x(kind, end, post):
                if kind in ("nsa", "fox", "mlp"):
                    inverse_rms()
                    acc_full.due(me, 3)
                    r = at(6144, TOKENS)
                    step(nc.vector.tensor_copy(r, bank(3, 0, TOKENS)))
                for b in range(4):
                    acc, xb = bank(4 + b), xs(2 * b, 2)
                    if kind in ("nsa", "fox", "mlp"):
                        for c in (2 * b, 2 * b + 1):
                            ins = nc.vector.scalar_tensor_tensor(at(c * TOKENS, TOKENS), bank(4 + b, (c % 2) * TOKENS, TOKENS), C("post_gains", post * KC + c, 1), r,
                                                                 ALU.mult, ALU.mult)
                        step(ins)
                        ins = nc.vector.tensor_tensor(xb, xb, at(b * 512, 512), ALU.add)
                    elif kind == "ple":
                        dve.wait_ge(*sg_ready.due(me))
                        step(nc.vector.tensor_tensor(at(b * 512, 512), at(b * 512, 512), acc, ALU.mult))
                        ins = nc.vector.tensor_tensor(xb, xb, at(b * 512, 512), ALU.add)
                    else:
                        if b < 3:
                            dve.wait_ge(*acc_full.due(me))
                        else:
                            dve.wait_ge(unit_used.sem, end)
                        if kind == "ffn":
                            ins = nc.vector.scalar_tensor_tensor(xb, acc, 0.5, xb, ALU.mult, ALU.add)
                        elif kind == "stick":
                            ins = nc.vector.tensor_tensor(xb, acc, xb, ALU.add)
                        else:
                            for c in (2 * b, 2 * b + 1):
                                ins = nc.vector.scalar_tensor_tensor(xs(c), bank(4 + b, (c % 2) * TOKENS, TOKENS), C("pool_scale", c, 1), xs(c), ALU.mult, ALU.add)
                    ins.then_inc(x_ready.sem, 1)

            def evacuate(dst, done, width=512, parts=1, t=None, scale=None):
                dve.wait_ge(unit_used.sem, done + (t.i * t.units if t else 0))
                src = bank(2 * (blocks_done[me] % 3) + 1, 0, width)
                blocks_done[me] += 1
                if parts > 1:
                    src = src.rearrange("p (s d) -> p s d", s=parts)
                if scale is None:
                    ins = nc.vector.tensor_copy(dst, src)
                else:
                    ins = nc.vector.tensor_scalar(dst, src, scale, None, ALU.mult)
                ins.then_inc(proj_free[1].sem, 1)

            def transposed_low(g):
                dve.wait_ge(*hT_hi_done.due(me))
                nc.vector.tensor_tensor(chunk(hT_lo, 2 * g, 2), bank(6 + g % 2), f(chunk(hT_hi, 2 * g, 2)), ALU.subtract).then_inc(hT_ready.sem, 1)

            def stick(u0):
                each = {sq_ready: 2, rstdq_ready: 2, qk_full: 4}
                with dve.Fori(0, 2) as i:
                    t = Turn(i, each, 6)
                    for b, off in enumerate((0, DM)):
                        evacuate(at(off + 512, 512), u0 + 2 * b + 2, t=t)
                        rows = at(off, DM).rearrange("p (a d) -> p a d", d=DH)
                        dve.wait_ge(*sq_ready.due(me, turn=t))
                        nc.vector.tensor_reduce(ssq, at(ACT_AT, DM).rearrange("p (a d) -> p a d", d=DH), AX.X, ALU.add).then_inc(ssq_ready.sem, 1)
                        split_to(u0 + 4 + 2 * (b + 1), t)
                        dve.wait_ge(*rstdq_ready.due(me, turn=t))
                        nc.vector.tensor_tensor(rows, rows, rstdq.unsqueeze(2).broadcast_to((P, HEADS, DH)), ALU.mult).then_inc(qn_ready.sem, 1)
                        split_to(u0 + 5 + 2 * (b + 1), t)
                    evacuate(arena[:, bass.ds(i * 512 + (QKV + 4096 + DM), 512)], u0 + 6, t=t)
                    split_to(u0 + 5 + 6, t)
                    qk_full.due(me, 2)
                    for half in range(2):
                        dve.wait_ge(*qk_full.due(me, turn=t))
                        nc.vector.tensor_scalar(arena[:, bass.ds(i * DM + (KT + half * 512), 512)], bank(6 + half), C("k_gain"), None, ALU.mult).then_inc(tr_dve.sem, 1)
                split[me] += 6
                for sig, n in each.items():
                    sig.due(me, n)

                def keep(n):
                    dve.wait_ge(*l_ready.due(me))
                    nc.vector.scalar_tensor_tensor(NST[0], ps[:, 0:1024], 0.0, at(0, 1024), ALU.max, ALU.add)
                    nc.vector.scalar_tensor_tensor(NST[1], ps[:, 1024:1536], 0.0, at(1024, 512), ALU.max, ALU.add).then_inc(nst_raw.sem, 1)
                    if n >= 2:
                        dve.wait_ge(*hT_full.due(me))
                    nc.vector.scalar_tensor_tensor(LOGW[n % 2][0], ps[:, 0:1024], 0.0, at(0, 1024), ALU.min, ALU.subtract)
                    nc.vector.scalar_tensor_tensor(LOGW[n % 2][1], ps[:, 1024:1536], 0.0, at(1024, 512), ALU.min, ALU.subtract).then_inc(z_used.sem, 1)

                split_to(u0 + 16)
                keep(0)
                for n in range(GROUPS + 1):
                    if n < GROUPS:
                        dve.wait_ge(*after_full.due(me))
                        dve.wait_ge(*z_used.due(me))
                        a, b = LOGW[n % 2]
                        nc.vector.tensor_tensor(a, a, ps[:, 3 * 512:5 * 512], ALU.add)
                        nc.vector.tensor_tensor(b, b, bank(5), ALU.add).then_inc(warg_ready.sem, 1)
                    if n + 1 < GROUPS:
                        keep(n + 1)
                    if n:
                        transposed_low(n - 1)

            def slots(ap):
                return ap.rearrange("p (pair odd) -> p odd pair", odd=2).unsqueeze(3)

            def softmax_attention(jobs, gates=None):
                rows = TT * HG

                def by_row(ap):
                    return ap.rearrange("p (a d) -> p a d", a=rows)

                def masked_scores(n):
                    g, br = jobs[n]
                    dve.wait_ge(*s_full.due(me))
                    s0, m0 = (n % 2) * 1536, (n % 2) * 8
                    if br == "cmp":
                        S = at(s0, 256)
                        s4 = S.rearrange("p (t h c) -> p t h c", t=TT, h=HG)
                        c4 = bank(0, 0, 256).rearrange("p (t h c) -> p t h c", t=TT, h=HG)
                        m3 = K("cmp_mask").rearrange("p (t c) -> p t c", t=TT)
                        for t in range(TT):
                            ins = nc.vector.tensor_tensor(s4[:, t], c4[:, t], m3[:, t].unsqueeze(1).broadcast_to((P, HG, CPAD)), ALU.add)
                        ins.then_inc(s_used.sem, 1)
                        dve.wait_ge(*s_used.due(me))
                        m = nmax[:, m0:m0 + rows]
                        step(nc.vector.tensor_reduce(m, by_row(S), AX.X, ALU.max, negate=True))
                        nc.vector.tensor_tensor(by_row(S), by_row(S), m.unsqueeze(2).broadcast_to((P, rows, CPAD)), ALU.add).then_inc(max_ready.sem, 1)
                        return
                    sA, sB = at(s0, 1024).rearrange("p (h k) -> p h k", h=HG), at(s0 + 1024, 512).rearrange("p (h k) -> p h k", h=HG)
                    if br != "fox":
                        nc.vector.tensor_tensor(sA, ps[:, 0:1024].rearrange("p (h k) -> p h k", h=HG),
                                                K("mask").unsqueeze(1).broadcast_to((P, HG, 2 * P)), ALU.add)
                        ins = nc.vector.tensor_tensor(sB, bank(2).rearrange("p (h k) -> p h k", h=HG),
                                                      K("mask", P, P).unsqueeze(1).broadcast_to((P, HG, P)), ALU.add)
                    else:
                        for s in range(HG):
                            h = HG * g + SLOT_HEAD[s]
                            nc.vector.scalar_tensor_tensor(sA[:, s], ps[:, s * 256:(s + 1) * 256], cq[:, HEADS + h:HEADS + h + 1], K("mask"), ALU.add, ALU.add)
                            ins = nc.vector.scalar_tensor_tensor(sB[:, s], bank(2, s * P, P), cq[:, h:h + 1], K("mask", P, P), ALU.add, ALU.add)
                    ins.then_inc(s_used.sem, 1)
                    dve.wait_ge(*s_used.due(me))
                    nc.vector.tensor_reduce(nmax[:, m0:m0 + HG], sB, AX.X, ALU.max, negate=True)
                    nc.vector.tensor_reduce(nmax[:, m0 + HG:m0 + 2 * HG], sA, AX.X, ALU.max, negate=True).then_inc(max_ready.sem, 1)

                def weights(n):
                    g, br = jobs[n]
                    dve.wait_ge(*p_done.due(me))
                    s0, m0 = (n % 2) * 1536, (n % 2) * 8
                    coef, total = coefs[:, m0:m0 + rows], rsum[:, m0:m0 + rows]
                    c3 = coef.rearrange("p (t h) -> p t h", t=TT)
                    if br == "cmp":
                        step(nc.vector.tensor_reduce(total, by_row(at(s0, 256)), AX.X, ALU.add))
                    ins = nc.vector.reciprocal(coef, total)
                    if br != "fox":
                        step(ins)
                        ins = nc.vector.tensor_tensor(c3, c3, gates[:, :, HG * g:HG * (g + 1), ("cmp", "slc", "win").index(br)], ALU.mult)
                    if br == "cmp":
                        step(ins)
                        step(nc.vector.tensor_tensor(c3, c3, K("cmp_valid").unsqueeze(2).broadcast_to((P, TT, HG)), ALU.mult))
                        nc.vector.tensor_tensor(by_row(at(s0, 256)), by_row(at(s0, 256)), coef.unsqueeze(2).broadcast_to((P, rows, CPAD)), ALU.mult).then_inc(pB_ready.sem, 1)
                    else:
                        ins.then_inc(coef_ready.sem, 1)
                        dve.wait_ge(*coef_ready.due(me))
                        B = at(s0 + 1024, 512).rearrange("p (o a k) -> p o a k", o=2, a=2)
                        nc.vector.tensor_tensor(B, B, slots(coef[:, 0:HG]).broadcast_to((P, 2, 2, P)), ALU.mult).then_inc(pB_ready.sem, 1)

                masked_scores(0)
                masked_scores(1)
                weights(0)
                for n in range(len(jobs) + 1):
                    if n < len(jobs):
                        dve.wait_ge(*t_full.due(me))
                        if jobs[n][1] != "cmp":
                            nc.vector.tensor_copy(at(ACT_AT, 512), bank(5)).then_inc(tB_done.sem, 1)
                    if n + 1 < len(jobs):
                        weights(n + 1)
                    if n == len(jobs) or n and jobs[n][0] != jobs[n - 1][0]:
                        transposed_low(jobs[n - 1][0])
                    if n + 2 < len(jobs):
                        masked_scores(n + 2)

            def fox(u0):
                evacuate(fl[:, HEADS:2 * HEADS], u0 + 1, HEADS)
                dve.wait_ge(*proj_free[0].due(me))
                dve.wait_ge(*proj_free[1].due(me))
                fl3 = fl.rearrange("p (t h) -> p t h", t=TT)
                nc.vector.tensor_tensor(fl3, fl3, C("b_f").unsqueeze(1).broadcast_to((P, TT, HEADS)), ALU.add).then_inc(fl_soft.sem, 1)
                split_to(u0 + 6)
                dve.wait_ge(*l_ready.due(me))
                nc.vector.scalar_tensor_tensor(fl, fl, 0.0, at(ACT_AT, 2 * HEADS), ALU.min, ALU.subtract).then_inc(logf_ready.sem, 1)
                with dve.Fori(0, 2) as i:
                    t = Turn(i, {}, 6)
                    for b, off in enumerate((QT, KT)):
                        evacuate(arena[:, bass.ds(i * DM + (off + 512), 512)], u0 + 3 + 2 * b, t=t, scale=QSCALE if b == 0 else None)
                        split_to(u0 + 6 + 2 * (b + 1), t)
                    evacuate(arena[:, bass.ds(i * 512 + (QKV + 4096 + DM), 512)], u0 + 7, t=t)
                    split_to(u0 + 6 + 6, t)
                split[me] += 6
                split_to(u0 + 17)
                dve.wait_ge(*c_full.due(me))
                nc.vector.tensor_copy(cq, bank(6, 0, 2 * HEADS))
                nc.vector.tensor_scalar(sil[0:HEADS, 0:TOKENS], ps[0:HEADS, 7 * 512:7 * 512 + TOKENS], -1.0, None, ALU.mult).then_inc(c_ready.sem, 1)
                softmax_attention(FOX_JOBS)

            def rotate(x, tok, heads, turn, last):
                x1, x2 = x[:, :, 0:32], x[:, :, 32:64]
                c = K("cos", tok * 32, 32).unsqueeze(1).broadcast_to((P, heads, 32))
                s = K("sin", tok * 32, 32).unsqueeze(1).broadcast_to((P, heads, 32))
                t = [at(KT + turn % 2 * 1536 + i * 512, heads * 32).rearrange("p (h d) -> p h d", h=heads) for i in range(3)]
                nc.vector.tensor_tensor(t[0], x1, c, ALU.mult)
                nc.vector.tensor_tensor(t[1], x2, s, ALU.mult)
                nc.vector.tensor_tensor(t[2], x1, s, ALU.mult)
                step(nc.vector.tensor_tensor(x2, x2, c, ALU.mult))
                nc.vector.tensor_tensor(x1, t[0], t[1], ALU.subtract)
                ins = nc.vector.tensor_tensor(x2, x2, t[2], ALU.add)
                if last:
                    ins.then_inc(qn_ready.sem, 1)

            def nsa(u0):
                for b in range(5):
                    if b < 2:
                        dst = at(DM + b * 512, 512)
                    else:
                        off, stride = [(2048, 512), (3072, 1024), (3584, 1024)][b - 2]
                        dst = at(off, 2 * stride).rearrange("p (s d) -> p s d", s=2)[:, :, 256:512]
                    evacuate(dst, u0 + 2 * b + 2, parts=1 if b < 2 else 2)
                    split_to(u0 + 5 + 2 * (b + 1))
                evacuate(at(5168, 48), u0 + 11, 48)
                split_to(u0 + 17)
                for tok in range(TT):
                    dve.wait_ge(*proj_free[tok].due(me, 14))
                for tok in range(TT):
                    rotate(at(tok * DM, DM).rearrange("p (h d) -> p h d", d=DH), tok, HEADS, tok, True)
                for tok in range(TT):
                    for i, sec in enumerate((2048, 3072, 3584)):
                        rotate(at(sec + tok * 256, 256).rearrange("p (h d) -> p h d", d=DH), tok, GROUPS, TT + 3 * tok + i, sec == 3584)
                qk_full.due(me, 2)
                for b in (2, 3):
                    dve.wait_ge(*qk_full.due(me))
                    nc.vector.tensor_scalar(at(QT + b * 512, 512), bank(b), QSCALE, None, ALU.mult).then_inc(tr_dve.sem, 1)
                qk_full.due(me, 2)
                for b in range(2):
                    dve.wait_ge(*qk_full.due(me))
                    nc.vector.tensor_copy(at(KT + 1024 + b * 512, 512), bank(6 + b)).then_inc(tr_dve.sem, 1)
                qk_full.due(me, 2)
                for b in range(2):
                    dve.wait_ge(*qk_full.due(me))
                    src = bank(2 + b).rearrange("p (g t) -> p g t", g=2)
                    dst = at(1024 + b * 512, 512).rearrange("p (g t) -> p g t", g=2)
                    nc.vector.tensor_copy(dst[0:DH], src[0:DH])
                    nc.vector.tensor_copy(dst[DH:P, :, 0:TOKENS - 1], src[DH:P, :, 1:TOKENS]).then_inc(tr_dve.sem, 1)
                dve.wait_ge(*tr_act.due(me, 10))
                dve.wait_ge(*tr_dve.due(me, 10))
                half = CMP_LEN // 2
                for kv in range(2):
                    pos = C("cmp_pos", kv * half, half).unsqueeze(2).broadcast_to((P, half, NCMP))
                    for g in range(GROUPS):
                        tokens = at(kv * 1024 + g * TOKENS, TOKENS)
                        src = tokens.rearrange("p (b j) -> p j b", j=CMP_STRIDE)
                        dst = at(2048 + kv * 960, 960).rearrange("p (j g b) -> p j g b", j=half, g=GROUPS)[:, :, g, :]
                        q = half // 2
                        nc.vector.tensor_tensor(dst[:, 0:q], src[:, 0:CMP_STRIDE:2, 0:NCMP], pos[:, 0:q], ALU.add)
                        ins = nc.vector.tensor_tensor(dst[:, q:half], src[:, 0:CMP_STRIDE:2, 1:NCMP + 1], pos[:, q:half], ALU.add)
                ins.then_inc(win_tmp.sem, 1)
                dve.wait_ge(*win_hi.due(me))
                nc.vector.tensor_tensor(hT_lo[:, 0:1920], at(2048, 1920), f(hT_hi[:, 0:1920]), ALU.subtract).then_inc(win_ready.sem, 1)
                split_to(u0 + 19)
                dve.wait_ge(*cmp_full.due(me))
                by_parity = bank(0, 0, 128).rearrange("p (g c) -> p g c", g=GROUPS).unsqueeze(2).broadcast_to((P, GROUPS, 2, CPAD))
                nc.vector.tensor_tensor(at(CMP_K, 256).rearrange("p (g o c) -> p g o c", g=GROUPS, o=2), by_parity,
                                        K("parity").unsqueeze(1).unsqueeze(3).broadcast_to((P, GROUPS, 2, CPAD)), ALU.mult)
                by_head = bank(1, 0, 256).rearrange("p (g d) -> p g d", g=GROUPS).unsqueeze(2).broadcast_to((P, GROUPS, HG, DH))
                nc.vector.tensor_tensor(sil[:].rearrange("p (g h d) -> p g h d", g=GROUPS, h=HG), by_head,
                                        K("head_block").unsqueeze(1).unsqueeze(3).broadcast_to((P, GROUPS, HG, DH)), ALU.mult).then_inc(cmp_kv.sem, 1)
                dve.wait_ge(*gates_ready.due(me))
                softmax_attention(NSA_JOBS, at(5120, 96).rearrange("p (t h x) -> p t h x", t=TT, x=3))

            def pool(u0):
                for b in range(2):
                    evacuate(at(DM + b * 512, 512), u0 + 2 * b + 2)
                    split_to(u0 + 5 + 2 * (b + 1))
                for tok in range(TT):
                    dve.wait_ge(*u_hi_done.due(me))
                    nc.vector.tensor_tensor(hT_lo[:, tok * DM:(tok + 1) * DM], at(tok * DM, DM), f(hT_hi[:, tok * DM:(tok + 1) * DM]),
                                            ALU.subtract).then_inc(u_ready.sem, 1)
                dve.wait_ge(*row_in.due(me, 16))
                for b in range(4):
                    if b < 3:
                        dve.wait_ge(*pool_full.due(me))
                    else:
                        dve.wait_ge(unit_used.sem, u0 + 5)
                    inv = at(7168 + b * TOKENS, TOKENS).unsqueeze(1).broadcast_to((P, 2, TOKENS))
                    nc.vector.tensor_tensor(at(2048 + b * 512, 512).rearrange("p (c t) -> p c t", c=2),
                                            bank(b).rearrange("p (c t) -> p c t", c=2), inv, ALU.mult).then_inc(pooled.sem, 1)
                for b in range(4):
                    dve.wait_ge(*hT_hi_done.due(me))
                    nc.vector.tensor_tensor(chunk(hT_lo, 2 * b, 2), at(2048 + b * 512, 512), f(chunk(hT_hi, 2 * b, 2)), ALU.subtract).then_inc(hT_ready.sem, 1)

            nc.vector.memset(nhalf, -0.5).then_inc(proj_free[1].sem, 3)
            dve.wait_ge(const_in.sem, 32)
            dve.wait_ge(x_in_done.sem, 16)
            norms, posts = 0, 0
            for (kind, n), u0, nxt in zip(stages, starts, stages[1:] + [("", 0)]):
                normalise(norms)
                norms += 1
                split_to(u0 + 5)
                if kind == "ffn":
                    mlp(u0, FFN_BLOCKS, 2, 2, 4, 2)
                elif kind == "mlp":
                    mlp(u0, MLP_BLOCKS, 1, 3, 4, 3)
                elif kind != "ple":
                    {"stick": stick, "pool": pool, "nsa": nsa, "fox": fox}[kind](u0)
                if nxt[0] == "ple":
                    dve.wait_ge(*p_hi_done.due(me))
                    row_in.due(me, 16)
                    nc.vector.tensor_tensor(chunk(hid_lo, 0, 2), at(9216, 512), f(chunk(hid_hi, 0, 2)), ALU.subtract).then_inc(p_ready.sem, 1)
                add_to_x(kind, u0 + n, posts)
                posts += kind in ("nsa", "fox", "mlp")

        @block.gpsimd
        def _(pool):
            me = "pool"

            def step(ins):
                ins.then_inc(pool_step.sem, 1)
                pool.wait_ge(*pool_step.due(me))

            def inverse_rms(sums, tmp, dst, n, width):
                step(nc.gpsimd.tensor_scalar(tmp, sums, 1.0 / width, EPS, ALU.mult, ALU.add))
                return nc.gpsimd.tensor_tensor(dst, tmp, nhalf[:, 0:n], ALU.pow)

            def inverse_rms_of_tokens():
                pool.wait_ge(*var_ready.due(me))
                nc.gpsimd.tensor_tensor(rstd, var, nhalf[:, 0:TT], ALU.pow).then_inc(rstd_ready.sem, 1)

            def causal_zero(z, heads):
                return nc.gpsimd.affine_select(out=z, in_=z, compare_op=ALU.is_gt, fill=0.0, base=0,
                                               pattern=[[0, heads], [1, P]], channel_multiplier=-1)

            def diagonal_zero(a, b):
                causal_zero(a.rearrange("p (h q) -> p h q", h=HG)[:, :, 0:P], HG)
                return causal_zero(b.rearrange("p (h q) -> p h q", h=HG), HG)

            def second_tile_weights(jobs):
                for n, (_, br) in enumerate(jobs):
                    if br == "cmp":
                        continue
                    pool.wait_ge(*coef_ready.due(me))
                    A = at((n % 2) * 1536, 1024).rearrange("p (o a k) -> p o a k", o=2, a=2)
                    c = coefs[:, (n % 2) * 8 + HG:(n % 2) * 8 + 2 * HG].rearrange("p (pair odd) -> p odd pair", odd=2)
                    nc.gpsimd.tensor_tensor(A, A, c.unsqueeze(3).broadcast_to((P, 2, 2, 2 * P)), ALU.mult).then_inc(pA_ready.sem, 1)

            pool.wait_ge(proj_free[1].sem, 3)
            layer = 0
            for (kind, _), nxt in zip(stages, stages[1:] + [("", 0)]):
                inverse_rms_of_tokens()
                if kind == "stick":
                    for block in range(4):
                        pool.wait_ge(*ssq_ready.due(me))
                        inverse_rms(ssq, varq, rstdq, HEADS, DH).then_inc(rstdq_ready.sem, 1)
                    for n in range(-1, GROUPS):
                        if n + 1 < GROUPS:
                            pool.wait_ge(*nst_raw.due(me))
                            diagonal_zero(*NST).then_inc(nst_ready.sem, 1)
                        if n >= 0:
                            pool.wait_ge(*w_raw.due(me))
                            diagonal_zero(*LOGW[n % 2]).then_inc(w_ready.sem, 1)
                    hT_ready.due(me, KC + GROUPS)
                elif kind == "pool":
                    pool.wait_ge(*hT_ready.due(me, KC))
                    pool.dma_start(at(7168, 4 * TOKENS), count_in).then_inc(row_in.sem, 16)
                    hT_ready.due(me, 4)
                else:
                    pool.wait_ge(*hT_ready.due(me, KC))
                    if kind == "nsa":
                        nc.gpsimd.memset(at(5216, 512), 0.0).then_inc(zeros_ready.sem, 1)
                    if nxt[0] == "ple":
                        pool.dma_start(at(9216, 2 * TOKENS), p_in[layer]).then_inc(row_in.sem, 16)
                        layer += 1
                    if kind in ("nsa", "fox"):
                        second_tile_weights(NSA_JOBS if kind == "nsa" else FOX_JOBS)
                        hT_ready.due(me, GROUPS)
                    if kind in ("nsa", "fox", "mlp"):
                        inverse_rms_of_tokens()



def chunks(w):
    k, n = w.shape[0] // P, w.shape[1]
    return w.reshape(k, P, n).transpose(1, 0, 2).reshape(P, k * n)


def as_units(a):
    n = -(-a.shape[1] // UNIT)
    if a.shape[1] != n * UNIT:
        a = np.concatenate([a, np.zeros((P, n * UNIT - a.shape[1]), a.dtype)], axis=1)
    return [a[:, i * UNIT:(i + 1) * UNIT] for i in range(n)]


def interleave(up, down):
    out = list(up[0])
    for j in range(1, len(up)):
        out += up[j] + down[j - 1]
    return out + down[-1]


def ffn_units(gu, down):
    up = [as_units(chunks(np.concatenate([gu[:, 256 * j:256 * (j + 1)], gu[:, D_FF + 256 * j:D_FF + 256 * (j + 1)]], axis=1)))
          for j in range(FFN_BLOCKS)]
    return interleave(up, [as_units(chunks(down[256 * j:256 * (j + 1)])) for j in range(FFN_BLOCKS)])


def mlp_units(w_up, w_down):
    return interleave([as_units(chunks(w_up[:, 256 * j:256 * (j + 1)])) for j in range(MLP_BLOCKS)],
                      [as_units(chunks(w_down[256 * j:256 * (j + 1)])) for j in range(MLP_BLOCKS)])


def block_units(w, order):
    return [u for b in order for u in as_units(chunks(w[:, 512 * b:512 * (b + 1)]))]


QKV_ORDER = [0, 2, 4, 1, 3, 5]


def band():
    out = np.zeros((TT, P, len(WINDOWS), TOKENS), np.float32)
    t = np.arange(TOKENS)
    for i, w in enumerate(WINDOWS):
        full = ((t[:, None] <= t[None, :]) & (t[:, None] > t[None, :] - w)).astype(np.float32)
        full[t, t] -= np.minimum(t + 1, w)
        out[:, :, i, :] = full.reshape(TT, P, TOKENS)
    return out.transpose(1, 0, 2, 3).reshape(P, -1)


def constants():
    out = np.zeros((P, NCONST), np.float32)

    def put(name, a):
        o, n = CONST[name]
        out[:, o:o + n] = np.asarray(a, np.float32).reshape(P, n)

    i = np.arange(P)
    put("ident", np.eye(P))
    put("after_neg", -(i[:, None] > i[None, :]).astype(np.float32))
    put("ones_neg", -np.ones((P, P)))
    put("upto", i[:, None] <= i[None, :])
    put("ones", np.ones((P, P)))
    put("mask", np.concatenate([np.zeros((P, P)), np.where(i[None, :] <= i[:, None], 0.0, NEG)], axis=1))
    inv = np.float32(10000.0) ** (-np.arange(0, DH, 2, dtype=np.float32) / np.float32(DH))
    angle = (np.arange(TOKENS, dtype=np.float32)[:, None] * inv[None, :]).astype(np.float32)
    put("cos", np.cos(angle).reshape(TT, P, 32).transpose(1, 0, 2))
    put("sin", np.sin(angle).reshape(TT, P, 32).transpose(1, 0, 2))
    t, c = np.arange(TOKENS), np.arange(CPAD)
    seen = (c[None, :] < NCMP) & (c[None, :] * CMP_STRIDE + CMP_LEN - 1 <= t[:, None])
    put("cmp_mask", np.where(seen, 0.0, NEG).reshape(TT, P, CPAD).transpose(1, 0, 2))
    put("cmp_valid", (t >= CMP_LEN - 1).astype(np.float32).reshape(TT, P).T)
    put("parity", i[:, None] // DH == np.arange(2)[None, :])
    put("head_block", i[:, None] // CPAD == np.arange(HG)[None, :])
    return out


def small_parameters(v):
    out = np.zeros((P, NCOLS), np.float32)

    def put(name, a):
        o, n = COLS[name]
        out[:, o:o + n] = a.reshape(P, n)

    gains = [g[i] for i in range(2) for g in (v["norm_ffn1"], v["norm_mix"], v["norm_ffn2"], v["norm_ple"])]
    gains += [v["norm_g_2"][i, j] for i in range(2) for j in (0, 2)]
    put("gains", np.stack(gains).reshape(12, KC, P).transpose(2, 0, 1))
    put("post_gains", np.stack([v["norm_g_2"][i, j] for i in range(2) for j in (1, 3)]).reshape(4, KC, P).transpose(2, 0, 1))
    put("pool_scale", v["pool_scale"][0].reshape(KC, P).T)
    put("q_gain", np.concatenate([v["q_norm"][0], v["q_norm"][0]]))
    put("k_gain", np.concatenate([v["k_norm"][0], v["k_norm"][0]]))
    put("cmp_pos", v["nsa_cmp_pos_2"][0].reshape(2, CMP_LEN // 2, 2, DH).transpose(2, 3, 0, 1))
    put("cmp_w2", v["nsa_cmp_w2_2"][0].reshape(2, 2, P, DH).transpose(2, 0, 1, 3))
    put("b_f", np.broadcast_to(v["fox_b_f_2"][0], (P, HEADS)))
    return out


def kernel(**inputs):
    import concourse.bacc as bacc
    from concourse.bass_utils import run_bass_kernel_spmd

    v = {k: np.asarray(a) for k, a in inputs.items()}
    units = []
    for i in range(2):
        units += ffn_units(v["w_ffn1_gu"][i], v["w_ffn1_down"][i])
        if i == 0:
            units += block_units(v["w_qkv"][0], QKV_ORDER) + block_units(v["w_o"][0], range(2))
        else:
            units += block_units(v["w_pool_in"][0], range(2)) + as_units(band())
            units += as_units(v["w_pool_grp"][0].reshape(4, 2, P, 256).transpose(2, 0, 1, 3).reshape(P, -1))
        units += ffn_units(v["w_ffn2_gu"][i], v["w_ffn2_down"][i])
        units += as_units(chunks(v["w_ple_proj"][i])) + block_units(v["w_ple_gate"][i], range(2))
    w = v["nsa_w_in_2"][0]
    units += block_units(w[:, :2560], range(5)) + as_units(chunks(w[:, 2560:]))
    for kv in range(2):
        units += as_units(chunks(v["nsa_cmp_w1_2"][0, kv]))
    units += block_units(v["nsa_w_out_2"][0], range(2)) + mlp_units(v["mlp_w_up_2"][0], v["mlp_w_down_2"][0])
    w = v["fox_w_in_2"][0]
    units += as_units(chunks(w[:, 3072:])) + block_units(w[:, :3072], QKV_ORDER)
    units += block_units(v["fox_w_out_2"][0], range(2)) + mlp_units(v["mlp_w_up_2"][1], v["mlp_w_down_2"][1])

    t = np.arange(TOKENS)
    counts = np.stack([np.float32(1) / np.minimum(t + 1, w).astype(np.float32) for w in WINDOWS])
    arrays = {
        "weights": np.stack(units),
        "x": np.ascontiguousarray(v["x"][0].T.reshape(KC, P, TOKENS).transpose(1, 0, 2).reshape(P, KC * TOKENS)),
        "constants": constants(),
        "parameters": small_parameters(v),
        "p": np.ascontiguousarray(v["p"][:, 0].transpose(0, 2, 1).reshape(2, 2, P, TOKENS).transpose(0, 2, 1, 3).reshape(2, P, 2 * TOKENS)),
        "counts": np.ascontiguousarray(np.broadcast_to(counts.reshape(1, -1), (P, 4 * TOKENS))),
    }
    nc = bacc.Bacc("TRN2", target_bir_lowering=False, num_devices=1)
    args = [nc.dram_tensor(n, a.shape, mybir.dt.float32, kind="ExternalInput").ap() for n, a in arrays.items()]
    out = nc.dram_tensor("out", (4, P, 2 * TOKENS), mybir.dt.float32, kind="ExternalOutput").ap()
    network_kernel(nc, *args, out)
    got = run_bass_kernel_spmd(nc, [arrays], core_ids=[0]).results[0]["out"]
    return np.ascontiguousarray(got.reshape(4, P, 2, TOKENS).transpose(3, 0, 2, 1)).reshape(1, TOKENS, DM)
```

```python
from contextlib import ExitStack

import numpy as np

import concourse.bass as bass
from concourse import mybir

P = 128
TOKENS, DM = 256, 1024
TT = TOKENS // P
KC = DM // P
HEADS, DH = 16, 64
PAIRS = HEADS // 2
SLOT_HEAD = (0, 2, 1, 3)
GROUPS = 4
HG = HEADS // GROUPS
PLE = 256
D_FF, D_MLP = 2816, 4096
FFN_BLOCKS = D_FF // 256
MLP_BLOCKS = D_MLP // 256
HID = 4 * 256 + 8
HC = 2
WINDOWS = (2, 4, 8, 16)
CMP_LEN, CMP_STRIDE = 32, 16
NCMP = (TOKENS - CMP_LEN) // CMP_STRIDE + 1
NWIN = GROUPS * NCMP
CPAD = 32
CMP_HID = 256
EPS = 1e-6
QSCALE = DH ** -0.5
NEG = -1e30

UNIT = 2048
RAW, RING = 3, 6

FFN_U = 3 * FFN_BLOCKS
MLP_U = 2 * MLP_BLOCKS
STAGES = [
    ("ffn", FFN_U), ("stick", 16), ("ffn", FFN_U), ("ple", 5),
    ("ffn", FFN_U), ("pool", 6), ("ffn", FFN_U), ("ple", 5),
    ("nsa", 19), ("mlp", MLP_U), ("fox", 17), ("mlp", MLP_U),
]

CONST = {}
_at = 0
for _name, _n in [("ident", P), ("after_neg", P), ("ones_neg", P), ("ones", P),
                  ("mask", 2 * P), ("cmp_mask", TT * CPAD),
                  ("cmp_valid", TT), ("head_block", HG), ("in_slot", HG), ("in_group", GROUPS)]:
    CONST[_name] = (_at, _n)
    _at += _n
NCONST = _at
COLS = {}
_at = 0
for _name, _n in [("gains", 12 * KC), ("post_gains", 4 * KC), ("pool_scale", KC), ("q_gain", 1), ("k_gain", 1), ("cmp_pos", 2 * CMP_LEN // 2),
                  ("cmp_w2", 2 * 2 * DH), ("b_f", 1)]:
    COLS[_name] = (_at, _n)
    _at += _n
NCOLS = _at

QKV = 0
QT, KT = 6144, 8192
SQUARES = 4096
ACT_AT = 10240
NSA_K, NSA_V = 0, 512
NSA_DUP = 1024
NSA_WIN = 3072
TABLE = 4992
GATES = 5888
CMP_K = 5984
NSA_KV = 9216
NARENA = 11264

NSA_TABLE = {"cos": (0, TOKENS), "sin": (TOKENS, TOKENS), "swap": (2 * TOKENS, P), "dup": (2 * TOKENS + P, 2 * P)}
NTABLE = 2 * TOKENS + 3 * P

FOX_JOBS = [(g, "fox") for g in range(GROUPS)]
NSA_JOBS = [(g, b) for g in range(GROUPS) for b in ("slc", "win", "cmp")]


POST = ("nsa", "fox", "mlp")


class Signal:

    def __init__(self, nc, ctx, name, free=0):
        self.sem = ctx.enter_context(nc.semaphore(name))
        self.free = free
        self.seen = {}

    def due(self, who, step=1, turn=None):
        v = self.seen.get(who, 0 if who == "pe" else self.free) + step
        self.seen[who] = v
        if turn is not None:
            v = v + turn.i * turn.each[self]
        return self.sem, v


class Turn:

    def __init__(self, i, each, units):
        self.i, self.each, self.units = i, each, units


def network_kernel(nc, stream, x_in, consts_in, cols_in, p_in, count_in, table_in, out):
    f32, f32r = mybir.dt.float32, mybir.dt.float32r
    ALU, ACT, AX = mybir.AluOpType, mybir.ActivationFunctionType, mybir.AxisListType
    stages = STAGES
    starts, units_total = [], 0
    norm_of, norms_total = [], 0
    for kind, n in stages:
        starts.append(units_total)
        units_total += n
        norm_of.append(norms_total)
        norms_total += 2 if kind in POST else 1

    ctx = ExitStack()
    with ctx:
        def sb(name, cols, dt=f32):
            return ctx.enter_context(nc.sbuf_tensor(name, [P, cols], dt))

        raw = sb("raw", RAW * UNIT)
        w_hi, w_lo = sb("w_hi", RING * UNIT, f32r), sb("w_lo", RING * UNIT, f32r)
        X = sb("X", KC * TOKENS)
        hT_hi, hT_lo = sb("hT_hi", KC * TOKENS, f32r), sb("hT_lo", KC * TOKENS, f32r)
        hid_hi, hid_lo = sb("hid_hi", HID, f32r), sb("hid_lo", HID, f32r)
        arena = sb("arena", NARENA)
        sil = sb("sil", TT * 512)
        const = sb("const", NCONST)
        cols = sb("cols", NCOLS)
        stat = sb("stat", 192)
        spare = sb("spare", 512)
        R = spare[:, 0:TOKENS]
        ps = ctx.enter_context(nc.psum_tensor("ps", [P, 8 * 512], f32))

        def bank(b, a=0, n=512):
            return ps[:, b * 512 + a:b * 512 + a + n]

        def at(off, n):
            return arena[:, off:off + n]

        def f(ap):
            return ap.bitcast(f32)

        NST = [(sil[:, 0:1024], at(ACT_AT, 512)), (at(QT, 1024), spare[:, 0:512])]
        LOGS = at(0, 1024), at(1024, 512)
        LOGW = [(at(1536, 1024), at(2560, 512)), (at(3072, 1024), at(ACT_AT + 512, 512)),
                (at(KT + 512, 1024), at(QT + 1024, 512)), (at(QT + 1536, 1024), at(KT + 1536, 512))]

        def table(name, a=0, n=None):
            o, m = NSA_TABLE[name]
            return at(TABLE + o + a, m - a if n is None else n)

        QS = [sil[:, 0:512], sil[:, 512:1024]]
        GATES_T, HIDC = at(TABLE, TOKENS), at(TABLE + TOKENS, 2 * CMP_HID)
        HIDK, HIDV = at(NSA_WIN + 1024, 256), at(ACT_AT, 1024)

        LOGF, LOG1P = at(ACT_AT, TOKENS), at(ACT_AT + TOKENS, TOKENS)
        MINUS_C = sil[:, 0:TOKENS]
        SLOT_C = at(2048, HG * TOKENS)
        SLOT_HI, SLOT_LO = hid_hi[:, 0:HG * TOKENS], hid_lo[:, 0:HG * TOKENS]
        IN_GROUP = hid_hi[:, HID - 8:HID - 8 + GROUPS]

        def K(name, a=0, n=None):
            o, m = CONST[name]
            return const[:, o + a:o + a + (m - a if n is None else n)]

        def C(name, a=0, n=None):
            o, m = COLS[name]
            return cols[:, o + a:o + a + (m - a if n is None else n)]

        def xs(c, n=1):
            return X[:, c * TOKENS:(c + n) * TOKENS]

        def chunk(t, c, n=1):
            return t[:, c * TOKENS:(c + n) * TOKENS]

        def pool_u(hid, h, half, tok, a, n):
            return hid[:, tok * 512 + a:tok * 512 + a + n] if half == 0 else h[:, DM + tok * 512 + a:DM + tok * 512 + a + n]

        def pooled_chunk(hid, h, g, c, n=1):
            return chunk(h, 2 * g + c, n) if g < 2 else chunk(hid, 2 * (g - 2) + c, n)

        def lhs(t, c, tok):
            return t[:, c * TOKENS + tok * P:c * TOKENS + (tok + 1) * P]

        def unit_cols(t, u, a, n):
            s = (u % RING) * UNIT
            return t[:, s + a:s + a + n]

        ident = K("ident")
        var, rstd = stat[:, 0:TT], stat[:, 4:4 + TT]
        nhalf = stat[:, 8:24]
        ssq, varq, rstdq = stat[:, 24:40], stat[:, 40:56], stat[:, 56:72]
        q_gain8 = stat[:, 72:73]
        nmax, rsum, coefs = stat[:, 80:96], stat[:, 96:112], stat[:, 112:128]
        cq = stat[:, 128:160]

        def S(name, free=0):
            return Signal(nc, ctx, name, free)

        cols_in_done, const_in, x_in_done = S("cols_in_done"), S("const_in"), [S(f"x_in_done{i}") for i in range(2)]
        row_in, out_done = S("row_in"), S("out_done")
        raw_in = [S(f"raw_in{r}") for r in range(RAW)]
        hi_done, lo_done, unit_used = S("hi_done"), S("lo_done"), S("unit_used")
        x_ready, normed, squares_ready = S("x_ready"), S("normed"), S("squares_ready")
        squares_added, sums_full = S("squares_added"), S("sums_full")
        var_ready, rstd_ready, rstd_full, rstd_read = S("var_ready"), S("rstd_ready"), S("rstd_full"), S("rstd_read")
        hT_full, hT_hi_done, hT_ready = S("hT_full"), S("hT_hi_done"), S("hT_ready")
        gu_full, scaled, silu_done, second_scaled = S("gu_full"), S("scaled"), S("silu_done"), S("second_scaled")
        hid_ready, hid_hi_done, hid_split = S("hid_ready"), S("hid_hi_done"), S("hid_split")
        acc_full = S("acc_full")
        proj_full, proj_free = S("proj_full"), [S("proj_free0", 3), S("proj_free1", 3)]
        p_hi_done, p_ready, sg_ready = S("p_hi_done"), S("p_ready"), S("sg_ready")
        u_hi_done, pool_full, pooled = S("u_hi_done"), S("pool_full"), S("pooled")
        sq_ready, ssq_ready, rstdq_ready, qn_ready = S("sq_ready"), S("ssq_ready"), S("rstdq_ready"), S("qn_ready")
        qk_full, tr_act, tr_dve = S("qk_full"), S("tr_act"), S("tr_dve")
        z_full, z_used, l_ready, l_used, nst_raw, nst_ready = S("z_full"), S("z_used"), S("l_ready"), S("l_used"), S("nst_raw"), S("nst_ready")
        after_full, warg_ready, w_raw, w_ready = S("after_full"), S("warg_ready"), S("w_raw"), S("w_ready")
        s_full, s_used, max_ready, p_done = S("s_full"), S("s_used"), S("max_ready"), S("p_done")
        t_full, tA_done, tB_done = S("t_full"), S("tA_done"), S("tB_done")
        coef_ready, pA_ready, pB_ready = S("coef_ready"), S("pA_ready"), S("pB_ready")
        zeros_ready = S("zeros_ready")
        cos_done, rot_full, rope_done, dup_full, dup_act, dup_dve = (
            S("cos_done"), S("rot_full"), S("rope_done"), S("dup_full"), S("dup_act"), S("dup_dve"))
        gatesT_ready, hidT_full, hidcV_ready, hid_cmp = S("gatesT_ready"), S("hidT_full"), S("hidcV_ready"), S("hid_cmp")
        gates_ready, win_tmp, win_hi, win_ready = S("gates_ready"), S("win_tmp"), S("win_hi"), S("win_ready")
        hidc_ready, cmp_full, cmp_kv = S("hidc_ready"), S("cmp_full"), S("cmp_kv")
        c_taken, slot_c, slot_hi, slot_split = S("c_taken"), S("slot_c"), S("slot_hi"), S("slot_split")
        fl_soft, c_full, c_ready = S("fl_soft"), S("c_full"), S("c_ready")
        act_step, dve_step, pool_step, even_done = S("act_step"), S("dve_step"), S("pool_step"), S("even_done")

        split = {"act": 0, "dve": 0}
        blocks_done = {"pe": 0, "act": 0, "dve": 0}

        def all_of(who, sigs, n):
            for s in sigs:
                s.due(who, n)

        block = ctx.enter_context(nc.Block())

        @block.sync
        def _(sp):
            view = stream.rearrange("(n r) p c -> n r p c", r=RAW)

            def first(r):
                sp.dma_start(raw[:, r * UNIT:(r + 1) * UNIT], view[0, r]).then_inc(raw_in[r].sem, 16)

            sp.dma_start(cols[:], cols_in).then_inc(cols_in_done.sem, 16)
            first(0)
            for i in range(2):
                sp.dma_start(xs(i * KC // 2, KC // 2), x_in[:, i * KC // 2 * TOKENS:(i + 1) * KC // 2 * TOKENS]).then_inc(x_in_done[i].sem, 16)
            first(1)
            sp.dma_start(const[:], consts_in).then_inc(const_in.sem, 16)
            first(2)
            with sp.Fori(1, units_total // RAW) as n:
                for r in range(RAW):
                    sp.wait_ge(lo_done.sem, n * RAW + (r - RAW + 1))
                    sp.dma_start(raw[:, r * UNIT:(r + 1) * UNIT], view[n, r]).then_inc(raw_in[r].sem, 16)
            for b in range(4):
                sp.wait_ge(x_ready.sem, 4 * (len(stages) - 1) + b + 1)
                sp.dma_start(out[b], xs(2 * b, 2)).then_inc(out_done.sem, 16)
            sp.wait_ge(out_done.sem, 16 * 4)

        @block.tensor
        def _(pe):
            me = "pe"

            def unit_ready(u, t=None):
                pe.wait_ge(lo_done.sem, u + 1 + (t.i * t.units if t else 0))

            def three(dst, a_hi, a_lo, b_hi, b_lo, start, stop):
                nc.tensor.matmul(dst, a_hi, b_hi, start=start, stop=False, skip_group_check=True)
                nc.tensor.matmul(dst, a_hi, b_lo, start=False, stop=False, skip_group_check=True)
                return nc.tensor.matmul(dst, a_lo, b_hi, start=False, stop=stop, skip_group_check=True)

            def columns(us, fresh=False, mid={}, own=None):
                per = KC // len(us)
                b0 = 2 * (blocks_done[me] % 3) if own is None else own
                blocks_done[me] += 1
                for tok in range(TT):
                    free = proj_free[tok].due(me)
                    if own is None:
                        pe.wait_ge(*free)
                for k in range(KC):
                    if k in mid:
                        mid[k]()
                    u = us[k // per]
                    if k % per == 0:
                        unit_ready(u)
                    if fresh:
                        pe.wait_ge(*hT_ready.due(me))
                    a = (k % per) * 512
                    for tok in range(TT):
                        mm = three(bank(b0 + tok), lhs(hT_hi, k, tok), lhs(hT_lo, k, tok), unit_cols(w_hi, u, a, 512),
                                   unit_cols(w_lo, u, a, 512), k == 0, k == KC - 1)
                        if (k, tok) == (KC - 1, 0):
                            mm.then_inc(proj_full.sem, 1)
                    if k % per == per - 1:
                        mm.then_inc(unit_used.sem, 1)

            def tile3(dst, u, a, b_hi, b_lo, start, stop):
                return three(dst, unit_cols(w_hi, u, a, P), unit_cols(w_lo, u, a, P), b_hi, b_lo, start, stop)

            def half(b0, m):
                return bank(b0 + m // 2, (m % 2) * TOKENS, TOKENS)

            def up(us, b0, tiles, full, fresh, t=None, mid={}):
                per = KC // len(us)
                for k in range(KC):
                    if k in mid:
                        mid[k]()
                    u = us[k // per]
                    if k % per == 0:
                        unit_ready(u, t)
                    if fresh:
                        pe.wait_ge(*hT_ready.due(me))
                    for m in range(tiles):
                        mm = tile3(half(b0, m), u, ((k % per) * tiles + m) * P, chunk(hT_hi, k), chunk(hT_lo, k),
                                   k == 0 and m % 2 == 0, k == KC - 1)
                        if full and (k, m) == (KC - 1, 1):
                            mm.then_inc(full.sem, 1)
                    if k % per == per - 1:
                        mm.then_inc(unit_used.sem, 1)

            def project(u):
                pe.wait_ge(*hT_ready.due(me, GROUPS))
                for k in range(KC):
                    for m in range(KC):
                        v = u + 2 * (m // 4) + k // 4
                        if m % 4 == 0 and k % 4 == 0:
                            unit_ready(v)
                        mm = tile3(half(4, m), v, ((k % 4) * 4 + m % 4) * P, chunk(hT_hi, k), chunk(hT_lo, k),
                                   k == 0 and m % 2 == 0, k == KC - 1)
                        if (k, m) in ((4, 0), (KC - 1, 4), (KC - 1, 6), (KC - 1, 7)):
                            mm.then_inc(unit_used.sem, 1)
                        elif k == KC - 1 and m % 2 == 1:
                            mm.then_inc(acc_full.sem, 1)

            def sum_squares(pairs, b):
                for p in pairs:
                    pe.wait_ge(*squares_ready.due(me))
                    for c in (2 * p, 2 * p + 1):
                        for tok in range(TT):
                            mm = nc.tensor.matmul(bank(b, tok * P, P), at(SQUARES + c * TOKENS + tok * P, P), K("ones"),
                                                  start=c + tok == 0, stop=c == KC - 1, skip_group_check=True)
                if pairs[-1] == 3:
                    mm.then_inc(sums_full.sem, 1)

            def spread(b):
                pe.wait_ge(*rstd_ready.due(me))
                for tok in range(TT):
                    mm = nc.tensor.matmul(bank(b, TOKENS + tok * P, P), rstd[:, tok:tok + 1].broadcast_to((P, P)), ident, start=True, stop=True, skip_group_check=True)
                mm.then_inc(rstd_full.sem, 1)

            def sums(s):
                if s:
                    pe.wait_ge(x_ready.sem, 4 * s)
                else:
                    pe.wait_ge(const_in.sem, 16)
                squares_ready.due(me, 4)
                pe.wait_ge(*squares_added.due(me))
                for tok in range(TT):
                    mm = nc.tensor.matmul(bank(7, tok * P, P), at(SQUARES + tok * P, P), K("ones"), start=tok == 0, stop=True, skip_group_check=True)
                mm.then_inc(sums_full.sem, 1)

            def post_norm(first):
                sum_squares(range(first, 4), 3)
                spread(3)

            def mlp(s, u0, blocks, ups, banks, turns, per_turn):
                step = ups + 1

                def down(u, first, last, t=None):
                    h = HC if last else 0
                    unit_ready(u, t)
                    pe.wait_ge(*hid_split.due(me, turn=t))
                    for b in range(4):
                        if last and b == 3 and ups == 1:
                            sum_squares([0], 3)
                        for c in range(HC):
                            for m in (2 * b, 2 * b + 1):
                                mm = tile3(half(4, m), u, c * DM + m * P, chunk(hid_hi, h + c), chunk(hid_lo, h + c),
                                           first and c == 0 and m % 2 == 0, last and c == HC - 1)
                        if b == 3:
                            mm.then_inc(unit_used.sem, 1)
                        elif last:
                            mm.then_inc(acc_full.sem, 1)

                def one(j, u, t=None, mid={}):
                    up(list(range(u, u + ups)), ups * (j % banks), 2 * ups, gu_full if ups == 2 else None, j == 0, t, mid)
                    if j:
                        down(u + ups, j == 1, False, t)

                norm = {6: lambda: sums(s)}, {2: lambda: spread(7)}
                if ups == 1:
                    norm = {}, {1: lambda: sums(s), 4: lambda: spread(7)}
                one(0, u0, mid=norm[0])
                one(1, u0 + ups, mid=norm[1])
                u = u0 + ups + step
                with pe.Fori(0, turns) as i:
                    t = Turn(i, {hid_split: per_turn}, per_turn * step)
                    for b in range(per_turn):
                        one(2 + b, u + b * step, t)
                hid_split.due(me, per_turn * (turns - 1))
                u += turns * per_turn * step
                for j in range(2 + turns * per_turn, blocks):
                    one(j, u)
                    u += step
                down(u, False, True)

            def columns_t(us, fresh=False, mid={}):
                b0 = 2 * (blocks_done[me] % 3)
                blocks_done[me] += 1
                for tok in range(TT):
                    pe.wait_ge(*proj_free[tok].due(me))
                up(us, b0, 4, proj_full, fresh, None, mid)

            def head(off, h, a=0, n=TOKENS):
                r = DH * (h % 2)
                return arena[r:r + DH, off + (h // 2) * TOKENS + a:off + (h // 2) * TOKENS + a + n]

            def A(b0, h, a, n):
                return ps[:, b0 * 512 + h * 256 + a:b0 * 512 + h * 256 + a + n]

            def stick(s, u0):
                def transpose_half(off):
                    pe.wait_ge(*qn_ready.due(me))
                    for p in range(PAIRS // 2):
                        for tok in range(TT):
                            mm = nc.tensor.transpose(bank(6 + p // 2, (p % 2) * TOKENS + tok * P, P), at(off + tok * 512 + p * P, P), ident)
                        if p % 2 == 1:
                            mm.then_inc(qk_full.sem, 1)

                columns([u0, u0 + 1], fresh=True)
                sums(s)
                rstd_ready.due(me)
                columns([u0 + 2, u0 + 3])
                transpose_half(0)
                columns([u0 + 4, u0 + 5])
                transpose_half(DM)
                columns([u0 + 6, u0 + 7])
                transpose_half(0)
                columns([u0 + 8, u0 + 9])
                transpose_half(DM)
                for tok in range(TT):
                    pe.wait_ge(*proj_free[tok].due("pe_all", 5))
                pe.wait_ge(*tr_act.due(me, 4))
                pe.wait_ge(*tr_dve.due(me, 2))

                def scores(g):
                    if g:
                        pe.wait_ge(*z_used.due(me))
                    for s in range(HG):
                        h = HG * g + SLOT_HEAD[s]
                        nc.tensor.matmul(A(0, s, 0, 256), head(KT, h, 0, P), head(QT, h), start=True, stop=True)
                        if s == 2:
                            pe.wait_ge(*even_done.due(me))
                        mm = nc.tensor.matmul(bank(2, s * P, P), head(KT, h, P, P), head(QT, h, P, P), start=True, stop=True)
                        if s == 1:
                            mm.then_inc(even_done.sem, 1)
                    mm.then_inc(z_full.sem, 1)

                def after(g):
                    if g:
                        pe.wait_ge(*warg_ready.due(me))
                    pe.wait_ge(*nst_ready.due(me))
                    nA, nB = NST[g % 2]
                    for b in range(2):
                        nc.tensor.matmul(bank(3 + b), K("after_neg"), nA[:, b * 512:(b + 1) * 512], start=True, stop=False, skip_group_check=True)
                        for s in (2 * b, 2 * b + 1):
                            nc.tensor.matmul(A(3, s, P, P), K("ones_neg"), nB[:, s * P:(s + 1) * P], start=False, stop=True, skip_group_check=True)
                    nc.tensor.matmul(bank(5), K("after_neg"), nB, start=True, stop=True).then_inc(after_full.sem, 1)

                def weighted(g):
                    pe.wait_ge(*w_ready.due(me))
                    wA, wB = LOGW[g]
                    for s in range(HG):
                        j = SLOT_HEAD[s]
                        h = HG * g + j
                        r, o = DH * (h % 2), (6 + g % 2) * 512 + (j // 2) * TOKENS
                        v0, v1 = at(QKV + 4096 + h * DH, DH), at(QKV + 4096 + DM + h * DH, DH)
                        nc.tensor.matmul(ps[r:r + DH, o:o + 256], v0, wA[:, s * 256:(s + 1) * 256], start=True, stop=False, skip_group_check=True)
                        mm = nc.tensor.matmul(ps[r:r + DH, o + P:o + 256], v1, wB[:, s * P:(s + 1) * P], start=False, stop=True, skip_group_check=True)
                    mm.then_inc(hT_full.sem, 1)

                def second_half():
                    pe.wait_ge(*tr_dve.due(me, 2))

                scores(0)
                second_half()
                columns([u0 + 10, u0 + 11], mid={2: lambda: scores(1), 5: lambda: scores(2)}, own=6)
                after(0)
                scores(3)
                after(1)
                for tok in range(TT):
                    pe.wait_ge(*proj_free[tok].due("pe_all"))
                for n in range(GROUPS):
                    weighted(n)
                    if n + 2 < GROUPS:
                        after(n + 2)
                z_used.due(me)
                project(u0 + 12)

            def softmax_attention(jobs, q_of, k_of, v_of, prologue, v_ready=None):
                heads_before = hT_ready.seen[me]

                def scores(n):
                    g, br = jobs[n]
                    if n >= 2:
                        pe.wait_ge(*s_used.due(me, 2 if n == 2 and br != "cmp" else 1))
                    b0 = 3 if n == 1 else 0
                    if br == "cmp":
                        if g == 0:
                            pe.wait_ge(*cmp_kv.due(me))
                        for qt in range(TT):
                            for j in range(HG):
                                mm = nc.tensor.matmul(ps[:, (qt * HG + j) * P:(qt * HG + j + 1) * P], q_of(HG * g + j, qt * P, P), cmp_keys(g), start=True, stop=True, skip_group_check=True)
                        mm.then_inc(s_full.sem, 1)
                        return
                    one = br != "fox"
                    if not one:
                        pick = IN_GROUP[:, g:g + 1].broadcast_to((P, P))
                        for b in range(3):
                            for part in (SLOT_HI, SLOT_LO):
                                c = part[:, b * 512:(b + 1) * 512] if b < 2 else part.rearrange("p (s t) -> p s t", s=HG)[:, :, 0:P]
                                nc.tensor.matmul(bank(b0 + b), pick, c, start=part is SLOT_HI, stop=False, skip_group_check=True)
                    for s in range(HG):
                        h = HG * g + SLOT_HEAD[s]
                        nc.tensor.matmul(A(b0, s, 0, 256), q_of(h, P, P), k_of(br, h, 0, 256), start=one, stop=True, skip_group_check=True)
                        if s == 2 and not one:
                            pe.wait_ge(*even_done.due(me))
                        mm = nc.tensor.matmul(bank(b0 + 2, s * P, P), q_of(h, 0, P), k_of(br, h, 0, P), start=one, stop=True, skip_group_check=True)
                        if s == 1 and not one:
                            mm.then_inc(even_done.sem, 1)
                    mm.then_inc(s_full.sem, 1)

                def transposed(n):
                    g, br = jobs[n]
                    s0 = (n % 2) * 1536
                    pe.wait_ge(*pB_ready.due(me))
                    if br == "cmp":
                        for qt in range(TT):
                            mm = nc.tensor.transpose(bank(3, qt * P, P), at(s0 + qt * P, P), ident)
                    else:
                        pe.wait_ge(*pA_ready.due(me))
                        for s in range(HG):
                            sA, sB = at(s0 + s * 256, 256), at(s0 + 1024 + s * P, P)
                            nc.tensor.transpose(A(3, s, 0, P), sB, ident)
                            nc.tensor.transpose(A(3, s, P, P), sA[:, 0:P], ident)
                            mm = nc.tensor.transpose(bank(5, s * P, P), sA[:, P:256], ident)
                    mm.then_inc(t_full.sem, 1)

                def weighted(n):
                    g, br = jobs[n]
                    first = n == 0 or jobs[n - 1][0] != g
                    last = n == len(jobs) - 1 or jobs[n + 1][0] != g
                    pe.wait_ge(*tA_done.due(me))
                    if br != "cmp":
                        pe.wait_ge(*tB_done.due(me))
                    if first and g >= 2:
                        pe.wait_ge(hT_ready.sem, heads_before + g - 1)
                    if n == 0 and v_ready:
                        v_ready()
                    tA, tB = at(3072, 1024), at(ACT_AT, 512)
                    for s in range(HG):
                        j = SLOT_HEAD[s]
                        h = HG * g + j
                        r, o = DH * (h % 2), (6 + g % 2) * 512 + (j // 2) * TOKENS
                        if br == "cmp":
                            mm = nc.tensor.matmul(ps[r:r + DH, o:o + TOKENS], sil[:, h * DH:(h + 1) * DH], tA[:, 0:TOKENS], start=first and j < 2, stop=last, skip_group_check=True)
                        else:
                            nc.tensor.matmul(ps[r:r + DH, o:o + TOKENS], v_of(br, h, 0), tA[:, s * 256:(s + 1) * 256], start=first and j < 2, stop=False, skip_group_check=True)
                            mm = nc.tensor.matmul(ps[r:r + DH, o + P:o + TOKENS], v_of(br, h, 1), tB[:, s * P:(s + 1) * P], start=False, stop=last, skip_group_check=True)
                    if last:
                        mm.then_inc(hT_full.sem, 1)

                prologue(scores)
                for n in range(len(jobs)):
                    transposed(n)
                    if n + 2 < len(jobs):
                        scores(n + 2)
                    weighted(n)
                s_used.due(me)

            def fox(s, u0):
                up([u0], 6, 1, None, True)
                for b in range(4):
                    columns_t([u0 + 1 + 2 * b, u0 + 2 + 2 * b], mid={} if b else {3: lambda: sums(s), 6: lambda: spread(7)})
                columns([u0 + 9, u0 + 10])
                pe.wait_ge(*c_ready.due(me))
                for tok in range(TT):
                    mm = nc.tensor.transpose(bank(6, tok * HEADS, HEADS), MINUS_C[0:HEADS, tok * P:(tok + 1) * P], ident[0:HEADS, 0:HEADS])
                mm.then_inc(c_full.sem, 1)
                pe.wait_ge(*slot_split.due(me))
                for tok in range(TT):
                    pe.wait_ge(*proj_free[tok].due("pe_all", 12))
                pe.wait_ge(*c_taken.due(me))

                def v_ready():
                    for tok in range(TT):
                        pe.wait_ge(*proj_free[tok].due("pe_all"))

                def prologue(scores):
                    scores(0)
                    columns([u0 + 11, u0 + 12], mid={2: lambda: scores(1)}, own=6)

                softmax_attention(
                    FOX_JOBS, lambda h, a, n: head(QT, h, a, n), lambda br, h, a, n: head(KT, h, a, n),
                    lambda br, h, tok: at(QKV + 4096 + tok * DM + h * DH, DH), prologue, v_ready)
                project(u0 + 13)

            def rows_of(h):
                r = DH * (h // HG % 2)
                return slice(r, r + DH)

            def cmp_keys(g):
                return arena[rows_of(g * HG), CMP_K:CMP_K + P]

            def nsa(s, u0):
                def rot(banks):
                    for b in range(TT):
                        pe.wait_ge(*proj_free[b].due("pe_rot"))
                        if b < banks:
                            nc.tensor.matmul(bank(6 + b), table("swap"), QS[b], start=True, stop=True).then_inc(rot_full.sem, 1)

                def duplicate(off):
                    for g in range(GROUPS):
                        mm = nc.tensor.matmul(bank(6 + g // 2, (g % 2) * TOKENS, TOKENS), table("dup", (g % 2) * P, P),
                                              at(off + (g // 2) * TOKENS, TOKENS), start=True, stop=True, skip_group_check=True)
                        if g % 2 == 1:
                            mm.then_inc(dup_full.sem, 1)

                def rot_after(sig, n, banks):
                    def go():
                        pe.wait_ge(*sig.due(me, n))
                        rot(banks)
                    return go

                def first_rot():
                    pe.wait_ge(*row_in.due(me, 64))
                    rot(2)

                for tok in range(TT):
                    proj_free[tok].due("pe_rot", 8)
                columns_t([u0, u0 + 1], fresh=True, mid={6: lambda: sums(s)})
                columns_t([u0 + 2, u0 + 3], mid={1: lambda: spread(7), 5: first_rot})
                columns_t([u0 + 4, u0 + 5], mid={4: rot_after(rope_done, 2, 1)})
                pe.wait_ge(*rope_done.due(me))
                duplicate(NSA_K)
                columns_t([u0 + 6, u0 + 7], mid={4: rot_after(dup_act, 2, 2)})
                pe.wait_ge(*rope_done.due(me, 2))
                duplicate(NSA_V)
                columns([u0 + 8, u0 + 9], mid={4: rot_after(dup_dve, 2, 2)})
                pe.wait_ge(*rope_done.due(me, 2))
                up([u0 + 10], 6, 1, None, False)

                for kv, (hi, lo) in enumerate(((hid_hi, hid_lo), (hT_hi, hT_lo))):
                    pe.wait_ge(*win_ready.due(me))
                    for jj in range(CMP_LEN // 2):
                        u, w = u0 + 11 + 2 * kv + jj // 8, jj * NWIN
                        if jj % 8 == 0:
                            unit_ready(u)
                        a = (jj % 8) * CMP_HID
                        mm = three(bank(4 + kv, 0, CMP_HID), hi[:, w:w + P], lo[:, w:w + P], unit_cols(w_hi, u, a, CMP_HID),
                                   unit_cols(w_lo, u, a, CMP_HID), jj == 0, jj == CMP_LEN // 2 - 1)
                        if jj % 8 == 7:
                            mm.then_inc(unit_used.sem, 1)

                def transpose_hidden():
                    pe.wait_ge(*gatesT_ready.due(me))
                    for tok in range(TT):
                        mm = nc.tensor.transpose(bank(7, 128 + tok * 48, 48), GATES_T[0:48, tok * P:(tok + 1) * P], ident[0:48, 0:48])
                    for kv in range(2):
                        pe.wait_ge(*hidc_ready.due(me))
                        for fc in range(2):
                            mm = nc.tensor.transpose(bank(6 + kv, fc * 64, NWIN), HIDC[0:NWIN, kv * CMP_HID + fc * P:kv * CMP_HID + (fc + 1) * P], ident[0:NWIN, 0:NWIN])
                        mm.then_inc(hidT_full.sem, 1)

                def compress():
                    pe.wait_ge(*s_used.due(me))
                    pe.wait_ge(*hid_cmp.due(me))
                    pe.wait_ge(*hidcV_ready.due(me))
                    for half in range(2):
                        for fc in range(2):
                            nc.tensor.matmul(ps[DH * half:DH * half + DH, 0:P], C("cmp_w2", fc * DH, DH), HIDK[:, fc * P:(fc + 1) * P],
                                             start=fc == 0, stop=fc == 1, skip_group_check=True)
                    for g in range(GROUPS):
                        for fc in range(2):
                            mm = nc.tensor.matmul(bank(1, g * DH, DH), HIDV[:, fc * 512 + g * P:fc * 512 + (g + 1) * P], C("cmp_w2", 128 + fc * DH, DH),
                                                  start=fc == 0, stop=fc == 1, skip_group_check=True)
                    mm.then_inc(cmp_full.sem, 1)

                def prologue(scores):
                    scores(0)
                    transpose_hidden()
                    scores(1)
                    compress()

                softmax_attention(
                    NSA_JOBS, lambda h, a, n: arena[rows_of(h), QT + (h // (2 * HG) * HG + h % HG) * TOKENS + a:][:, 0:n],
                    lambda br, h, a, n: arena[rows_of(h), KT + (0 if br == "slc" else 512) + h // (2 * HG) * TOKENS + a:][:, 0:n],
                    lambda br, h, tok: at(NSA_KV + (0 if br == "slc" else 512) + tok * 256 + h // HG * DH, DH),
                    prologue)
                project(u0 + 15)

            def pool(s, u0):
                columns([u0, u0 + 1], fresh=True)
                sums(s)
                rstd_ready.due(me)
                columns([u0 + 2, u0 + 3])
                ub = u0 + 4
                unit_ready(ub)
                for tok in range(TT):
                    proj_free[tok].due("pe_u", 6)
                for c in range(KC):
                    if c % 4 == 0:
                        for tok in range(TT):
                            pe.wait_ge(*proj_free[tok].due("pe_u"))
                    for tt in range(TT):
                        rhs = unit_cols(w_hi, ub, (tt * 4 + c // 2) * TOKENS, TOKENS)
                        dst = bank(c // 2, (c % 2) * TOKENS, TOKENS)
                        nc.tensor.matmul(dst, pool_u(hid_hi, hT_hi, c // 4, tt, c % 4 * P, P), rhs, start=tt == 0, stop=False, skip_group_check=True)
                        mm = nc.tensor.matmul(dst, pool_u(hid_lo, hT_lo, c // 4, tt, c % 4 * P, P), rhs, start=False, stop=tt == 1, skip_group_check=True)
                    if c == KC - 1:
                        mm.then_inc(unit_used.sem, 1)
                    elif c % 2 == 1:
                        mm.then_inc(pool_full.sem, 1)
                ug = u0 + 5
                unit_ready(ug)
                for g in range(4):
                    pe.wait_ge(*hT_ready.due(me))
                    for m in (2 * g, 2 * g + 1):
                        for c in range(2):
                            mm = tile3(half(4, m), ug, (g * 2 + c) * 256 + (m % 2) * P, pooled_chunk(hid_hi, hT_hi, g, c), pooled_chunk(hid_lo, hT_lo, g, c),
                                       c == 0 and m % 2 == 0, c == 1)
                    mm.then_inc((acc_full if g < 3 else unit_used).sem, 1)

            def ple(s, u0):
                up([u0, u0 + 1], 0, 4, gu_full, True, mid={6: lambda: sums(s)})
                up([u0 + 2, u0 + 3], 2, 4, gu_full, False, mid={1: lambda: spread(7)})
                unit_ready(u0 + 4)
                pe.wait_ge(*p_ready.due(me))
                pe.wait_ge(rstd_read.sem, norm_of[s] + 1 - sum(kind in ("stick", "pool") for kind, _ in stages[:s]))
                for m in range(KC):
                    for c in range(2):
                        mm = tile3(half(4, m), u0 + 4, c * DM + m * P, chunk(hid_hi, c), chunk(hid_lo, c),
                                   c == 0 and m % 2 == 0, c == 1)
                    if m % 2 == 1:
                        mm.then_inc((acc_full if m < KC - 1 else unit_used).sem, 1)

            for s, ((kind, _), u0) in enumerate(zip(stages, starts)):
                if kind == "ffn":
                    mlp(s, u0, FFN_BLOCKS, 2, 2, 4, 2)
                elif kind == "mlp":
                    mlp(s, u0, MLP_BLOCKS, 1, 3, 4, 3)
                else:
                    {"stick": stick, "ple": ple, "pool": pool, "nsa": nsa, "fox": fox}[kind](s, u0)
                if kind in POST:
                    post_norm(1 if kind == "mlp" else 0)

        @block.scalar
        def _(act):
            me = "act"

            def split_to(n, t=None):
                n = min(n, units_total)
                while split[me] < n:
                    u = split[me]
                    split[me] += 1
                    more = t.i * t.units if t else 0
                    act.wait_ge(raw_in[u % RAW].sem, 16 * (u // RAW + 1) + (t.i * (16 * t.units // RAW) if t else 0))
                    if u >= RING:
                        act.wait_ge(unit_used.sem, u - RING + 1 + more)
                    r = u % RAW
                    nc.scalar.activation(unit_cols(w_hi, u, 0, UNIT), raw[:, r * UNIT:(r + 1) * UNIT], ACT.Copy).then_inc(hi_done.sem, 1)

            def step(ins):
                ins.then_inc(act_step.sem, 1)
                act.wait_ge(*act_step.due(me))

            def prepare(s):
                if s and stages[s - 1][0] == "ple":
                    act.wait_ge(unit_used.sem, starts[s] - 1)
                for b in range(4):
                    if s > 0:
                        act.wait_ge(*x_ready.due(me))
                    elif b % 2 == 0:
                        split_to(b // 2 + 1)
                        act.wait_ge(x_in_done[b // 2].sem, 16)
                    for c in (2 * b, 2 * b + 1):
                        nc.scalar.activation(chunk(hT_hi, c), xs(c), ACT.Copy, scale=C("gains", s * KC + c, 1)).then_inc(hT_hi_done.sem, 1)
                    nc.scalar.activation(at(SQUARES + b * 512, 512), xs(2 * b, 2), ACT.Square).then_inc(squares_ready.sem, 1)

            def square_acc(end):
                for b in range(4):
                    if b < 3:
                        act.wait_ge(*acc_full.due(me))
                    else:
                        act.wait_ge(unit_used.sem, end)
                    nc.scalar.activation(at(SQUARES + b * 512, 512), bank(4 + b), ACT.Square).then_inc(squares_ready.sem, 1)
                split_to(end + 5)

            def mlp(s, u0, blocks, ups, banks, turns, per_turn):
                step_u = ups + 1

                def one(j, u, t=None):
                    more = t.i * t.units if t else 0
                    if ups == 2:
                        act.wait_ge(*scaled.due(me, turn=t))
                        ins = nc.scalar.activation(sil[:, 0:512], sil[:, 0:512], ACT.Silu)
                    else:
                        act.wait_ge(unit_used.sem, u + 1 + more)
                        ins = nc.scalar.activation(sil[:, 0:512], bank(j % banks), ACT.Relu)
                    ins.then_inc(silu_done.sem, 1)
                    last = j == blocks - 1
                    ahead = u + ups + RING
                    if not last and j:
                        split_to(ahead - 1, t)
                    act.wait_ge(*hid_ready.due(me, turn=t))
                    if j and not last:
                        act.wait_ge(unit_used.sem, u + step_u + more)
                    nc.scalar.activation(chunk(hid_hi, HC if last else 0, HC), at(ACT_AT, 512), ACT.Copy).then_inc(hid_hi_done.sem, 1)
                    split_to(ahead - 1 if last else ahead, t)

                one(0, u0)
                one(1, u0 + ups)
                u = u0 + ups + step_u
                each = {scaled: per_turn, hid_ready: per_turn}
                with act.Fori(0, turns) as i:
                    t = Turn(i, each, per_turn * step_u)
                    for b in range(per_turn):
                        one(2 + b, u + b * step_u, t)
                if ups == 2:
                    scaled.due(me, per_turn * (turns - 1))
                hid_ready.due(me, per_turn * (turns - 1))
                split[me] += (turns - 1) * per_turn * step_u
                u += turns * per_turn * step_u
                for j in range(2 + turns * per_turn, blocks):
                    one(j, u)
                    u += step_u

            def evacuate(dst, parts=1, own=None):
                act.wait_ge(*proj_full.due(me))
                src = bank(2 * (blocks_done[me] % 3) if own is None else own)
                blocks_done[me] += 1
                nc.scalar.activation(dst, src if parts == 1 else src.rearrange("p (s d) -> p s d", s=parts), ACT.Copy, scale=rstd[:, 0:1]).then_inc(proj_free[0].sem, 1)

            def transposed_high(n):
                act.wait_ge(*hT_full.due(me))
                nc.scalar.activation(chunk(hT_hi, 2 * n, 2), bank(6 + n % 2), ACT.Copy).then_inc(hT_hi_done.sem, 1)

            def stick(s, u0):
                act.wait_ge(rstd_ready.sem, norm_of[s] + 1)
                for i in range(2):
                    for b, off in enumerate((0, DM)):
                        if (i, b) == (1, 1):
                            act.wait_ge(*qk_full.due(me, 2))
                        evacuate(at(off, 512))
                        if b == 1:
                            for half in range(2):
                                act.wait_ge(*qk_full.due(me))
                                nc.scalar.activation(at(i * DM + QT + half * 512, 512), bank(6 + half), ACT.Copy, scale=q_gain8).then_inc(tr_act.sem, 1)
                        for tok in range(TT):
                            act.wait_ge(*proj_free[tok].due(me))
                        nc.scalar.activation(at(ACT_AT, DM), at(off, DM), ACT.Square).then_inc(sq_ready.sem, 1)
                        split_to(u0 + 7 + 4 * i + 2 * b)
                evacuate(at(QKV + 4096, 512))
                split_to(u0 + 15)
                qk_full.due(me, 2)
                for tok in range(TT):
                    proj_free[tok].due(me, 2)
                nc.scalar.preload_act_table_set("natural_log_exp_and_others")

                def copy(n):
                    act.wait_ge(*z_full.due(me))
                    nc.scalar.activation(LOGW[n][0], ps[:, 0:1024], ACT.Copy)
                    nc.scalar.activation(LOGW[n][1], bank(2), ACT.Copy).then_inc(z_used.sem, 1)

                def logs(n):
                    act.wait_ge(*z_used.due(me))
                    if n:
                        act.wait_ge(*l_used.due(me))
                    a, b = LOGS
                    nc.scalar.activation(a, LOGW[n][0], ACT.Abs)
                    step(nc.scalar.activation(b, LOGW[n][1], ACT.Abs))
                    nc.scalar.activation(a, a, ACT.Exp, scale=-1.0)
                    step(nc.scalar.activation(b, b, ACT.Exp, scale=-1.0))
                    nc.scalar.activation(a, a, ACT.Ln, bias=1.0)
                    nc.scalar.activation(b, b, ACT.Ln, bias=1.0).then_inc(l_ready.sem, 1)

                copy(0)
                logs(0)
                copy(1)
                logs(1)
                copy(2)
                logs(2)
                evacuate(at(QKV + 4096 + 512, 512), own=6)
                for n in range(GROUPS):
                    act.wait_ge(*warg_ready.due(me))
                    nc.scalar.activation(LOGW[n][0], LOGW[n][0], ACT.Exp)
                    nc.scalar.activation(LOGW[n][1], LOGW[n][1], ACT.Exp).then_inc(w_raw.sem, 1)
                    if n == 0:
                        copy(3)
                        logs(3)
                    if n:
                        transposed_high(n - 1)
                    if n == 1:
                        split_to(u0 + 16)
                transposed_high(GROUPS - 1)
                split_to(u0 + 18)
                l_used.due(me)

            def softmax_attention(jobs, between):
                def exponentials(n):
                    act.wait_ge(*max_ready.due(me))
                    s0, m0 = (n % 2) * 1536, (n % 2) * 8
                    if jobs[n][1] == "cmp":
                        nc.scalar.activation(at(s0, 256), at(s0, 256), ACT.Exp).then_inc(p_done.sem, 1)
                        return
                    for s in range(HG):
                        for qt in range(TT):
                            e = at(s0 + s * 256, 256) if qt else at(s0 + 1024 + s * P, P)
                            c, to = m0 + qt * HG + s, m0 + qt * HG + SLOT_HEAD[s]
                            ins = nc.scalar.activation(e, e, ACT.Exp, bias=nmax[:, c:c + 1], accum_out=rsum[:, to:to + 1])
                    ins.then_inc(p_done.sem, 1)

                exponentials(0)
                for n in range(len(jobs) + 1):
                    if n + 1 < len(jobs):
                        exponentials(n + 1)
                    if n in between:
                        between[n]()
                    if n < len(jobs):
                        act.wait_ge(*t_full.due(me))
                        w = 256 if jobs[n][1] == "cmp" else 1024
                        nc.scalar.activation(at(3072, w), ps[:, 3 * 512:3 * 512 + w], ACT.Copy).then_inc(tA_done.sem, 1)
                    if n == len(jobs) or n and jobs[n][0] != jobs[n - 1][0]:
                        transposed_high(jobs[n - 1][0])

            def fox(s, u0):
                nc.scalar.preload_act_table_set("natural_log_exp_and_others")
                split_to(u0 + 6)
                act.wait_ge(*fl_soft.due(me))
                step(nc.scalar.activation(LOG1P, LOGF, ACT.Abs))
                step(nc.scalar.activation(LOG1P, LOG1P, ACT.Exp, scale=-1.0))
                nc.scalar.activation(LOG1P, LOG1P, ACT.Ln, bias=1.0).then_inc(l_ready.sem, 1)
                nc.scalar.activation(IN_GROUP, K("in_group"), ACT.Copy)
                act.wait_ge(*slot_c.due(me))
                nc.scalar.activation(SLOT_HI, SLOT_C, ACT.Copy).then_inc(slot_hi.sem, 1)
                proj_full.due(me, 4)
                blocks_done[me] += 4
                split_to(u0 + 14)
                evacuate(at(QKV + 4096, 512))
                split_to(u0 + 16)
                softmax_attention(FOX_JOBS, {0: lambda: evacuate(at(QKV + 4096 + 512, 512), own=6)})
                split_to(u0 + 19)

            def nsa(s, u0):
                split_to(u0 + 9)
                for b in range(2):
                    act.wait_ge(*dup_full.due(me))
                    src, dst = bank(6 + b).rearrange("p (g t) -> p g t", g=2), at(NSA_DUP + b * 512, 512).rearrange("p (g t) -> p g t", g=2)
                    nc.scalar.activation(dst[0:DH], src[0:DH], ACT.Copy)
                    nc.scalar.activation(dst[DH:P, :, 0:TOKENS - 1], src[DH:P, :, 1:TOKENS], ACT.Copy).then_inc(dup_act.sem, 1)
                split_to(u0 + 13)
                act.wait_ge(*win_tmp.due(me))
                nc.scalar.activation(hid_hi[:, 0:NWIN * 16], at(NSA_WIN, NWIN * 16), ACT.Copy).then_inc(win_hi.sem, 1)
                proj_full.due(me, 4)
                blocks_done[me] += 4
                evacuate(at(NSA_KV, 1024).rearrange("p (s t d) -> p s t d", s=2, t=TT)[:, :, 0], parts=2)
                act.wait_ge(unit_used.sem, u0 + 11)
                act.wait_ge(*win_tmp.due(me))
                nc.scalar.activation(hT_hi[:, 0:NWIN * 16], at(NSA_WIN + NWIN * 16, NWIN * 16), ACT.Copy).then_inc(win_hi.sem, 1)
                act.wait_ge(*scaled.due(me))
                nc.scalar.activation(GATES_T[0:48], GATES_T[0:48], ACT.Sigmoid).then_inc(gatesT_ready.sem, 1)
                split_to(u0 + 17)
                nc.scalar.preload_act_table(ACT.Silu)
                for kv in range(2):
                    act.wait_ge(unit_used.sem, u0 + 13 + 2 * kv)
                    nc.scalar.activation(HIDC[0:NWIN, kv * CMP_HID:(kv + 1) * CMP_HID], bank(4 + kv, 0, CMP_HID)[0:NWIN], ACT.Silu).then_inc(hidc_ready.sem, 1)
                nc.scalar.preload_act_table(ACT.Exp)
                act.wait_ge(*zeros_ready.due(me, 2))
                act.wait_ge(*hidT_full.due(me))
                for fc in range(2):
                    ins = nc.scalar.activation(HIDK[:, fc * P:(fc + 1) * P].rearrange("p (g c) -> p g c", g=GROUPS)[:, :, 0:NCMP],
                                               bank(6, fc * 64, NWIN).rearrange("p (g c) -> p g c", g=GROUPS), ACT.Copy)
                ins.then_inc(hid_cmp.sem, 1)
                softmax_attention(NSA_JOBS, {5: lambda: split_to(u0 + 18)})
                split_to(u0 + 21)

            def pool(s, u0):
                act.wait_ge(rstd_ready.sem, norm_of[s] + 1)
                for b in range(2):
                    b0 = 2 * (blocks_done[me] % 3)
                    blocks_done[me] += 1
                    act.wait_ge(*proj_full.due(me))
                    for tok in range(TT):
                        if b or tok:
                            act.wait_ge(unit_used.sem, u0 + 2 * b + 2)
                        nc.scalar.activation(pool_u(hid_hi, hT_hi, b, tok, 0, 512), bank(b0 + tok), ACT.Copy, scale=rstd[:, tok:tok + 1]).then_inc(u_hi_done.sem, 1)
                    if b == 0:
                        split_to(u0 + 8)
                for g in range(4):
                    act.wait_ge(*pooled.due(me))
                    nc.scalar.activation(pooled_chunk(hid_hi, hT_hi, g, 0, 2), at(2048 + g * 512, 512), ACT.Copy).then_inc(hT_hi_done.sem, 1)
                split_to(u0 + 9)

            def ple(s, u0):
                nc.scalar.preload_act_table(ACT.Sigmoid)
                for q in range(4):
                    act.wait_ge(*scaled.due(me))
                    nc.scalar.activation(at(q * 512, 512), at(q * 512, 512), ACT.Sigmoid).then_inc(sg_ready.sem, 1)
                    if q == 1:
                        split_to(u0 + 7)

            nc.scalar.preload_act_table(ACT.Silu)
            act.wait_ge(cols_in_done.sem, 16)
            nc.scalar.activation(q_gain8, C("q_gain"), ACT.Copy, scale=QSCALE).then_inc(proj_free[0].sem, 3)
            for s, ((kind, n), u0) in enumerate(zip(stages, starts)):
                if kind == "ple":
                    act.wait_ge(*row_in.due(me, 16))
                    act.wait_ge(unit_used.sem, u0 - 1)
                    nc.scalar.activation(chunk(hid_hi, 0, 2), at(9216, 512), ACT.Copy).then_inc(p_hi_done.sem, 1)
                prepare(s)
                if s == 0:
                    act.wait_ge(const_in.sem, 16)
                    nc.scalar.activation(hid_hi[:, HID - 8:HID], ident[:, 0:8], ACT.Copy)
                elif kind == "ffn":
                    nc.scalar.preload_act_table(ACT.Silu)
                split_to(u0 + {"mlp": 6, "ffn": 6}.get(kind, 5))
                if kind == "ffn":
                    mlp(s, u0, FFN_BLOCKS, 2, 2, 4, 2)
                elif kind == "mlp":
                    mlp(s, u0, MLP_BLOCKS, 1, 3, 4, 3)
                else:
                    {"stick": stick, "ple": ple, "pool": pool, "nsa": nsa, "fox": fox}[kind](s, u0)
                if kind in POST:
                    square_acc(u0 + n)
                else:
                    acc_full.due(me, 3)
                if kind == "pool":
                    row_in.due(me, 16)

        @block.vector
        def _(dve):
            me = "dve"

            def split_to(n, t=None):
                n = min(n, units_total)
                while split[me] < n:
                    u = split[me]
                    split[me] += 1
                    dve.wait_ge(hi_done.sem, u + 1 + (t.i * t.units if t else 0))
                    r = u % RAW
                    nc.vector.tensor_tensor(unit_cols(w_lo, u, 0, UNIT), raw[:, r * UNIT:(r + 1) * UNIT], f(unit_cols(w_hi, u, 0, UNIT)),
                                            ALU.subtract).then_inc(lo_done.sem, 1)

            def step(ins):
                ins.then_inc(dve_step.sem, 1)
                dve.wait_ge(*dve_step.due(me))

            def low(s, pair):
                for c in (2 * pair, 2 * pair + 1):
                    dve.wait_ge(*hT_hi_done.due(me))
                    nc.vector.scalar_tensor_tensor(chunk(hT_lo, c), xs(c), C("gains", s * KC + c, 1), f(chunk(hT_hi, c)), ALU.mult, ALU.subtract).then_inc(hT_ready.sem, 1)

            def mean_square(b):
                dve.wait_ge(*sums_full.due(me))
                nc.vector.tensor_scalar(var, ps[:, b * 512:b * 512 + TT * P:P], 1.0 / DM, EPS, ALU.mult, ALU.add).then_inc(var_ready.sem, 1)

            def take_rstd(b):
                dve.wait_ge(*rstd_full.due(me))
                nc.vector.tensor_copy(R, bank(b, TOKENS, TOKENS)).then_inc(rstd_read.sem, 1)
                dve.wait_ge(*rstd_read.due(me))

            def by_token(n):
                return R.unsqueeze(1).broadcast_to((P, n, TOKENS))

            def chunked(ap):
                return ap.rearrange("p (c t) -> p c t", t=TOKENS)

            def times_rstd(dst, src, scale=None):
                if scale is None:
                    return nc.vector.tensor_tensor(chunked(dst), chunked(src), by_token(2), ALU.mult)
                return nc.vector.scalar_tensor_tensor(chunked(dst), chunked(src), scale, by_token(2), ALU.mult, ALU.mult)

            def mlp(s, u0, blocks, ups, banks, turns, per_turn):
                step_u = ups + 1

                def one(j, u, t=None):
                    second = at(ACT_AT + 512, 512)
                    if ups == 2:
                        b0 = 2 * (j % banks)
                        dve.wait_ge(*gu_full.due(me, turn=t))
                        times_rstd(sil[:, 0:512], bank(b0)).then_inc(scaled.sem, 1)
                        dve.wait_ge(unit_used.sem, u + 2 + (t.i * t.units if t else 0))
                        times_rstd(second, bank(b0 + 1)).then_inc(second_scaled.sem, 1)
                        dve.wait_ge(*silu_done.due(me, turn=t))
                        dve.wait_ge(*second_scaled.due(me, turn=t))
                        factors = sil[:, 0:512], second
                    else:
                        dve.wait_ge(*silu_done.due(me, turn=t))
                        times_rstd(second, sil[:, 0:512]).then_inc(second_scaled.sem, 1)
                        dve.wait_ge(*second_scaled.due(me, turn=t))
                        factors = second, second
                    if j:
                        dve.wait_ge(*hid_split.due(me, turn=t))
                    nc.vector.tensor_tensor(at(ACT_AT, 512), *factors, ALU.mult).then_inc(hid_ready.sem, 1)
                    last = j == blocks - 1
                    ahead = u + ups + RING
                    if not last and j:
                        split_to(ahead - 1, t)
                    dve.wait_ge(*hid_hi_done.due(me, turn=t))
                    h = HC if last else 0
                    nc.vector.tensor_tensor(chunk(hid_lo, h, HC), at(ACT_AT, 512), f(chunk(hid_hi, h, HC)), ALU.subtract).then_inc(hid_split.sem, 1)
                    split_to(ahead - 1 if last else ahead, t)

                mean_square(7)
                split_to(u0 + (5 if ups == 2 else 4))
                take_rstd(7)
                one(0, u0)
                one(1, u0 + ups)
                u = u0 + ups + step_u
                each = {silu_done: per_turn, second_scaled: per_turn, hid_hi_done: per_turn, hid_split: per_turn}
                if ups == 2:
                    each[gu_full] = per_turn
                with dve.Fori(0, turns) as i:
                    t = Turn(i, each, per_turn * step_u)
                    for b in range(per_turn):
                        one(2 + b, u + b * step_u, t)
                for sig, n in each.items():
                    sig.due(me, n * (turns - 1))
                split[me] += (turns - 1) * per_turn * step_u
                u += turns * per_turn * step_u
                for j in range(2 + turns * per_turn, blocks):
                    one(j, u)
                    u += step_u
                hid_split.due(me)

            def add_to_x(s, kind, end, post):
                more = s + 1 < len(stages)
                if kind in POST:
                    mean_square(3)
                    acc_full.due(me, 3)
                    take_rstd(3)

                    def normed_pair(b):
                        for c in (2 * b, 2 * b + 1):
                            ins = nc.vector.scalar_tensor_tensor(at(c * TOKENS, TOKENS), bank(4 + b, (c % 2) * TOKENS, TOKENS), C("post_gains", post * KC + c, 1), R,
                                                                 ALU.mult, ALU.mult)
                        ins.then_inc(normed.sem, 1)

                    def add(b):
                        nc.vector.tensor_tensor(xs(2 * b, 2), xs(2 * b, 2), at(b * 512, 512), ALU.add).then_inc(x_ready.sem, 1)

                    normed_pair(0)
                    dve.wait_ge(*normed.due(me))
                    add(0)
                    normed_pair(1)
                    normed_pair(2)
                    if more:
                        low(s + 1, 0)
                    normed_pair(3)
                    if more:
                        low(s + 1, 1)
                    dve.wait_ge(*normed.due(me, 3))
                    dve.wait_ge(x_ready.sem, 4 * s + 3)
                    add(3)
                    if more:
                        low(s + 1, 2)
                        low(s + 1, 3)
                    return
                for b in range(4):
                    acc, xb = bank(4 + b), xs(2 * b, 2)
                    if b < 3:
                        dve.wait_ge(*acc_full.due(me))
                    else:
                        dve.wait_ge(unit_used.sem, end)
                    if kind == "ple":
                        dve.wait_ge(*sg_ready.due(me))
                        step(nc.vector.tensor_tensor(at(b * 512, 512), at(b * 512, 512), acc, ALU.mult))
                        ins = nc.vector.tensor_tensor(xb, xb, at(b * 512, 512), ALU.add)
                    elif kind == "ffn":
                        ins = nc.vector.scalar_tensor_tensor(xb, acc, 0.5, xb, ALU.mult, ALU.add)
                    elif kind == "stick":
                        ins = nc.vector.tensor_tensor(xb, acc, xb, ALU.add)
                    else:
                        for c in (2 * b, 2 * b + 1):
                            ins = nc.vector.scalar_tensor_tensor(xs(c), bank(4 + b, (c % 2) * TOKENS, TOKENS), C("pool_scale", c, 1), xs(c), ALU.mult, ALU.add)
                    ins.then_inc(x_ready.sem, 1)
                    if more and b:
                        low(s + 1, b - 1)
                if more:
                    low(s + 1, 3)

            def evacuate(dst, done, parts=1, own=None):
                dve.wait_ge(unit_used.sem, done)
                src = bank((2 * (blocks_done[me] % 3) if own is None else own) + 1)
                blocks_done[me] += 1
                if parts > 1:
                    src = src.rearrange("p (s d) -> p s d", s=parts)
                nc.vector.tensor_scalar(dst, src, rstd[:, 1:2], None, ALU.mult).then_inc(proj_free[1].sem, 1)

            def evacuate_t(dsts, done, scale=None):
                b0 = 2 * (blocks_done[me] % 3)
                blocks_done[me] += 1
                dve.wait_ge(*proj_full.due(me))
                times_rstd(dsts[0], bank(b0), scale).then_inc(proj_free[0].sem, 1)
                dve.wait_ge(unit_used.sem, done)
                times_rstd(dsts[1], bank(b0 + 1), scale).then_inc(proj_free[1].sem, 1)

            def transposed_low(g):
                dve.wait_ge(*hT_hi_done.due(me))
                nc.vector.tensor_tensor(chunk(hT_lo, 2 * g, 2), bank(6 + g % 2), f(chunk(hT_hi, 2 * g, 2)), ALU.subtract).then_inc(hT_ready.sem, 1)

            def stick(s, u0):
                def keys(i):
                    for half in range(2):
                        dve.wait_ge(*qk_full.due(me))
                        nc.vector.tensor_scalar(at(i * DM + KT + half * 512, 512), bank(6 + half), C("k_gain"), None, ALU.mult).then_inc(tr_dve.sem, 1)

                mean_square(7)
                proj_full.due(me, 6)
                dve.wait_ge(rstd_ready.sem, norm_of[s] + 1)
                for i in range(2):
                    for b, off in enumerate((0, DM)):
                        if (i, b) == (1, 0):
                            dve.wait_ge(*qk_full.due(me, 2))
                        evacuate(at(off + 512, 512), u0 + 4 * i + 2 * b + 2)
                        if (i, b) == (1, 0):
                            keys(0)
                        rows = at(off, DM).rearrange("p (a d) -> p a d", d=DH)
                        dve.wait_ge(*sq_ready.due(me))
                        nc.vector.tensor_reduce(ssq, at(ACT_AT, DM).rearrange("p (a d) -> p a d", d=DH), AX.X, ALU.add).then_inc(ssq_ready.sem, 1)
                        split_to(u0 + 6 + 4 * i + 2 * b)
                        dve.wait_ge(*rstdq_ready.due(me))
                        nc.vector.tensor_tensor(rows, rows, rstdq.unsqueeze(2).broadcast_to((P, HEADS, DH)), ALU.mult).then_inc(qn_ready.sem, 1)
                        split_to(u0 + 7 + 4 * i + 2 * b)
                evacuate(at(QKV + 4096 + DM, 512), u0 + 10)
                qk_full.due(me, 2)
                keys(1)
                split_to(u0 + 15)

                def stay(n):
                    dve.wait_ge(*l_ready.due(me))
                    for nst, z, l in zip(NST[n % 2], LOGW[n], LOGS):
                        ins = nc.vector.scalar_tensor_tensor(nst, z, 0.0, l, ALU.max, ALU.add)
                    ins.then_inc(nst_raw.sem, 1)

                def log_sigmoid(n):
                    dve.wait_ge(*nst_raw.due(me))
                    for z, l in zip(LOGW[n], LOGS):
                        ins = nc.vector.scalar_tensor_tensor(z, z, 0.0, l, ALU.min, ALU.subtract)
                    ins.then_inc(l_used.sem, 1)

                for n in range(2):
                    stay(n)
                    log_sigmoid(n)
                evacuate(at(QKV + 4096 + DM + 512, 512), u0 + 12, own=6)
                for n in range(GROUPS):
                    dve.wait_ge(*after_full.due(me))
                    dve.wait_ge(*l_used.due(me))
                    a, b = LOGW[n]
                    nc.vector.tensor_tensor(a, a, ps[:, 3 * 512:5 * 512], ALU.add)
                    nc.vector.tensor_tensor(b, b, bank(5), ALU.add).then_inc(warg_ready.sem, 1)
                    if n + 2 < GROUPS:
                        stay(n + 2)
                        log_sigmoid(n + 2)
                    if n:
                        transposed_low(n - 1)
                    if n == 1:
                        split_to(u0 + 16)
                transposed_low(GROUPS - 1)
                split_to(u0 + 18)

            def slots(ap):
                return ap.rearrange("p (pair odd) -> p odd pair", odd=2).unsqueeze(3)

            def softmax_attention(jobs, gates=None, early=(), spare={}):
                rows = TT * HG

                def by_row(ap):
                    return ap.rearrange("p (a d) -> p a d", a=rows)

                def masked_scores(n):
                    g, br = jobs[n]
                    dve.wait_ge(*s_full.due(me))
                    s0, m0 = (n % 2) * 1536, (n % 2) * 8
                    b0 = 3 if n == 1 else 0
                    if br == "cmp":
                        S = at(s0, 256)
                        s4 = S.rearrange("p (t h c) -> p t h c", t=TT, h=HG)
                        c4 = ps[:, 0:1024].rearrange("p (t h c) -> p t h c", t=TT, h=HG)[:, :, :, g * CPAD:(g + 1) * CPAD]
                        m3 = K("cmp_mask").rearrange("p (t c) -> p t c", t=TT)
                        for t in range(TT):
                            ins = nc.vector.tensor_tensor(s4[:, t], c4[:, t], m3[:, t].unsqueeze(1).broadcast_to((P, HG, CPAD)), ALU.add)
                        ins.then_inc(s_used.sem, 1)
                        dve.wait_ge(*s_used.due(me))
                        m = nmax[:, m0:m0 + rows]
                        step(nc.vector.tensor_reduce(m, by_row(S), AX.X, ALU.max, negate=True))
                        nc.vector.tensor_tensor(by_row(S), by_row(S), m.unsqueeze(2).broadcast_to((P, rows, CPAD)), ALU.add).then_inc(max_ready.sem, 1)
                        return
                    sA, sB = at(s0, 1024).rearrange("p (h k) -> p h k", h=HG), at(s0 + 1024, 512).rearrange("p (h k) -> p h k", h=HG)
                    if br != "fox":
                        nc.vector.tensor_tensor(sA, ps[:, b0 * 512:(b0 + 2) * 512].rearrange("p (h k) -> p h k", h=HG),
                                                K("mask").unsqueeze(1).broadcast_to((P, HG, 2 * P)), ALU.add)
                        ins = nc.vector.tensor_tensor(sB, bank(b0 + 2).rearrange("p (h k) -> p h k", h=HG),
                                                      K("mask", P, P).unsqueeze(1).broadcast_to((P, HG, P)), ALU.add)
                    else:
                        for s in range(HG):
                            h = HG * g + SLOT_HEAD[s]
                            nc.vector.scalar_tensor_tensor(sA[:, s], ps[:, b0 * 512 + s * 256:b0 * 512 + (s + 1) * 256], cq[:, HEADS + h:HEADS + h + 1], K("mask"), ALU.add, ALU.add)
                            ins = nc.vector.scalar_tensor_tensor(sB[:, s], bank(b0 + 2, s * P, P), cq[:, h:h + 1], K("mask", P, P), ALU.add, ALU.add)
                    ins.then_inc(s_used.sem, 1)
                    dve.wait_ge(*s_used.due(me))
                    nc.vector.tensor_reduce(nmax[:, m0:m0 + HG], sB, AX.X, ALU.max, negate=True)
                    nc.vector.tensor_reduce(nmax[:, m0 + HG:m0 + 2 * HG], sA, AX.X, ALU.max, negate=True).then_inc(max_ready.sem, 1)

                def weights(n):
                    g, br = jobs[n]
                    dve.wait_ge(*p_done.due(me))
                    s0, m0 = (n % 2) * 1536, (n % 2) * 8
                    coef, total = coefs[:, m0:m0 + rows], rsum[:, m0:m0 + rows]
                    c3 = coef.rearrange("p (t h) -> p t h", t=TT)
                    if br == "cmp":
                        step(nc.vector.tensor_reduce(total, by_row(at(s0, 256)), AX.X, ALU.add))
                    ins = nc.vector.reciprocal(coef, total)
                    if br != "fox":
                        step(ins)
                        ins = nc.vector.tensor_tensor(c3, c3, gates[:, :, HG * g:HG * (g + 1), ("cmp", "slc", "win").index(br)], ALU.mult)
                    if br == "cmp":
                        step(ins)
                        step(nc.vector.tensor_tensor(c3, c3, K("cmp_valid").unsqueeze(2).broadcast_to((P, TT, HG)), ALU.mult))
                        nc.vector.tensor_tensor(by_row(at(s0, 256)), by_row(at(s0, 256)), coef.unsqueeze(2).broadcast_to((P, rows, CPAD)), ALU.mult).then_inc(pB_ready.sem, 1)
                    else:
                        ins.then_inc(coef_ready.sem, 1)
                        dve.wait_ge(*coef_ready.due(me))
                        B = at(s0 + 1024, 512).rearrange("p (o a k) -> p o a k", o=2, a=2)
                        nc.vector.tensor_tensor(B, B, slots(coef[:, 0:HG]).broadcast_to((P, 2, 2, P)), ALU.mult).then_inc(pB_ready.sem, 1)

                masked_scores(0)
                if early:
                    early[0]()
                masked_scores(1)
                weights(0)
                if early:
                    early[1]()
                for n in range(len(jobs) + 1):
                    if n < len(jobs):
                        dve.wait_ge(*t_full.due(me))
                        if jobs[n][1] != "cmp":
                            nc.vector.tensor_copy(at(ACT_AT, 512), bank(5)).then_inc(tB_done.sem, 1)
                    if n + 1 < len(jobs):
                        weights(n + 1)
                    if n == len(jobs) or n and jobs[n][0] != jobs[n - 1][0]:
                        transposed_low(jobs[n - 1][0])
                    if n + 2 < len(jobs):
                        masked_scores(n + 2)
                    if n in spare:
                        split_to(spare[n])

            def fox(s, u0):
                mean_square(7)
                split_to(u0 + 6)
                take_rstd(7)
                dve.wait_ge(unit_used.sem, u0 + 1)
                step(nc.vector.tensor_tensor(LOGF, bank(6, 0, TOKENS), R, ALU.mult))
                nc.vector.tensor_scalar(LOGF, LOGF, C("b_f"), None, ALU.add).then_inc(fl_soft.sem, 1)
                dve.wait_ge(*l_ready.due(me))
                step(nc.vector.scalar_tensor_tensor(LOGF, LOGF, 0.0, LOG1P, ALU.min, ALU.subtract))
                nc.vector.tensor_tensor_scan(MINUS_C, K("ones")[:, 0:1].broadcast_to((P, TOKENS)), LOGF, 0.0, ALU.mult, ALU.subtract).then_inc(c_ready.sem, 1)
                dve.wait_ge(*c_ready.due(me))
                nc.vector.tensor_tensor(SLOT_C.rearrange("p (s t) -> p s t", s=HG), MINUS_C.unsqueeze(1).broadcast_to((P, HG, TOKENS)),
                                        K("in_slot").unsqueeze(2).broadcast_to((P, HG, TOKENS)), ALU.mult).then_inc(slot_c.sem, 1)
                dve.wait_ge(*slot_hi.due(me))
                nc.vector.tensor_tensor(SLOT_LO, SLOT_C, f(SLOT_HI), ALU.subtract).then_inc(slot_split.sem, 1)
                for b in range(4):
                    i, to = b // 2, (QT, KT)[b % 2]
                    evacuate_t([at(i * DM + to + c, 512) for c in (0, 512)], u0 + 3 + 2 * b, None if b % 2 else QSCALE)
                    split_to(u0 + 8 + 2 * b)
                proj_full.due(me, 2)
                evacuate(at(QKV + 4096 + DM, 512), u0 + 11)
                dve.wait_ge(*c_full.due(me))
                nc.vector.tensor_scalar(cq, bank(6, 0, 2 * HEADS), -1.0, None, ALU.mult).then_inc(c_taken.sem, 1)
                dve.wait_ge(*c_taken.due(me))
                split_to(u0 + 16)
                softmax_attention(FOX_JOBS, early=(lambda: None, lambda: evacuate(at(QKV + 4096 + DM + 512, 512), u0 + 13, own=6)))
                split_to(u0 + 19)

            def nsa(s, u0):
                def rope(b, dst):
                    dve.wait_ge(*rot_full.due(me))
                    dve.wait_ge(*cos_done.due(me))
                    x = QS[b].rearrange("p (c t) -> p c t", c=2)
                    step(nc.vector.tensor_tensor(x, bank(6 + b).rearrange("p (c t) -> p c t", c=2),
                                                 table("sin").unsqueeze(1).broadcast_to((P, 2, TOKENS)), ALU.mult))
                    nc.vector.tensor_tensor(dst, dst, QS[b], ALU.add).then_inc(rope_done.sem, 1)

                mean_square(7)
                split_to(u0 + 5)
                take_rstd(7)
                evacuate_t(QS, u0 + 2)
                split_to(u0 + 7)
                dve.wait_ge(*row_in.due(me, 16))
                rope(0, at(NSA_K, 512))
                rope(1, at(KT, 512))
                dve.wait_ge(*rope_done.due(me, 2))
                evacuate_t((QS[0], at(NSA_V, 512)), u0 + 4)
                split_to(u0 + 9)
                rope(0, at(KT + 512, 512))
                dve.wait_ge(*rope_done.due(me))
                evacuate_t(QS, u0 + 6, scale=QSCALE)
                split_to(u0 + 11)
                for b in range(2):
                    rope(b, at(QT + b * 512, 512))
                dve.wait_ge(*rope_done.due(me, 2))
                evacuate_t(QS, u0 + 8, scale=QSCALE)
                dup_full.due(me, 2)
                for b in range(2):
                    dve.wait_ge(*dup_full.due(me))
                    src, dst = bank(6 + b).rearrange("p (g t) -> p g t", g=2), at(NSA_DUP + 1024 + b * 512, 512).rearrange("p (g t) -> p g t", g=2)
                    nc.vector.tensor_copy(dst[0:DH], src[0:DH])
                    nc.vector.tensor_copy(dst[DH:P, :, 0:TOKENS - 1], src[DH:P, :, 1:TOKENS]).then_inc(dup_dve.sem, 1)
                split_to(u0 + 13)
                for b in range(2):
                    rope(b, at(QT + 1024 + b * 512, 512))

                def low_windows(kv, hi, lo):
                    dve.wait_ge(*win_hi.due(me))
                    nc.vector.tensor_tensor(lo[:, 0:NWIN * 16], at(NSA_WIN + kv * NWIN * 16, NWIN * 16), f(hi[:, 0:NWIN * 16]), ALU.subtract).then_inc(win_ready.sem, 1)

                low_windows(0, hid_hi, hid_lo)
                evacuate(at(NSA_KV, 1024).rearrange("p (s t d) -> p s t d", s=2, t=TT)[:, :, 1], u0 + 10, parts=2)
                proj_full.due(me)
                dve.wait_ge(unit_used.sem, u0 + 11)
                nc.vector.tensor_tensor(GATES_T[0:48], bank(6, 0, TOKENS)[0:48], R[0:48], ALU.mult).then_inc(scaled.sem, 1)
                low_windows(1, hT_hi, hT_lo)
                split_to(u0 + 17)

                def hidden_values():
                    hidT_full.due(me)
                    dve.wait_ge(*hidT_full.due(me))
                    dve.wait_ge(*zeros_ready.due(me, 2))
                    for fc in range(2):
                        dst = HIDV[:, fc * 512:(fc + 1) * 512].rearrange("p (g r c) -> p g r c", g=GROUPS, r=HG)
                        for g in range(GROUPS):
                            ins = nc.vector.tensor_copy(dst[:, g, :, 0:NCMP], bank(7, fc * 64 + g * NCMP, NCMP).unsqueeze(1).broadcast_to((P, HG, NCMP)))
                    ins.then_inc(hidcV_ready.sem, 1)
                    nc.vector.tensor_copy(at(GATES, 96), bank(7, 128, 96)).then_inc(gates_ready.sem, 1)
                    dve.wait_ge(*gates_ready.due(me))

                def compressed():
                    dve.wait_ge(*cmp_full.due(me))
                    dve.wait_ge(*rope_done.due(me, 2))
                    nc.vector.tensor_copy(at(CMP_K, P), bank(0, 0, P))
                    by_head = bank(1, 0, 256).rearrange("p (g d) -> p g d", g=GROUPS).unsqueeze(2).broadcast_to((P, GROUPS, HG, DH))
                    nc.vector.tensor_tensor(sil[:].rearrange("p (g h d) -> p g h d", g=GROUPS, h=HG), by_head,
                                            K("head_block").unsqueeze(1).unsqueeze(3).broadcast_to((P, GROUPS, HG, DH)), ALU.mult).then_inc(cmp_kv.sem, 1)

                softmax_attention(NSA_JOBS, at(GATES, 96).rearrange("p (t h x) -> p t h x", t=TT, x=3), early=(hidden_values, compressed), spare={5: u0 + 18})
                split_to(u0 + 21)

            def pool(s, u0):
                mean_square(7)
                proj_full.due(me, 2)
                dve.wait_ge(rstd_ready.sem, norm_of[s] + 1)
                for b in range(2):
                    b0 = 2 * (blocks_done[me] % 3)
                    blocks_done[me] += 1
                    for tok in range(TT):
                        dve.wait_ge(*u_hi_done.due(me))
                        nc.vector.scalar_tensor_tensor(pool_u(hid_lo, hT_lo, b, tok, 0, 512), bank(b0 + tok), rstd[:, tok:tok + 1],
                                                       f(pool_u(hid_hi, hT_hi, b, tok, 0, 512)), ALU.mult, ALU.subtract).then_inc(proj_free[tok].sem, 1)
                    if b == 0:
                        split_to(u0 + 8)
                dve.wait_ge(*row_in.due(me, 16))
                for b in range(4):
                    if b < 3:
                        dve.wait_ge(*pool_full.due(me))
                    else:
                        dve.wait_ge(unit_used.sem, u0 + 5)
                    inv = at(7168 + b * TOKENS, TOKENS).unsqueeze(1).broadcast_to((P, 2, TOKENS))
                    nc.vector.tensor_tensor(at(2048 + b * 512, 512).rearrange("p (c t) -> p c t", c=2),
                                            bank(b).rearrange("p (c t) -> p c t", c=2), inv, ALU.mult).then_inc(pooled.sem, 1)
                for b in range(4):
                    dve.wait_ge(*hT_hi_done.due(me))
                    nc.vector.tensor_tensor(pooled_chunk(hid_lo, hT_lo, b, 0, 2), at(2048 + b * 512, 512), f(pooled_chunk(hid_hi, hT_hi, b, 0, 2)),
                                            ALU.subtract).then_inc(hT_ready.sem, 1)

            def ple(s, u0):
                mean_square(7)
                split_to(u0 + 4)
                take_rstd(7)
                for q in range(4):
                    if q % 2 == 0:
                        dve.wait_ge(*gu_full.due(me))
                    else:
                        dve.wait_ge(unit_used.sem, u0 + 1 + q)
                    times_rstd(at(q * 512, 512), bank(q)).then_inc(scaled.sem, 1)
                    if q == 1:
                        split_to(u0 + 7)

            nc.vector.memset(nhalf, -0.5).then_inc(proj_free[1].sem, 3)
            dve.wait_ge(cols_in_done.sem, 16)
            posts = 0
            for i in range(2):
                split_to(i + 1)
                dve.wait_ge(x_in_done[i].sem, 16)
                low(0, 2 * i)
                low(0, 2 * i + 1)
            dve.wait_ge(const_in.sem, 16)
            nc.vector.tensor_copy(hid_lo[:, HID - 8:HID], ident[:, 0:8])
            for s, ((kind, n), u0, nxt) in enumerate(zip(stages, starts, stages[1:] + [("", 0)])):
                split_to(u0 + (5 if kind in ("stick", "pool") else 3))
                if kind == "ffn":
                    mlp(s, u0, FFN_BLOCKS, 2, 2, 4, 2)
                elif kind == "mlp":
                    mlp(s, u0, MLP_BLOCKS, 1, 3, 4, 3)
                else:
                    {"stick": stick, "ple": ple, "pool": pool, "nsa": nsa, "fox": fox}[kind](s, u0)
                if nxt[0] == "ple":
                    dve.wait_ge(*p_hi_done.due(me))
                    row_in.due(me, 16)
                    nc.vector.tensor_tensor(chunk(hid_lo, 0, 2), at(9216, 512), f(chunk(hid_hi, 0, 2)), ALU.subtract).then_inc(p_ready.sem, 1)
                add_to_x(s, kind, u0 + n, posts)
                posts += kind in POST

        @block.gpsimd
        def _(pool):
            me = "pool"

            def step(ins):
                ins.then_inc(pool_step.sem, 1)
                pool.wait_ge(*pool_step.due(me))

            def inverse_rms(sums, tmp, dst, n, width):
                step(nc.gpsimd.tensor_scalar(tmp, sums, 1.0 / width, EPS, ALU.mult, ALU.add))
                return nc.gpsimd.tensor_tensor(dst, tmp, nhalf[:, 0:n], ALU.pow)

            def inverse_rms_of_tokens():
                pool.wait_ge(*var_ready.due(me))
                nc.gpsimd.tensor_tensor(rstd, var, nhalf[:, 0:TT], ALU.pow).then_inc(rstd_ready.sem, 1)

            def add_squares():
                total = at(SQUARES, 512)
                pool.wait_ge(*squares_ready.due(me))
                for b in range(1, 4):
                    pool.wait_ge(*squares_ready.due(me))
                    step(nc.gpsimd.tensor_tensor(total, total, at(SQUARES + b * 512, 512), ALU.add))
                nc.gpsimd.tensor_tensor(at(SQUARES, TOKENS), at(SQUARES, TOKENS), at(SQUARES + TOKENS, TOKENS), ALU.add).then_inc(squares_added.sem, 1)

            def causal_zero(z, heads):
                return nc.gpsimd.affine_select(out=z, in_=z, compare_op=ALU.is_gt, fill=0.0, base=0,
                                               pattern=[[0, heads], [1, P]], channel_multiplier=-1)

            def diagonal_zero(a, b):
                causal_zero(a.rearrange("p (h q) -> p h q", h=HG)[:, :, 0:P], HG)
                return causal_zero(b.rearrange("p (h q) -> p h q", h=HG), HG)

            def nsa():
                pool.dma_start(at(TABLE, NTABLE), table_in).then_inc(row_in.sem, 16)
                nc.gpsimd.memset(HIDV, 0.0).then_inc(zeros_ready.sem, 1)
                pool.wait_ge(row_in.sem, 64)
                for tok in range(TT):
                    proj_free[tok].due(me, 8)

                def times_cos(b, dst):
                    pool.wait_ge(*proj_free[b].due(me))
                    if dst is None:
                        return
                    nc.gpsimd.tensor_tensor(dst.rearrange("p (c t) -> p c t", c=2), QS[b].rearrange("p (c t) -> p c t", c=2),
                                            table("cos").unsqueeze(1).broadcast_to((P, 2, TOKENS)), ALU.mult).then_inc(cos_done.sem, 1)

                def windows(kv, sig):
                    pool.wait_ge(*sig.due(me, 2))
                    half = CMP_LEN // 2
                    pos = C("cmp_pos", kv * half, half).unsqueeze(2).broadcast_to((P, half, NCMP))
                    for g in range(GROUPS):
                        src = at(NSA_DUP + kv * 1024 + g * TOKENS, TOKENS).rearrange("p (b j) -> p j b", j=CMP_STRIDE)
                        dst = at(NSA_WIN + kv * 16 * NWIN, 16 * NWIN).rearrange("p (j g b) -> p j g b", j=half, g=GROUPS)[:, :, g, :]
                        q = half // 2
                        nc.gpsimd.tensor_tensor(dst[:, 0:q], src[:, 0:CMP_STRIDE:2, 0:NCMP], pos[:, 0:q], ALU.add)
                        ins = nc.gpsimd.tensor_tensor(dst[:, q:half], src[:, 0:CMP_STRIDE:2, 1:NCMP + 1], pos[:, q:half], ALU.add)
                    ins.then_inc(win_tmp.sem, 1)
                    pool.wait_ge(*win_tmp.due(me))

                times_cos(0, at(NSA_K, 512))
                times_cos(1, at(KT, 512))
                times_cos(0, at(KT + 512, 512))
                times_cos(1, None)
                for b in range(2):
                    times_cos(b, at(QT + b * 512, 512))
                windows(0, dup_act)
                for b in range(2):
                    times_cos(b, at(QT + 1024 + b * 512, 512))
                windows(1, dup_dve)
                pool.wait_ge(*win_ready.due(me, 2))
                nc.gpsimd.memset(HIDK, 0.0).then_inc(zeros_ready.sem, 1)

            def second_tile_weights(jobs):
                for n, (_, br) in enumerate(jobs):
                    if br == "cmp":
                        continue
                    pool.wait_ge(*coef_ready.due(me))
                    A = at((n % 2) * 1536, 1024).rearrange("p (o a k) -> p o a k", o=2, a=2)
                    c = coefs[:, (n % 2) * 8 + HG:(n % 2) * 8 + 2 * HG].rearrange("p (pair odd) -> p odd pair", odd=2)
                    nc.gpsimd.tensor_tensor(A, A, c.unsqueeze(3).broadcast_to((P, 2, 2, 2 * P)), ALU.mult).then_inc(pA_ready.sem, 1)

            pool.wait_ge(proj_free[1].sem, 3)
            layer = 0
            for (kind, _), nxt in zip(stages, stages[1:] + [("", 0)]):
                add_squares()
                inverse_rms_of_tokens()
                if kind == "stick":
                    for block in range(4):
                        pool.wait_ge(*ssq_ready.due(me))
                        inverse_rms(ssq, varq, rstdq, HEADS, DH).then_inc(rstdq_ready.sem, 1)
                    for n in range(-1, GROUPS):
                        if n + 1 < GROUPS:
                            pool.wait_ge(*nst_raw.due(me))
                            diagonal_zero(*NST[(n + 1) % 2]).then_inc(nst_ready.sem, 1)
                        if n >= 0:
                            pool.wait_ge(*w_raw.due(me))
                            diagonal_zero(*LOGW[n]).then_inc(w_ready.sem, 1)
                    hT_ready.due(me, KC + GROUPS)
                elif kind == "pool":
                    pool.wait_ge(*hT_ready.due(me, KC))
                    pool.dma_start(at(7168, 4 * TOKENS), count_in).then_inc(row_in.sem, 16)
                    hT_ready.due(me, 4)
                else:
                    pool.wait_ge(*hT_ready.due(me, KC))
                    if kind == "nsa":
                        nsa()
                    if nxt[0] == "ple":
                        pool.dma_start(at(9216, 2 * TOKENS), p_in[layer]).then_inc(row_in.sem, 16)
                        layer += 1
                    if kind in ("nsa", "fox"):
                        second_tile_weights(NSA_JOBS if kind == "nsa" else FOX_JOBS)
                        hT_ready.due(me, GROUPS)
                    if kind in POST:
                        squares_ready.due(me, 4)
                        inverse_rms_of_tokens()
                        normed.due(me)
                        for b in (1, 2):
                            pool.wait_ge(*normed.due(me))
                            nc.gpsimd.tensor_tensor(xs(2 * b, 2), xs(2 * b, 2), at(b * 512, 512), ALU.add).then_inc(x_ready.sem, 1)
                        normed.due(me)



def chunks(w):
    k, n = w.shape[0] // P, w.shape[1]
    return w.reshape(k, P, n).transpose(1, 0, 2).reshape(P, k * n)


def as_units(a):
    n = -(-a.shape[1] // UNIT)
    if a.shape[1] != n * UNIT:
        a = np.concatenate([a, np.zeros((P, n * UNIT - a.shape[1]), a.dtype)], axis=1)
    return [a[:, i * UNIT:(i + 1) * UNIT] for i in range(n)]


def interleave(up, down):
    out = list(up[0])
    for j in range(1, len(up)):
        out += up[j] + down[j - 1]
    return out + down[-1]


def ffn_units(gu, down):
    up = [as_units(chunks(np.concatenate([gu[:, 256 * j:256 * (j + 1)], gu[:, D_FF + 256 * j:D_FF + 256 * (j + 1)]], axis=1)))
          for j in range(FFN_BLOCKS)]
    return interleave(up, [as_units(chunks(down[256 * j:256 * (j + 1)])) for j in range(FFN_BLOCKS)])


def mlp_units(w_up, w_down):
    return interleave([as_units(chunks(w_up[:, 256 * j:256 * (j + 1)])) for j in range(MLP_BLOCKS)],
                      [as_units(chunks(w_down[256 * j:256 * (j + 1)])) for j in range(MLP_BLOCKS)])


def block_units(w, order):
    return [u for b in order for u in as_units(chunks(w[:, 512 * b:512 * (b + 1)]))]


QKV_ORDER = [0, 2, 1, 3, 4, 5]


def band():
    out = np.zeros((TT, P, len(WINDOWS), TOKENS), np.float32)
    t = np.arange(TOKENS)
    for i, w in enumerate(WINDOWS):
        full = ((t[:, None] <= t[None, :]) & (t[:, None] > t[None, :] - w)).astype(np.float32)
        full[t, t] -= np.minimum(t + 1, w)
        out[:, :, i, :] = full.reshape(TT, P, TOKENS)
    return out.transpose(1, 0, 2, 3).reshape(P, -1)


def constants():
    out = np.zeros((P, NCONST), np.float32)

    def put(name, a):
        o, n = CONST[name]
        out[:, o:o + n] = np.asarray(a, np.float32).reshape(P, n)

    i = np.arange(P)
    put("ident", np.eye(P))
    put("after_neg", -(i[:, None] > i[None, :]).astype(np.float32))
    put("ones_neg", -np.ones((P, P)))
    put("ones", np.ones((P, P)))
    put("mask", np.concatenate([np.zeros((P, P)), np.where(i[None, :] <= i[:, None], 0.0, NEG)], axis=1))
    t, c = np.arange(TOKENS), np.arange(CPAD)
    seen = (c[None, :] < NCMP) & (c[None, :] * CMP_STRIDE + CMP_LEN - 1 <= t[:, None])
    put("cmp_mask", np.where(seen, 0.0, NEG).reshape(TT, P, CPAD).transpose(1, 0, 2))
    put("cmp_valid", (t >= CMP_LEN - 1).astype(np.float32).reshape(TT, P).T)
    put("head_block", i[:, None] // CPAD == np.arange(HG)[None, :])
    head = (i < HEADS)[:, None]
    put("in_slot", head & (i[:, None] % HG == np.array(SLOT_HEAD)[None, :]))
    put("in_group", head & (i[:, None] // HG == np.arange(GROUPS)[None, :]))
    return out


def nsa_tables():
    out = np.zeros((P, NTABLE), np.float32)
    i = np.arange(P)
    inv = np.float32(10000.0) ** (-np.arange(0, DH, 2, dtype=np.float32) / np.float32(DH))
    angle = (np.arange(TOKENS, dtype=np.float32)[:, None] * inv[None, :]).astype(np.float32).T[i % 32]
    first = (i % DH < 32)[:, None]
    for name, a in (("cos", np.cos(angle)), ("sin", np.where(first, -np.sin(angle), np.sin(angle))),
                    ("swap", i[:, None] == (i[None, :] ^ 32)),
                    ("dup", np.concatenate([i[:, None] == half * DH + i[None, :] % DH for half in range(2)], axis=1))):
        o, n = NSA_TABLE[name]
        out[:, o:o + n] = a
    return out


def small_parameters(v):
    out = np.zeros((P, NCOLS), np.float32)

    def put(name, a):
        o, n = COLS[name]
        out[:, o:o + n] = a.reshape(P, n)

    gains = [g[i] for i in range(2) for g in (v["norm_ffn1"], v["norm_mix"], v["norm_ffn2"], v["norm_ple"])]
    gains += [v["norm_g_2"][i, j] for i in range(2) for j in (0, 2)]
    put("gains", np.stack(gains).reshape(12, KC, P).transpose(2, 0, 1))
    put("post_gains", np.stack([v["norm_g_2"][i, j] for i in range(2) for j in (1, 3)]).reshape(4, KC, P).transpose(2, 0, 1))
    put("pool_scale", v["pool_scale"][0].reshape(KC, P).T)
    put("q_gain", np.concatenate([v["q_norm"][0], v["q_norm"][0]]))
    put("k_gain", np.concatenate([v["k_norm"][0], v["k_norm"][0]]))
    put("cmp_pos", v["nsa_cmp_pos_2"][0].reshape(2, CMP_LEN // 2, 2, DH).transpose(2, 3, 0, 1))
    put("cmp_w2", v["nsa_cmp_w2_2"][0].reshape(2, 2, P, DH).transpose(2, 0, 1, 3))
    put("b_f", np.pad(v["fox_b_f_2"][0], (0, P - HEADS))[:, None])
    return out


def kernel(**inputs):
    import concourse.bacc as bacc
    from concourse.bass_utils import run_bass_kernel_spmd

    v = {k: np.asarray(a) for k, a in inputs.items()}
    units = []
    for i in range(2):
        units += ffn_units(v["w_ffn1_gu"][i], v["w_ffn1_down"][i])
        if i == 0:
            units += block_units(v["w_qkv"][0], QKV_ORDER) + block_units(v["w_o"][0], range(2))
        else:
            units += block_units(v["w_pool_in"][0], range(2)) + as_units(band())
            units += as_units(v["w_pool_grp"][0].reshape(4, 2, P, 256).transpose(2, 0, 1, 3).reshape(P, -1))
        units += ffn_units(v["w_ffn2_gu"][i], v["w_ffn2_down"][i])
        units += block_units(v["w_ple_gate"][i], range(2)) + as_units(chunks(v["w_ple_proj"][i]))
    w = v["nsa_w_in_2"][0]
    q, kc, vc, ks, vs, kw, vw = np.split(w[:, :2560], [1024 + 256 * i for i in range(6)], axis=1)
    q = q.reshape(DM, 2, 2, HG, DH).transpose(0, 1, 3, 2, 4).reshape(DM, DM)
    units += block_units(np.concatenate([kc, ks, kw, vc, q, vs, vw], axis=1), range(5))
    units += as_units(chunks(np.concatenate([w[:, 2560:], np.zeros((DM, P - 3 * HEADS), np.float32)], axis=1)))
    for kv in range(2):
        units += as_units(chunks(v["nsa_cmp_w1_2"][0, kv]))
    units += block_units(v["nsa_w_out_2"][0], range(2)) + mlp_units(v["mlp_w_up_2"][0], v["mlp_w_down_2"][0])
    w = v["fox_w_in_2"][0]
    units += as_units(chunks(np.concatenate([w[:, 3072:], np.zeros((DM, P - HEADS), np.float32)], axis=1))) + block_units(w[:, :3072], QKV_ORDER)
    units += block_units(v["fox_w_out_2"][0], range(2)) + mlp_units(v["mlp_w_up_2"][1], v["mlp_w_down_2"][1])

    t = np.arange(TOKENS)
    counts = np.stack([np.float32(1) / np.minimum(t + 1, w).astype(np.float32) for w in WINDOWS])
    arrays = {
        "weights": np.stack(units),
        "x": np.ascontiguousarray(v["x"][0].T.reshape(KC, P, TOKENS).transpose(1, 0, 2).reshape(P, KC * TOKENS)),
        "constants": constants(),
        "parameters": small_parameters(v),
        "p": np.ascontiguousarray(v["p"][:, 0].transpose(0, 2, 1).reshape(2, 2, P, TOKENS).transpose(0, 2, 1, 3).reshape(2, P, 2 * TOKENS)),
        "counts": np.ascontiguousarray(np.broadcast_to(counts.reshape(1, -1), (P, 4 * TOKENS))),
    }
    arrays["nsa_tables"] = nsa_tables()
    nc = bacc.Bacc("TRN2", target_bir_lowering=False, num_devices=1)
    args = [nc.dram_tensor(n, a.shape, mybir.dt.float32, kind="ExternalInput").ap() for n, a in arrays.items()]
    out = nc.dram_tensor("out", (4, P, 2 * TOKENS), mybir.dt.float32, kind="ExternalOutput").ap()
    network_kernel(nc, *args, out)
    got = run_bass_kernel_spmd(nc, [arrays], core_ids=[0]).results[0]["out"]
    return np.ascontiguousarray(got.reshape(4, P, 2, TOKENS).transpose(3, 0, 2, 1)).reshape(1, TOKENS, DM)
```
